# Optimizing a Trainium2 kernel written in Bass

```python
import math
import jax, jax.numpy as jnp
from jax import lax
import numpy as np

D_MODEL = 1024
BATCH = 1
SEQ = 256
DEPTH = 1

D_RNN = 1024
N_RNN_BLOCKS = 16
RNN_BLOCK = D_RNN // N_RNN_BLOCKS
CONV_WIDTH = 4
LRU_C = 8.0
N_HEADS = 16
N_KV_HEADS = 4
HEAD_DIM = 64
ROT_DIM = HEAD_DIM // 4
ROPE_THETA = 500000.0
N_IDX_HEADS = 8
IDX_DIM = 64
IDX_ROT_DIM = IDX_DIM // 4
TOPK_MAX = 256
Q_BLOCK = 128
D_FF = -(-8 * D_MODEL // (3 * 256)) * 256
EPS = 1e-6

IN_SPLITS = (D_RNN, D_RNN, N_HEADS * HEAD_DIM, N_KV_HEADS * HEAD_DIM, N_KV_HEADS * HEAD_DIM,
             N_IDX_HEADS * IDX_DIM, IDX_DIM, N_IDX_HEADS, D_MODEL, D_MODEL)
D_IN = sum(IN_SPLITS)


def rms_norm(x, g):
    x32 = x.astype(jnp.float32)
    y = x32 * lax.rsqrt(jnp.mean(x32 * x32, axis=-1, keepdims=True) + EPS)
    return (y * g.astype(jnp.float32)).astype(x.dtype)

def layer_norm(x, g, b):
    x32 = x.astype(jnp.float32)
    mu = jnp.mean(x32, axis=-1, keepdims=True)
    var = jnp.mean(jnp.square(x32 - mu), axis=-1, keepdims=True)
    y = (x32 - mu) * lax.rsqrt(var + EPS)
    return (y * g.astype(jnp.float32) + b.astype(jnp.float32)).astype(x.dtype)

def partial_rope(x, rot_dim):
    s = x.shape[1]
    half = rot_dim // 2
    inv_freq = ROPE_THETA ** (-jnp.arange(half, dtype=jnp.float32) / half)
    ang = jnp.arange(s, dtype=jnp.float32)[:, None] * inv_freq[None, :]
    cos = jnp.cos(ang)[None, :, None, :]
    sin = jnp.sin(ang)[None, :, None, :]
    xr = x[..., :rot_dim].astype(jnp.float32)
    x1, x2 = xr[..., :half], xr[..., half:]
    rot = jnp.concatenate([x1 * cos - x2 * sin, x2 * cos + x1 * sin], axis=-1).astype(x.dtype)
    return jnp.concatenate([rot, x[..., rot_dim:]], axis=-1)

def causal_depthwise_conv(x, w, b):
    s = x.shape[1]
    xp = jnp.pad(x, ((0, 0), (CONV_WIDTH - 1, 0), (0, 0)))
    out = b
    for k in range(CONV_WIDTH):
        out = out + xp[:, k:k + s] * w[k]
    return out

def rg_lru(x, w_a, b_a, w_x, b_x, lam):
    bsz, s, _ = x.shape
    xb = x.reshape(bsz, s, N_RNN_BLOCKS, RNN_BLOCK)
    r = jax.nn.sigmoid(jnp.einsum('bshi,hij->bshj', xb, w_a).reshape(bsz, s, D_RNN) + b_a)
    i = jax.nn.sigmoid(jnp.einsum('bshi,hij->bshj', xb, w_x).reshape(bsz, s, D_RNN) + b_x)
    log_a = (-LRU_C * r.astype(jnp.float32)) * jax.nn.softplus(-lam.astype(jnp.float32))
    a = jnp.exp(log_a)
    u = jnp.sqrt(-jnp.expm1(2.0 * log_a)) * (i * x).astype(jnp.float32)

    def combine(left, right):
        a_l, b_l = left
        a_r, b_r = right
        return a_r * a_l, a_r * b_l + b_r

    _, h = lax.associative_scan(combine, (a, u), axis=1)
    return h.astype(x.dtype)

def dsa_sparse_attention(q, k, v, iq, ik, iw):
    bsz, s = q.shape[0], q.shape[1]
    topk = min(TOPK_MAX, s // 4)
    n_blk = s // Q_BLOCK
    rep = N_HEADS // N_KV_HEADS
    key_pos = jnp.arange(s)
    gather = jax.vmap(lambda t, idx: t[idx])

    def to_blocks(t):
        return jnp.moveaxis(t.reshape(bsz, n_blk, Q_BLOCK, *t.shape[2:]), 1, 0)

    def one_block(args):
        blk, qb, iqb, iwb = args
        q_pos = blk * Q_BLOCK + jnp.arange(Q_BLOCK)
        causal = key_pos[None, :] <= q_pos[:, None]
        logits = jnp.einsum('bqhd,bsd->bqhs', iqb, ik, preferred_element_type=jnp.float32)
        score = jnp.einsum('bqhs,bqh->bqs', jax.nn.relu(logits), iwb.astype(jnp.float32))
        score = jnp.where(causal[None], score, -jnp.inf)
        _, idx = lax.top_k(score, topk)
        valid = idx <= q_pos[None, :, None]
        k_sel = gather(k, idx)
        v_sel = gather(v, idx)
        qg = qb.reshape(bsz, Q_BLOCK, N_KV_HEADS, rep, HEAD_DIM)
        att = jnp.einsum('bqgrd,bqkgd->bqgrk', qg, k_sel,
                         preferred_element_type=jnp.float32) * (HEAD_DIM ** -0.5)
        att = jnp.where(valid[:, :, None, None, :], att, -jnp.inf)
        p = jax.nn.softmax(att, axis=-1).astype(v.dtype)
        o = jnp.einsum('bqgrk,bqkgd->bqgrd', p, v_sel)
        return o.reshape(bsz, Q_BLOCK, N_HEADS * HEAD_DIM)

    out = lax.map(one_block, (jnp.arange(n_blk), to_blocks(q), to_blocks(iq), to_blocks(iw)))
    return jnp.moveaxis(out, 0, 1).reshape(bsz, s, N_HEADS * HEAD_DIM)

def first_inputs(seed: int = 0) -> dict:
    key = jax.random.key(seed)
    ks = jax.random.split(key, 24)
    f32 = jnp.float32

    def nrm(k, shape, fan_in):
        return jax.random.normal(k, shape, f32) * (fan_in ** -0.5)

    def gain(k, shape):
        return 1.0 + 0.05 * jax.random.normal(k, shape, f32)

    L = DEPTH
    u = jax.random.uniform(ks[9], (L, D_RNN), f32, 0.9, 0.999)
    s_lam = u ** (1.0 / LRU_C)
    rg_lambda = jnp.log(s_lam) - jnp.log1p(-s_lam)
    return {
        "x": jax.random.normal(ks[0], (BATCH, SEQ, D_MODEL), f32),
        "norm_mix_pre": gain(ks[1], (L, D_MODEL)),
        "w_in": nrm(ks[2], (L, D_MODEL, D_IN), D_MODEL),
        "conv_w": nrm(ks[3], (L, CONV_WIDTH, D_RNN), CONV_WIDTH),
        "conv_b": 0.02 * jax.random.normal(ks[4], (L, D_RNN), f32),
        "rg_w_a": nrm(ks[5], (L, N_RNN_BLOCKS, RNN_BLOCK, RNN_BLOCK), RNN_BLOCK),
        "rg_b_a": 0.02 * jax.random.normal(ks[6], (L, D_RNN), f32),
        "rg_w_x": nrm(ks[7], (L, N_RNN_BLOCKS, RNN_BLOCK, RNN_BLOCK), RNN_BLOCK),
        "rg_b_x": 0.02 * jax.random.normal(ks[8], (L, D_RNN), f32),
        "rg_lambda": rg_lambda,
        "idx_k_ln_g": gain(ks[10], (L, IDX_DIM)),
        "idx_k_ln_b": 0.02 * jax.random.normal(ks[11], (L, IDX_DIM), f32),
        "w_rnn_out": nrm(ks[12], (L, D_RNN, D_MODEL), D_RNN),
        "w_att_out": nrm(ks[13], (L, N_HEADS * HEAD_DIM, D_MODEL), N_HEADS * HEAD_DIM),
        "w_o": nrm(ks[14], (L, D_MODEL, D_MODEL), D_MODEL),
        "norm_mix_post": gain(ks[15], (L, D_MODEL)),
        "norm_ffn_pre": gain(ks[16], (L, D_MODEL)),
        "w_ffn_gate": nrm(ks[17], (L, D_MODEL, D_FF), D_MODEL),
        "w_ffn_up": nrm(ks[18], (L, D_MODEL, D_FF), D_MODEL),
        "w_ffn_down": nrm(ks[19], (L, D_FF, D_MODEL), D_FF),
        "norm_ffn_post": gain(ks[20], (L, D_MODEL)),
    }

def first_block(x, norm_mix_pre, w_in, conv_w, conv_b, rg_w_a, rg_b_a, rg_w_x, rg_b_x, rg_lambda,
              idx_k_ln_g, idx_k_ln_b, w_rnn_out, w_att_out, w_o, norm_mix_post,
              norm_ffn_pre, w_ffn_gate, w_ffn_up, w_ffn_down, norm_ffn_post):
    bsz, s, _ = x.shape
    idx_w_scale = (N_IDX_HEADS ** -0.5) * (IDX_DIM ** -0.5)
    for l in range(DEPTH):
        h = rms_norm(x, norm_mix_pre[l])
        proj = h @ w_in[l]
        parts = []
        start = 0
        for width in IN_SPLITS:
            parts.append(proj[..., start:start + width])
            start += width
        xr, gr, q, k, v, iq, ik, iw, g_a, g_b = parts

        xc = causal_depthwise_conv(xr, conv_w[l], conv_b[l])
        y_rnn = rg_lru(xc, rg_w_a[l], rg_b_a[l], rg_w_x[l], rg_b_x[l], rg_lambda[l]) * jax.nn.gelu(gr)
        y_a = y_rnn @ w_rnn_out[l]

        q = partial_rope(q.reshape(bsz, s, N_HEADS, HEAD_DIM), ROT_DIM)
        k = partial_rope(k.reshape(bsz, s, N_KV_HEADS, HEAD_DIM), ROT_DIM)
        v = v.reshape(bsz, s, N_KV_HEADS, HEAD_DIM)
        iq = partial_rope(iq.reshape(bsz, s, N_IDX_HEADS, IDX_DIM), IDX_ROT_DIM)
        ik = layer_norm(ik, idx_k_ln_g[l], idx_k_ln_b[l])
        ik = partial_rope(ik[:, :, None, :], IDX_ROT_DIM)[:, :, 0, :]
        iw = iw * idx_w_scale
        y_att = dsa_sparse_attention(q, k, v, iq, ik, iw)
        y_b = y_att @ w_att_out[l]

        merged = jax.nn.sigmoid(g_a) * y_a + jax.nn.sigmoid(g_b) * y_b
        mix = merged @ w_o[l]
        x = x + rms_norm(mix, norm_mix_post[l])

        h = rms_norm(x, norm_ffn_pre[l])
        f = (jax.nn.silu(h @ w_ffn_gate[l]) * (h @ w_ffn_up[l])) @ w_ffn_down[l]
        x = x + rms_norm(f, norm_ffn_post[l])
    return x


DEPTH_2 = 2

GRID_W = 64
CTX_LEN = 256
ROPE_THETA_2 = 10000.0
A_Q_HEADS = 8
A_KV_HEADS = 2
A_WIDTH = A_Q_HEADS * HEAD_DIM
A_KV_WIDTH = A_KV_HEADS * HEAD_DIM
B_WIDTH = D_MODEL // 2
B_WINDOWS = (2, 4, 8, 16)
B_GROUPS = len(B_WINDOWS)
B_GROUP_W = B_WIDTH // B_GROUPS
EVEN_IN = A_WIDTH + 2 * A_KV_WIDTH + B_WIDTH
EVEN_MIX = A_WIDTH + B_WIDTH
C_Q_HEADS = 16
C_KV_HEADS = 4
C_WIDTH = C_Q_HEADS * HEAD_DIM
C_KV_WIDTH = C_KV_HEADS * HEAD_DIM
ODD_IN = C_WIDTH + 2 * C_KV_WIDTH
WINDOW = 128
N_SIDE = WINDOW // Q_BLOCK
BAND_BLOCKS = 2 * N_SIDE + 1
BAND_LEN = BAND_BLOCKS * Q_BLOCK
FFN_HIDDEN = int(math.ceil(8 * D_MODEL / 3 / 256)) * 256
N_EVEN = (DEPTH_2 + 1) // 2
N_ODD = DEPTH_2 // 2


def rmsnorm(x, g):
    xf = x.astype(jnp.float32)
    y = xf * lax.rsqrt(jnp.mean(xf * xf, axis=-1, keepdims=True) + EPS)
    return (y * g.astype(jnp.float32)).astype(x.dtype)

def modulate(x, g, shift, scale):
    return rmsnorm(x, g) * (1 + scale) + shift

def split_heads(t, h):
    return t.reshape(t.shape[0], t.shape[1], h, HEAD_DIM)

def axial_rope(x, rows, cols):
    hd = x.shape[-1]
    quarter = hd // 4
    freqs = ROPE_THETA_2 ** (-jnp.arange(quarter, dtype=jnp.float32) / quarter)

    def rot(a, pos):
        ang = pos.astype(jnp.float32)[:, None] * freqs[None, :]
        cos = jnp.cos(ang)[None, :, None, :]
        sin = jnp.sin(ang)[None, :, None, :]
        a1, a2 = a[..., :quarter], a[..., quarter:]
        return jnp.concatenate([a1 * cos - a2 * sin, a2 * cos + a1 * sin], axis=-1)

    out = jnp.concatenate([rot(x[..., :hd // 2], rows), rot(x[..., hd // 2:], cols)], axis=-1)
    return out.astype(x.dtype)

def dense_gqa_blocks(q, k, v):
    B, S, H, hd = q.shape
    KV = k.shape[2]
    G = H // KV
    nb = S // Q_BLOCK
    scale = 1.0 / math.sqrt(hd)
    qb = q.reshape(B, nb, Q_BLOCK, KV, G, hd).transpose(1, 0, 2, 3, 4, 5)

    def one(qblk):
        s = jnp.einsum('bqkgd,btkd->bkgqt', qblk, k, preferred_element_type=jnp.float32) * scale
        p = jax.nn.softmax(s, axis=-1).astype(v.dtype)
        return jnp.einsum('bkgqt,btkd->bqkgd', p, v)

    o = lax.map(one, qb)
    return o.transpose(1, 0, 2, 3, 4, 5).reshape(B, S, H * hd)

def ctx_attention(q, k, v, sink=None):
    B, T, H, hd = q.shape
    KV = k.shape[2]
    G = H // KV
    scale = 1.0 / math.sqrt(hd)
    qg = q.reshape(B, T, KV, G, hd)
    s = jnp.einsum('bqkgd,btkd->bkgqt', qg, k, preferred_element_type=jnp.float32) * scale
    if sink is not None:
        s_sink = jnp.broadcast_to(sink.reshape(KV, G)[None, :, :, None, None].astype(jnp.float32),
                                  (B, KV, G, T, 1))
        s = jnp.concatenate([s, s_sink], axis=-1)
    p = jax.nn.softmax(s, axis=-1)
    if sink is not None:
        p = p[..., :-1]
    o = jnp.einsum('bkgqt,btkd->bqkgd', p.astype(v.dtype), v)
    return o.reshape(B, T, H * hd)

def window_gqa_blocks(q, k, v, k_ctx, v_ctx, sink):
    B, S, H, hd = q.shape
    KV = k.shape[2]
    G = H // KV
    C = k_ctx.shape[1]
    nb = S // Q_BLOCK
    scale = 1.0 / math.sqrt(hd)
    qb = q.reshape(B, nb, Q_BLOCK, KV, G, hd).transpose(1, 0, 2, 3, 4, 5)

    def band(t):
        tp = jnp.pad(t, ((0, 0), (WINDOW, WINDOW), (0, 0), (0, 0)))
        tp = tp.reshape(B, nb + 2 * N_SIDE, Q_BLOCK, KV, hd)
        tb = jnp.concatenate([tp[:, j:j + nb] for j in range(BAND_BLOCKS)], axis=2)
        return tb.transpose(1, 0, 2, 3, 4)

    kb, vb = band(k), band(v)
    n_i = jnp.arange(nb)[:, None, None]
    q_i = jnp.arange(Q_BLOCK)[None, :, None]
    k_j = jnp.arange(BAND_LEN)[None, None, :]
    qpos = n_i * Q_BLOCK + q_i
    kpos = n_i * Q_BLOCK - WINDOW + k_j
    mask = (kpos >= 0) & (kpos < S) & (jnp.abs(qpos - kpos) <= WINDOW)
    sink_l = sink.reshape(KV, G)[None, :, :, None, None].astype(jnp.float32)

    def one(args):
        qblk, kblk, vblk, m = args
        s_w = jnp.einsum('bqkgd,btkd->bkgqt', qblk, kblk, preferred_element_type=jnp.float32) * scale
        s_w = jnp.where(m[None, None, None], s_w, -jnp.inf)
        s_c = jnp.einsum('bqkgd,btkd->bkgqt', qblk, k_ctx, preferred_element_type=jnp.float32) * scale
        s_s = jnp.broadcast_to(sink_l, (B, KV, G, Q_BLOCK, 1))
        p = jax.nn.softmax(jnp.concatenate([s_w, s_c, s_s], axis=-1), axis=-1).astype(v.dtype)
        o = jnp.einsum('bkgqt,btkd->bqkgd', p[..., :BAND_LEN], vblk)
        o = o + jnp.einsum('bkgqt,btkd->bqkgd', p[..., BAND_LEN:BAND_LEN + C], v_ctx)
        return o

    o = lax.map(one, (qb, kb, vb, mask))
    return o.transpose(1, 0, 2, 3, 4, 5).reshape(B, S, H * hd)

def centred_mean(u, w):
    S = u.shape[1]
    cs = jnp.pad(jnp.cumsum(u.astype(jnp.float32), axis=1), ((0, 0), (1, 0), (0, 0)))
    t = jnp.arange(S)
    lo = jnp.clip(t - w // 2, 0, S)
    hi = jnp.clip(t + w - w // 2, 0, S)
    cnt = (hi - lo).astype(jnp.float32)
    return ((cs[:, hi] - cs[:, lo]) / cnt[None, :, None]).astype(u.dtype)

def pool_mixer(u, w_pool, pool_scale):
    B, S, _ = u.shape
    diffs = []
    for g, w in enumerate(B_WINDOWS):
        ug = u[..., g * B_GROUP_W:(g + 1) * B_GROUP_W]
        diffs.append(centred_mean(ug, w) - ug)
    d = jnp.stack(diffs, axis=2)
    y = jnp.einsum('bsgc,gcd->bsgd', d, w_pool).reshape(B, S, B_WIDTH)
    return y * pool_scale

def even_mixer(h, hc, w_in, w_out, q_gain, k_gain, w_pool, pool_scale, rows, cols, with_ctx):
    def project(t):
        p = t @ w_in
        q, k, v, u = jnp.split(p, [A_WIDTH, A_WIDTH + A_KV_WIDTH, A_WIDTH + 2 * A_KV_WIDTH], axis=-1)
        q = rmsnorm(split_heads(q, A_Q_HEADS), q_gain)
        k = rmsnorm(split_heads(k, A_KV_HEADS), k_gain)
        return q, k, split_heads(v, A_KV_HEADS), u

    q, k, v, u = project(h)
    qc, kc, vc, uc = project(hc)
    q = axial_rope(q, rows, cols)
    k = axial_rope(k, rows, cols)
    a = dense_gqa_blocks(q, jnp.concatenate([k, kc], axis=1), jnp.concatenate([v, vc], axis=1))
    b = pool_mixer(u, w_pool, pool_scale)
    y = jnp.concatenate([a, b], axis=-1) @ w_out
    yc = None
    if with_ctx:
        ac = ctx_attention(qc, kc, vc)
        bc = pool_mixer(uc, w_pool, pool_scale)
        yc = jnp.concatenate([ac, bc], axis=-1) @ w_out
    return y, yc

def odd_mixer(h, hc, w_in, w_out, sink, rows, cols, with_ctx):
    def project(t):
        p = t @ w_in
        q, k, v = jnp.split(p, [C_WIDTH, C_WIDTH + C_KV_WIDTH], axis=-1)
        return split_heads(q, C_Q_HEADS), split_heads(k, C_KV_HEADS), split_heads(v, C_KV_HEADS)

    q, k, v = project(h)
    qc, kc, vc = project(hc)
    q = axial_rope(q, rows, cols)
    k = axial_rope(k, rows, cols)
    y = window_gqa_blocks(q, k, v, kc, vc, sink) @ w_out
    yc = None
    if with_ctx:
        yc = ctx_attention(qc, kc, vc, sink) @ w_out
    return y, yc

def swiglu(h, w_in, w_out):
    g, u = jnp.split(h @ w_in, 2, axis=-1)
    return (jax.nn.silu(g) * u) @ w_out

def second_inputs(seed: int = 0) -> dict:
    key = jax.random.key(seed)
    ks = jax.random.split(key, 24)
    D = D_MODEL

    def nrm(k, shape, std):
        return jax.random.normal(k, shape, dtype=jnp.float32) * std

    return {
        "x": nrm(ks[0], (BATCH, SEQ, D), 1.0),
        "c": nrm(ks[1], (BATCH, D), 1.0),
        "ctx": nrm(ks[2], (BATCH, CTX_LEN, D), 1.0),
        "c_ctx": nrm(ks[3], (D,), 1.0),
        "w_mod": nrm(ks[4], (DEPTH_2, D, 6 * D), 0.5 * D ** -0.5),
        "b_mod": nrm(ks[5], (DEPTH_2, 6 * D), 0.02),
        "g_pre_mix": 1.0 + nrm(ks[6], (DEPTH_2, D), 0.05),
        "g_post_mix": 1.0 + nrm(ks[7], (DEPTH_2, D), 0.05),
        "g_pre_ffn": 1.0 + nrm(ks[8], (DEPTH_2, D), 0.05),
        "g_post_ffn": 1.0 + nrm(ks[9], (DEPTH_2, D), 0.05),
        "we_in": nrm(ks[10], (N_EVEN, D, EVEN_IN), D ** -0.5),
        "we_out": nrm(ks[11], (N_EVEN, EVEN_MIX, D), EVEN_MIX ** -0.5),
        "we_q_gain": 1.0 + nrm(ks[12], (N_EVEN, HEAD_DIM), 0.05),
        "we_k_gain": 1.0 + nrm(ks[13], (N_EVEN, HEAD_DIM), 0.05),
        "we_pool": nrm(ks[14], (N_EVEN, B_GROUPS, B_GROUP_W, B_GROUP_W), B_GROUP_W ** -0.5),
        "we_pool_scale": 1.0 + nrm(ks[15], (N_EVEN, B_WIDTH), 0.1),
        "wo_in": nrm(ks[16], (N_ODD, D, ODD_IN), D ** -0.5),
        "wo_out": nrm(ks[17], (N_ODD, C_WIDTH, D), C_WIDTH ** -0.5),
        "wo_sink": nrm(ks[18], (N_ODD, C_Q_HEADS), 0.5),
        "w_ffn_in": nrm(ks[19], (DEPTH_2, D, 2 * FFN_HIDDEN), D ** -0.5),
        "w_ffn_out": nrm(ks[20], (DEPTH_2, FFN_HIDDEN, D), FFN_HIDDEN ** -0.5),
    }

def second_block(x, c, ctx, c_ctx, w_mod, b_mod, g_pre_mix, g_post_mix, g_pre_ffn, g_post_ffn,
              we_in, we_out, we_q_gain, we_k_gain, we_pool, we_pool_scale,
              wo_in, wo_out, wo_sink, w_ffn_in, w_ffn_out):
    S = x.shape[1]
    ROWS = S // GRID_W
    rows = jnp.repeat(jnp.arange(ROWS, dtype=jnp.int32), GRID_W)
    cols = jnp.tile(jnp.arange(GRID_W, dtype=jnp.int32), ROWS)
    silu_c = jax.nn.silu(c)
    silu_cc = jax.nn.silu(c_ctx)

    for l in range(DEPTH_2):
        with_ctx = l < DEPTH_2 - 1
        mod = (silu_c @ w_mod[l] + b_mod[l])[:, None, :]
        mod_c = (silu_cc @ w_mod[l] + b_mod[l])[None, None, :]
        sh_m, sc_m, gt_m, sh_f, sc_f, gt_f = jnp.split(mod, 6, axis=-1)
        csh_m, csc_m, cgt_m, csh_f, csc_f, cgt_f = jnp.split(mod_c, 6, axis=-1)

        h = modulate(x, g_pre_mix[l], sh_m, sc_m)
        hc = modulate(ctx, g_pre_mix[l], csh_m, csc_m)
        i = l // 2
        if l % 2 == 0:
            y, yc = even_mixer(h, hc, we_in[i], we_out[i], we_q_gain[i], we_k_gain[i],
                               we_pool[i], we_pool_scale[i], rows, cols, with_ctx)
        else:
            y, yc = odd_mixer(h, hc, wo_in[i], wo_out[i], wo_sink[i], rows, cols, with_ctx)

        x = x + gt_m * rmsnorm(y, g_post_mix[l])
        h = modulate(x, g_pre_ffn[l], sh_f, sc_f)
        x = x + gt_f * rmsnorm(swiglu(h, w_ffn_in[l], w_ffn_out[l]), g_post_ffn[l])

        if with_ctx:
            ctx = ctx + cgt_m * rmsnorm(yc, g_post_mix[l])
            hc = modulate(ctx, g_pre_ffn[l], csh_f, csc_f)
            ctx = ctx + cgt_f * rmsnorm(swiglu(hc, w_ffn_in[l], w_ffn_out[l]), g_post_ffn[l])
    return x


def setup_inputs(seed=0):
    out = dict(first_inputs(seed))
    for name, value in second_inputs(seed + 1).items():
        if name != "x":
            out[name + "_2"] = value
    return out


def reference(
    x, norm_mix_pre, w_in, conv_w, conv_b, rg_w_a, rg_b_a, rg_w_x, rg_b_x, rg_lambda,
    idx_k_ln_g, idx_k_ln_b, w_rnn_out, w_att_out, w_o, norm_mix_post, norm_ffn_pre, w_ffn_gate,
    w_ffn_up, w_ffn_down, norm_ffn_post, c_2, ctx_2, c_ctx_2, w_mod_2, b_mod_2, g_pre_mix_2,
    g_post_mix_2, g_pre_ffn_2, g_post_ffn_2, we_in_2, we_out_2, we_q_gain_2, we_k_gain_2,
    we_pool_2, we_pool_scale_2, wo_in_2, wo_out_2, wo_sink_2, w_ffn_in_2, w_ffn_out_2,
):
    x = first_block(
        x, norm_mix_pre, w_in, conv_w, conv_b, rg_w_a, rg_b_a, rg_w_x, rg_b_x, rg_lambda,
        idx_k_ln_g, idx_k_ln_b, w_rnn_out, w_att_out, w_o, norm_mix_post, norm_ffn_pre,
        w_ffn_gate, w_ffn_up, w_ffn_down, norm_ffn_post,
    )
    return second_block(
        x, c_2, ctx_2, c_ctx_2, w_mod_2, b_mod_2, g_pre_mix_2, g_post_mix_2, g_pre_ffn_2,
        g_post_ffn_2, we_in_2, we_out_2, we_q_gain_2, we_k_gain_2, we_pool_2, we_pool_scale_2,
        wo_in_2, wo_out_2, wo_sink_2, w_ffn_in_2, w_ffn_out_2,
    )


_drawn_inputs = setup_inputs


def setup_inputs(seed=0):
    import zlib

    import numpy as np

    out = dict(_drawn_inputs(seed))
    spreads = {}
    factors = {'rg_b_a': 8.0,
     'rg_b_x': 8.0,
     'g_pre_mix_2': 5.108,
     'g_post_mix_2': 4.486,
     'g_pre_ffn_2': 3.269,
     'g_post_ffn_2': 4.762,
     'we_q_gain_2': 8.0,
     'we_k_gain_2': 8.0,
     'we_pool_scale_2': 3.35,
     'wo_sink_2': 8.0}
    for name, (base, spread) in spreads.items():
        noise = np.random.default_rng([zlib.crc32(name.encode()), seed]).standard_normal(out[name].shape)
        drawn = base * np.exp(spread * noise) if base else spread * noise
        out[name] = __import__('jax').numpy.asarray(drawn.astype(out[name].dtype))
    for name, factor in factors.items():
        out[name] = (out[name] * factor).astype(out[name].dtype)
    return out
```

```python
import math
from contextlib import ExitStack

import numpy as np
import concourse.bass as bass
from concourse import mybir

F32 = mybir.dt.float32
I32 = mybir.dt.int32
ACT = mybir.ActivationFunctionType
ALU = mybir.AluOpType
AX = mybir.AxisListType

P = 128
S = 256
NT = S // P
D = 1024
KC = D // P
HD = 64
F = 2816
FC = F // P
NB = 512
FB = F // S
N_IN = 6216
C_XR, C_GR, C_Q, C_K, C_V, C_IQ, C_IK, C_IW, C_GA, C_GB = 0, 1024, 2048, 3072, 3328, 3584, 4096, 4160, 4168, 5192
N_EVEN, N_ODD = 1280, 1536
TOPK = 64
EPS = 1e-6
SCALE = HD ** -0.5
IDX_SCALE = (8 ** -0.5) * (64 ** -0.5)
MASKED = -1e30
TAKEN = -3e38
RING = 4

SV1 = [("norm_mix_pre", 8), ("conv_w", 32), ("conv_b", 8), ("rg_b_a", 8), ("rg_b_x", 8), ("rg_lambda", 8),
       ("norm_ffn_pre", 8), ("g_pre_mix_2", 16), ("g_pre_ffn_2", 16), ("c_2", 8), ("c_ctx_2", 8)]
SV2 = [("we_pool_scale_2", 4), ("g_post_mix_2", 16), ("g_post_ffn_2", 16)]
SV3 = [("b_mod_2", 96)]

MODG = 8
PRODUCTS = [("in_a", 16, 8), ("in_tail", 2, 1), ("in_b", 8, 4), ("mod0", MODG, 1), ("mod1", MODG, 1),
            ("mod2", MODG, 1), ("y_a", 4, 2), ("mod3", MODG, 1), ("y_b", 4, 2), ("w_o", 4, 2), ("mod4", MODG, 1),
            ("up1", 22, FB), ("down1", 11, 2), ("mod5", MODG, 1),
            ("qkv_c0", 6, 3), ("qkv_x0", 6, 3), ("out_x0", 4, 2), ("out_c0", 4, 2),
            ("up_x0", 22, FB), ("down_x0", 11, 2), ("up_c0", 22, FB), ("down_c0", 11, 2),
            ("kv_c1", 2, 1), ("qkv_x1", 6, 3), ("out_x1", 4, 2), ("up_x1", 22, FB), ("down_x1", 11, 2)]
TURNS = [("h1", 8), ("xr", 8), ("q", 8), ("kiq", 8), ("ik", 1), ("gr", 8), ("o1", 8), ("mrg", 8), ("hf1", 8),
         ("h_c0", 8), ("h_x0", 8), ("q_xc", 8), ("k_xc", 4), ("o_x", 4), ("o_c", 4), ("hf_x0", 8), ("hf_c0", 8),
         ("h_c1", 8), ("h_x1", 8), ("q_1", 8), ("k_1", 8), ("o_1", 8), ("hf_x1", 8)]
SUMS = ["n1", "p1", "nf1", "pf1", "n_c0", "n_x0", "p_x0", "p_c0", "nf_x0", "nf_c0", "pf_x0", "pf_c0",
        "n_c1", "n_x1", "p_x1", "nf_x1", "pf_x1"]
ATTN = [("a1", 16, (128, 256)), ("ax", 8, (512, 512)), ("ac", 8, (256, 256)), ("a1x", 16, (512, 512))]
FFNS = ["1", "_x0", "_c0", "_x1"]


def starts(items, *cols):
    at, sums = {}, [0] * len(cols)
    for it in items:
        at[it[0]] = tuple(sums)
        sums = [s + it[c] for s, c in zip(sums, cols)]
    return at


def n_act(n):
    return sum(i // 2 % 2 == 0 for i in range(n))


def build(nc, t_in, consts, out):
    prod = starts(PRODUCTS, 1, 2)
    n_slots = dict((n, s) for n, s, _ in PRODUCTS)
    turn_n = dict(TURNS)
    turn, ca, cd, ct = {}, 0, 0, 0
    for name, n in TURNS:
        turn[name] = (ct, ca, cd)
        ct, ca, cd = ct + n, ca + n_act(n), cd + n - n_act(n)
    sums = dict((n, i) for i, n in enumerate(SUMS))
    att0 = starts([(n, 2 * h) for n, h, _ in ATTN], 1)
    ffn_i = dict((n, i) for i, n in enumerate(FFNS))

    with ExitStack() as ctx:
        def sb(name, *shape):
            return ctx.enter_context(nc.sbuf_tensor(name, [P, *shape], F32))

        def sem(name):
            return ctx.enter_context(nc.semaphore(name))

        G = ctx.enter_context(nc.psum_tensor("G", [P, 4, NB], F32))
        T = ctx.enter_context(nc.psum_tensor("T", [P, 4, NB], F32))

        ring = sb("ring", RING, 2048)
        x = sb("x", NT, D)
        cx = sb("cx", NT, D)
        area = sb("area", NT * N_IN)
        Y = sb("Y", NT, D)
        Z = sb("Z", NT, D)
        HT = sb("HT", KC, S)
        rnn = sb("rnn", 8 * 259 + 4 * 2048)
        qT = sb("qT", 8, S)
        kT = sb("kT", 4, 2 * S)
        ikT = sb("ikT", S)
        bd = sb("bd", 2048 + 512)
        bias1 = sb("bias1", NT, S)
        causal = sb("causal", NT, S)
        ident = sb("ident", P)
        ones = sb("ones", P)
        svc = sb("svc", 260)
        scT = sb("scT", KC, 32)
        modcol = sb("modcol", 2, 48, 2)
        hscale = sb("hscale", 2, 2, 2, 8)
        gtg = sb("gtg", 2, 2, 2, 8)
        bc = sb("bc", 2, D)
        rope1 = sb("rope1", NT, 2, 8)
        rope2 = sb("rope2", NT, 2, 32)
        lnrow = sb("lnrow", 2, HD)
        nsink = sb("nsink", 16)
        ssb = sb("ssb", 2, 2)
        rs = sb("rs", 2, 2)
        rq = sb("rq", 6, 40)
        c8 = sb("c8", 10, 8)
        amin = sb("amin", 4)
        asum = sb("asum", 4)
        arec = sb("arec", 4)
        top8 = sb("top8", NT, 8)
        iws = sb("iws", NT, 8)

        proj = area[:, :].rearrange("p (t n) -> p t n", t=NT)
        hidT = area[:, 0:FC * S].rearrange("p (c s) -> p c s", c=FC)
        o_ = FC * S
        hid = area[:, o_:o_ + 1024].rearrange("p (b t n) -> p b t n", b=2, t=NT)
        gate = area[:, o_ + 1024:o_ + 2048].rearrange("p (b t n) -> p b t n", b=2, t=NT)
        o_ += 2048
        diag = area[:, o_:o_ + 1024].rearrange("p (c n) -> p c n", c=KC)
        bc2 = area[:, o_ + 1024:o_ + 3072].rearrange("p (r n) -> p r n", r=2)
        band = area[:, o_ + 3072:o_ + 4096].rearrange("p (t n) -> p t n", t=NT)
        qkgain = area[:, o_ + 4096:o_ + 4096 + 10 * HD]
        px = area[:, 0:NT * N_ODD].rearrange("p (t n) -> p t n", t=NT)
        pc = area[:, NT * N_ODD:2 * NT * N_ODD].rearrange("p (t n) -> p t n", t=NT)
        xpad = rnn[:, 0:8 * 259].rearrange("p (c n) -> p c n", c=8)
        o_ = 8 * 259
        xc, R1, R2, R3 = [rnn[:, o_ + 2048 * i:o_ + 2048 * (i + 1)].rearrange("p (c n) -> p c n", c=8) for i in range(4)]
        work = rnn[:, 0:4 * 516].rearrange("p (b n) -> p b n", b=4)
        pT = R1.rearrange("p (b c) n -> p b (c n)", b=4)
        HC = R2
        modrow = xc
        bda = bd[:, 0:1024].rearrange("p (c n) -> p c n", c=8)
        bdx = bd[:, 1024:2048].rearrange("p (c n) -> p c n", c=8)
        poolm = bd[:, 0:2048].rearrange("p (g k n) -> p g k n", g=4, k=NT)
        wpool = bd[:, 2048:2560].rearrange("p (g n) -> p g n", g=4)
        kd = Y[:, :, :].rearrange("p t n -> p (t n)").rearrange("p (k g n) -> p k g n", k=4, g=4)
        ikd = Z[:, 0, 0:2 * P].rearrange("p (t n) -> p t n", t=NT)
        svr = Z[:, 0, 0:3 * P].rearrange("p (i n) -> p i n", i=3)
        zf = Z[:, :, :].rearrange("p t n -> p (t n)")
        yf = Y[:, :, :].rearrange("p t n -> p (t n)")

        at, cols = 0, {}
        for base, rows in ((0, SV1), (P, SV2), (164, SV3)):
            at = base
            for name, n in rows:
                cols[name] = svc[:, at:at + n]
                at += n

        w_landed = [sem(f"w_landed{i}") for i in range(RING)]
        slot_read = sem("slot_read")
        ev_act = sem("ev_act")
        ev_dve = sem("ev_dve")
        turned = sem("turned")
        turn_act = sem("turn_act")
        turn_dve = sem("turn_dve")
        x_in = sem("x_in")
        sv_in = sem("sv_in")
        small_in = sem("small_in")
        late_in = sem("late_in")
        bd_in = sem("bd_in")
        bd_zero = sem("bd_zero")
        band_in = sem("band_in")
        pool_in = sem("pool_in")
        sv_turned = sem("sv_turned")
        sv_done = sem("sv_done")
        ss_done = sem("ss_done")
        rs_done = sem("rs_done")
        xn_act = sem("xn_act")
        xn_dve = sem("xn_dve")
        x_new = sem("x_new")
        c_silu = sem("c_silu")
        dstep = sem("dstep")
        astep = sem("astep")
        rnn_xc = sem("rnn_xc")
        rnn_gate = sem("rnn_gate")
        rnn_sig = sem("rnn_sig")
        rnn_ta = sem("rnn_ta")
        rnn_sq = sem("rnn_sq")
        rnn_root = sem("rnn_root")
        softp_z = sem("softp_z")
        softp_e = sem("softp_e")
        softp = sem("softp")
        gelu_in = sem("gelu_in")
        gelu_t = sem("gelu_t")
        gelu_ok = sem("gelu_ok")
        qk_ready = sem("qk_ready")
        idx_mm = sem("idx_mm")
        idx_relu = sem("idx_relu")
        idx_acc = sem("idx_acc")
        sg_ready = sem("sg_ready")
        mrg_ok = sem("mrg_ok")
        mod_turned = sem("mod_turned")
        mod_ok = sem("mod_ok")
        diag_ok = sem("diag_ok")
        bc_mm = sem("bc_mm")
        bc_ok = sem("bc_ok")
        pool_mm = sem("pool_mm")
        pool_d = sem("pool_d")
        pool_y = sem("pool_y")
        pool_ok = sem("pool_ok")
        hid_turned = sem("hid_turned")
        hidT_ok = sem("hidT_ok")
        a_mm = sem("a_mm")
        a_min = sem("a_min")
        a_exp = sem("a_exp")
        a_turned = sem("a_turned")
        a_pT = sem("a_pT")
        a_pv = sem("a_pv")
        a_o = sem("a_o")
        stored = sem("stored")

        pstep = sem("pstep")
        rnn_y = sem("rnn_y")
        rnn_scan = sem("rnn_scan")
        hs_ok = sem("hs_ok")
        SV_DMAS = 1 + len(SV1) + len(SV2) + len(SV3)
        kT_junk = kT[:, :, :].rearrange("p g n -> p (g n)").rearrange("p (t n) -> p t n", t=NT)

        def modrow_of(g):
            return modrow.rearrange("p c n -> p (c n)")[:, (g % 4) * NB:(g % 4 + 1) * NB]

        def chunks(w):
            return w.rearrange("(k p) n -> p k n", p=P)

        w = {n: t_in[n] for n in t_in}
        w_in = chunks(w["w_in"][0])
        ring4 = ring[:, :, :].rearrange("p r (k n) -> p r k n", k=4)
        ring2 = ring[:, :, :].rearrange("p r (k n) -> p r k n", k=2)
        up_w = {"1": (chunks(w["w_ffn_gate"][0]), chunks(w["w_ffn_up"][0])),
                "0": tuple(chunks(w["w_ffn_in_2"][0][:, i * F:(i + 1) * F]) for i in range(2)),
                "_x1": tuple(chunks(w["w_ffn_in_2"][1][:, i * F:(i + 1) * F]) for i in range(2))}
        down_w = {"1": chunks(w["w_ffn_down"][0]), "0": chunks(w["w_ffn_out_2"][0]), "_x1": chunks(w["w_ffn_out_2"][1])}
        for n in ("_x0", "_c0"):
            up_w[n], down_w[n] = up_w["0"], down_w["0"]
        plain = {"y_a": w["w_rnn_out"][0], "y_b": w["w_att_out"][0], "w_o": w["w_o"][0], "qkv_c0": w["we_in_2"][0],
                 "qkv_x0": w["we_in_2"][0], "out_x0": w["we_out_2"][0], "out_c0": w["we_out_2"][0],
                 "qkv_x1": w["wo_in_2"][0], "kv_c1": w["wo_in_2"][0][:, D:N_ODD], "out_x1": w["wo_out_2"][0]}

        class Steps:

            def __init__(self, eng, s):
                self.eng, self.s, self.n = eng, s, 0

            def __call__(self, ins):
                self.n += 1
                ins.then_inc(self.s, 1)

            def wait(self, back=0):
                self.eng.wait_ge(self.s, self.n - back)

        block = ctx.enter_context(nc.Block())

        @block.sync
        def _(sp):
            def slot_free(s):
                if not isinstance(s, int) or s >= RING:
                    sp.wait_ge(slot_read, s - RING + 1)

            def fill(slot, s, parts):
                slot_free(s)
                for dst, src in parts:
                    sp.dma_start(dst, src).then_inc(w_landed[slot], 16)

            def half_block(slot, s, wv, half, col, n):
                fill(slot, s, [(ring4[:, slot, 2 * i:2 * i + 2, 0:n],
                                wv[:, 4 * half + 2 * i:4 * half + 2 * i + 2, col]) for i in range(2)])

            def product(name):
                s0 = prod[name][0]
                wv = chunks(plain[name])
                total = wv.shape[2]
                for b in range(-(-total // NB)):
                    n = min(NB, total - b * NB)
                    for h in range(2):
                        s = s0 + 2 * b + h
                        half_block(s % RING, s, wv, h, slice(b * NB, b * NB + n), n)

            def in_loop(name, col0, nblocks):
                s0, first = prod[name][0], 0
                if s0 == 0:
                    for j in range(RING):
                        half_block(j, j, w_in, j % 2, slice(col0 + (j // 2) * NB, col0 + (j // 2 + 1) * NB), NB)
                    first = 1
                with sp.Fori(first, nblocks // 2) as it:
                    for j in range(RING):
                        half_block((s0 + j) % RING, s0 + j + it * RING, w_in, j % 2,
                                   bass.ds(it * (2 * NB) + (col0 + (j // 2) * NB), NB), NB)

            def mod_group(g):
                s0 = prod[f"mod{g}"][0]
                wv = chunks(w["w_mod_2"][g // 3])
                for j in range(MODG):
                    c = ((g % 3) * 4 + j // 2) * NB
                    half_block((s0 + j) % RING, s0 + j, wv, j % 2, slice(c, c + NB), NB)

            def ffn(name):
                s0 = prod["up" + name][0]
                wg, wu = up_w[name]

                def half_pair(j, s, col):
                    slot, h = (s0 + j) % RING, j % 2
                    fill(slot, s, [(ring4[:, slot, :, S * i:S * i + S], wv[:, 4 * h:4 * h + 4, col])
                                   for i, wv in enumerate((wg, wu))])

                for j in range(2):
                    half_pair(j, s0 + j, slice(0, S))
                with sp.Fori(0, FB // 2) as it:
                    for j in range(2, 6):
                        half_pair(j, s0 + j + it * 4, bass.ds(it * (2 * S) + (j // 2) * S, S))
                s0 = prod["down" + name][0]
                wd = down_w[name]
                for j in range(FC // 2):
                    slot = (s0 + j) % RING
                    fill(slot, s0 + j, [(ring2[:, slot, i:i + 1, :], wd[:, 2 * j + i:2 * j + i + 1, :]) for i in range(2)])

            in_loop("in_a", 0, 8)
            s0 = prod["in_tail"][0]
            for h in range(2):
                half_block((s0 + h) % RING, s0 + h, w_in, h, slice(C_IK, C_GA), C_GA - C_IK)
            in_loop("in_b", C_GA, 4)
            for g in range(3):
                mod_group(g)
            product("y_a")
            mod_group(3)
            product("y_b")
            product("w_o")
            mod_group(4)
            ffn("1")
            mod_group(5)
            for n in ("qkv_c0", "qkv_x0", "out_x0", "out_c0"):
                product(n)
            ffn("_x0")
            ffn("_c0")
            for n in ("kv_c1", "qkv_x1", "out_x1"):
                product(n)
            ffn("_x1")
            sp.wait_ge(x_new, len([n for n in SUMS if n[0] == "p"]))
            sp.dma_start(out[0].rearrange("(t p) n -> p t n", p=P), x[:, :, :]).then_inc(stored, 16)
            sp.wait_ge(stored, 16)

        @block.tensor
        def _(pe):
            def free(waits):
                for s, v in waits:
                    pe.wait_ge(s, v)

            def pair_free(e):
                if not isinstance(e, int) or e >= 2:
                    pe.wait_ge(ev_act, e - 1)
                    pe.wait_ge(ev_dve, e - 1)

            def landed(s, fills=None):
                pe.wait_ge(w_landed[s % RING], 32 * (s // RING + 1) if fills is None else fills)

            def rows(s, half, e, lhsT, n, fills=None):
                landed(s, fills)
                for t in range(NT):
                    for k in range(4):
                        mm = nc.tensor.matmul(G[:, 2 * (e % 2) + t, 0:n], lhsT[:, 4 * half + k, t * P:(t + 1) * P],
                                              ring4[:, s % RING, k, 0:n], start=(half == 0 and k == 0),
                                              stop=(half == 1 and k == 3))
                mm.then_inc(slot_read, 1)

            def product(name, lhsT, total):
                s0, e0 = prod[name]
                for b in range(-(-total // NB)):
                    pair_free(e0 + b)
                    for h in range(2):
                        rows(s0 + 2 * b + h, h, e0 + b, lhsT, min(NB, total - b * NB))

            def in_loop(name, nblocks):
                s0, e0 = prod[name]
                first = 0
                if e0 < 2:
                    for j in range(4):
                        rows(s0 + j, j % 2, e0 + j // 2, HT, NB)
                    first = 1
                with pe.Fori(first, nblocks // 2) as it:
                    for j in range(4):
                        if j % 2 == 0:
                            pe.wait_ge(ev_act, it * 2 + (e0 + j // 2 - 1))
                            pe.wait_ge(ev_dve, it * 2 + (e0 + j // 2 - 1))
                        rows(s0 + j, j % 2, e0 + j // 2, HT, NB, it * 32 + 32 * ((s0 + j) // RING + 1))

            def mod_group(g):
                s0, e0 = prod[f"mod{g}"]
                pair_free(e0)
                if g == 0:
                    pe.wait_ge(c_silu, 1)
                for j in range(MODG):
                    landed(s0 + j)
                    q = j // 2
                    for k in range(4):
                        mm = nc.tensor.matmul(G[32 * q:32 * q + 32, 2 * (e0 % 2), :], scT[:, 4 * (j % 2) + k, :],
                                              ring4[:, (s0 + j) % RING, k, :], start=(j % 2 == 0 and k == 0),
                                              stop=(j % 2 == 1 and k == 3), tile_position=(0, 32 * q))
                    mm.then_inc(slot_read, 1)

            def mod_turn(g, waits):
                e0 = prod[f"mod{g}"][1]
                free(waits)
                pe.wait_ge(ev_act, e0 + 1)
                pe.wait_ge(ev_dve, e0 + 1)
                for c in range(4):
                    tr = nc.tensor.transpose(T[:, g % 4, c * P:(c + 1) * P],
                                             modrow_of(g)[:, c * P:(c + 1) * P], ident[:, :])
                tr.then_inc(mod_turned, 1)
                return [(mod_ok, g + 1)]

            def turn_stage(name, src, waits, ready=()):
                n, (c0, _, _) = turn_n[name], turn[name]
                free(waits)
                for s, v in ready:
                    pe.wait_ge(s, v)
                for i in range(n):
                    for t in range(NT):
                        tr = nc.tensor.transpose(T[:, i // 2, (i % 2) * S + t * P:(i % 2) * S + (t + 1) * P],
                                                 src(i, t), ident[:, :])
                    tr.then_inc(turned, 1)
                return [(turn_act, turn[name][1] + n_act(n)), (turn_dve, turn[name][2] + n - n_act(n))]

            def norm_turn(name, sname, src, waits):
                k = sums[sname] + 1
                n_x = 1 + [n for n in SUMS[:k] if n[0] == "n"].index(sname)
                return turn_stage(name, lambda i, t: src[:, t, i * P:(i + 1) * P], waits,
                                  [(xn_act, n_x), (xn_dve, n_x)])

            def ffn(name, lhsT, waits):
                f = ffn_i[name]
                s0, e0 = prod["up" + name]
                h0 = FB * f
                free(waits)

                def up_block(j, it=None):
                    more = 0 if it is None else it
                    pe.wait_ge(ev_act, more * 2 + (e0 + j - 1))
                    pe.wait_ge(ev_dve, more * 2 + (e0 + j - 1))
                    for h in range(2):
                        s = s0 + 2 * j + h
                        rows(s, h, e0 + j, lhsT, NB, more * 32 + 32 * (s // RING + 1))

                def turn_hidden(j, it=None):
                    more = 0 if it is None else it
                    pe.wait_ge(ev_dve, more * 2 + (e0 + j + 1))
                    if not (f == 0 and j < 2 and it is None):
                        pe.wait_ge(hidT_ok, more * 2 + (h0 + j - 1))
                    for c in range(2):
                        for t in range(NT):
                            tr = nc.tensor.transpose(T[:, j % 2, c * S + t * P:c * S + (t + 1) * P],
                                                     hid[:, j % 2, t, c * P:(c + 1) * P], ident[:, :])
                    tr.then_inc(hid_turned, 1)

                up_block(0)
                up_block(1)
                turn_hidden(0)
                up_block(2)
                turn_hidden(1)
                with pe.Fori(1, FB // 2) as it:
                    up_block(1, it)
                    turn_hidden(0, it)
                    up_block(2, it)
                    turn_hidden(1, it)
                turn_hidden(FB - 1)
                s0, e0 = prod["down" + name]
                pair_free(e0)
                pair_free(e0 + 1)
                pe.wait_ge(hidT_ok, h0 + FB)
                for j in range(FC // 2):
                    s = s0 + j
                    landed(s)
                    for k in range(2):
                        for t in range(NT):
                            for h in range(2):
                                mm = nc.tensor.matmul(G[:, 2 * ((e0 + h) % 2) + t, :],
                                                      hidT[:, 2 * j + k, t * P:(t + 1) * P],
                                                      ring2[:, s % RING, k, h * NB:(h + 1) * NB],
                                                      start=(j == 0 and k == 0), stop=(j == FC // 2 - 1 and k == 1))
                    mm.then_inc(slot_read, 1)
                return []

            def attention(name, qs, ks, vs, waits, ready=()):
                heads, nks = [a[1:] for a in ATTN if a[0] == name][0]
                u0 = att0[name][0]
                n = 2 * heads
                free(waits)
                for s, v in ready:
                    pe.wait_ge(s, v)

                def unit(u):
                    return 2 * (u // 4) + u % 2, (u // 2) % 2

                def scores(u):
                    h, t = unit(u)
                    if u >= 2:
                        pe.wait_ge(a_min, u0 + u - 1)
                    nc.tensor.matmul(T[:, u % 2, 0:nks[t]], qs(h, t), ks(h, t), start=True, stop=True).then_inc(a_mm, 1)

                def turn_probs(u):
                    h, t = unit(u)
                    pe.wait_ge(a_exp, u0 + u + 1)
                    if u >= 1:
                        pe.wait_ge(a_pT, u0 + u)
                    for k in range(nks[t] // P):
                        tr = nc.tensor.transpose(T[:, 2, k * P:(k + 1) * P], work[:, u % 4, k * P:(k + 1) * P], ident[:, :])
                    tr.then_inc(a_turned, 1)

                def values(u):
                    h, t = unit(u)
                    pe.wait_ge(a_pT, u0 + u + 1)
                    if u >= 1:
                        pe.wait_ge(a_o, u0 + u)
                    for k in range(nks[t] // P):
                        mm = nc.tensor.matmul(T[:, 3, (u % 2) * HD:(u % 2 + 1) * HD], pT[:, u % 4, k * P:(k + 1) * P],
                                              vs(h, k), start=(k == 0), stop=(k == nks[t] // P - 1))
                    mm.then_inc(a_pv, 1)

                for u in range(n + 2):
                    if u < n:
                        scores(u)
                    if 1 <= u <= n:
                        turn_probs(u - 1)
                    if u >= 2:
                        values(u - 2)
                return [(a_o, u0 + n)]

            def broadcast_row(k, waits):
                free(waits)
                pe.wait_ge(diag_ok, k + 1)
                for c in range(KC):
                    mm = nc.tensor.matmul(T[:, c // 4, (c % 4) * P:(c % 4 + 1) * P], ones[:, :], diag[:, c, :],
                                          start=True, stop=True)
                mm.then_inc(bc_mm, 1)
                return [(bc_ok, k + 1)]

            def half64(h):
                return slice((h % 2) * HD, (h % 2 + 1) * HD)

            pe.wait_ge(sv_in, 16 * SV_DMAS)
            for i, n in enumerate((P, 36, 96)):
                tr = nc.tensor.transpose(T[:, 0, i * P:i * P + n], svr[0:n, i, :], ident[0:n, 0:n])
            tr.then_inc(sv_turned, 1)
            busy = norm_turn("h1", "n1", Y, [(sv_done, 1)])
            free(busy)
            in_loop("in_a", 8)
            s0, e0 = prod["in_tail"]
            pair_free(e0)
            for h in range(2):
                rows(s0 + h, h, e0, HT, C_GA - C_IK)
            in_loop("in_b", 4)
            e = prod["in_b"][1]
            busy = turn_stage("xr", lambda i, t: proj[:, t, C_XR + i * P:C_XR + (i + 1) * P], busy,
                              [(ev_act, e), (ev_dve, e)])
            mod_group(0)
            free(busy)
            for c in range(8):
                pe.wait_ge(rnn_xc, c + 1)
                if c == 0:
                    pe.wait_ge(bd_in, 64)
                if c >= 4:
                    pe.wait_ge(rnn_sig, c - 3)
                for i, m in enumerate((bda, bdx)):
                    mm = nc.tensor.matmul(T[:, c % 4, i * S:(i + 1) * S], m[:, c, :], xc[:, c, :], start=True, stop=True)
                mm.then_inc(rnn_gate, 1)
            busy = [(rnn_sig, 8)]
            busy = turn_stage("q", lambda i, t: proj[:, t, C_Q + i * P:C_Q + (i + 1) * P], busy, [(qk_ready, 1)])
            busy = turn_stage("kiq", lambda i, t: kd[:, t, i, :] if i < 4 else
                              proj[:, t, C_IQ + (i - 4) * P:C_IQ + (i - 3) * P], busy)
            busy = turn_stage("ik", lambda i, t: ikd[:, t, :], busy)
            free(busy)
            for u in range(16):
                h, t = u // 2, u % 2
                if u >= 4:
                    pe.wait_ge(idx_relu, u - 3)
                nc.tensor.matmul(T[:, u % 4, 0:P * (t + 1)], kT[half64(h), h // 2, S + t * P:S + (t + 1) * P],
                                 ikT[half64(h), 0:P * (t + 1)], start=True, stop=True).then_inc(idx_mm, 1)
            mod_group(1)
            busy = turn_stage("gr", lambda i, t: proj[:, t, C_GR + i * P:C_GR + (i + 1) * P],
                              [(idx_relu, 16)], [(gelu_ok, 1)])
            mod_group(2)
            busy = attention("a1", lambda h, t: qT[half64(h), h // 2, t * P:(t + 1) * P],
                             lambda h, t: kT[half64(h), h // 4, 0:P * (t + 1)],
                             lambda h, k: proj[:, k, C_V + (h // 4) * HD:C_V + (h // 4 + 1) * HD], busy)
            pe.wait_ge(rnn_y, 1)
            product("y_a", R3, D)
            busy = turn_stage("o1", lambda i, t: Z[:, t, i * P:(i + 1) * P], busy)
            mod_group(3)
            free(busy)
            product("y_b", HT, D)
            busy = turn_stage("mrg", lambda i, t: Y[:, t, i * P:(i + 1) * P], busy, [(mrg_ok, 1)])
            free(busy)
            product("w_o", qT, D)
            for g in range(4):
                busy = mod_turn(g, busy)
            mod_group(4)
            busy = norm_turn("hf1", "nf1", Y, busy)
            ffn("1", HT, busy)
            mod_group(5)
            busy = []
            for g in (4, 5):
                busy = mod_turn(g, busy)
            busy = norm_turn("h_c0", "n_c0", Z, busy)
            free(busy)
            product("qkv_c0", HC, N_EVEN)
            busy = norm_turn("h_x0", "n_x0", Y, busy)
            free(busy)
            product("qkv_x0", HT, N_EVEN)
            busy = turn_stage("q_xc", lambda i, t: (px, pc)[i // 4][:, t, (i % 4) * P:(i % 4 + 1) * P], busy, [(qk_ready, 2)])
            busy = turn_stage("k_xc", lambda i, t: kd[:, 2 * (i // 2) + t, i % 2, :], busy)
            vcol = 640
            busy = attention("ax", lambda h, t: qT[half64(h), h // 2, t * P:(t + 1) * P],
                             lambda h, t: kT[half64(h), h // 4, :],
                             lambda h, k: (px, pc)[k // 2][:, k % 2, vcol + (h // 4) * HD:vcol + (h // 4 + 1) * HD], busy)
            busy = attention("ac", lambda h, t: qT[half64(h), 4 + h // 2, t * P:(t + 1) * P],
                             lambda h, t: kT[half64(h), h // 4, S:2 * S],
                             lambda h, k: pc[:, k, vcol + (h // 4) * HD:vcol + (h // 4 + 1) * HD], busy)
            free(busy)
            pe.wait_ge(pool_in, 16 * 2)
            for i, src in enumerate((px, pc)):
                if i == 1:
                    pe.wait_ge(pool_d, 2)
                for g in range(4):
                    for k in range(NT):
                        mm = nc.tensor.matmul(T[:, g // 2, (g % 2) * S:(g % 2 + 1) * S], src[:, k, 768 + g * P:768 + (g + 1) * P],
                                              poolm[:, g, k, :], start=(k == 0), stop=(k == 1))
                mm.then_inc(pool_mm, 1)
                pe.wait_ge(pool_d, 2 * i + 2)
                if i == 1:
                    pe.wait_ge(pool_ok, 4)
                for g in range(4):
                    mm = nc.tensor.matmul(T[:, 2 + g // 2, (g % 2) * S:(g % 2 + 1) * S], wpool[:, g, :], qT[:, 4 * i + g, :],
                                          start=True, stop=True)
                mm.then_inc(pool_y, 1)
            busy = [(pool_ok, 8)]
            busy = turn_stage("o_x", lambda i, t: Z[:, t, i * P:(i + 1) * P], busy)
            busy = turn_stage("o_c", lambda i, t: Z[:, t, NB + i * P:NB + (i + 1) * P], busy)
            free(busy)
            product("out_x0", HT, D)
            product("out_c0", HC, D)
            for k in range(4):
                busy = broadcast_row(k, busy)
            busy = norm_turn("hf_x0", "nf_x0", Y, busy)
            busy = norm_turn("hf_c0", "nf_c0", Z, busy)
            ffn("_x0", HT, busy)
            ffn("_c0", HC, [])
            busy = norm_turn("h_c1", "n_c1", Z, [])
            free(busy)
            product("kv_c1", HC, NB)
            busy = norm_turn("h_x1", "n_x1", Y, busy)
            free(busy)
            product("qkv_x1", HT, N_ODD)
            for k in (4, 5):
                busy = broadcast_row(k, busy)
            busy = turn_stage("q_1", lambda i, t: px[:, t, i * P:(i + 1) * P], busy, [(qk_ready, 3)])
            busy = turn_stage("k_1", lambda i, t: kd[:, 2 * (i // 4) + t, i % 4, :], busy)
            vcol1 = 1280
            busy = attention("a1x", lambda h, t: qT[half64(h), h // 2, t * P:(t + 1) * P],
                             lambda h, t: kT[half64(h), h // 4, :],
                             lambda h, k: (px, pc)[k // 2][:, k % 2, vcol1 + (h // 4) * HD:vcol1 + (h // 4 + 1) * HD], busy)
            busy = turn_stage("o_1", lambda i, t: Z[:, t, i * P:(i + 1) * P], busy)
            free(busy)
            product("out_x1", HT, D)
            busy = norm_turn("hf_x1", "nf_x1", Y, busy)
            ffn("_x1", HT, busy)

        @block.scalar
        def _(act):
            step = Steps(act, astep)

            act.dma_start(x[:, :, :], w["x"][0].rearrange("(t p) n -> p t n", p=P)).then_inc(x_in, 16)
            act.dma_start(ident[:, :], consts["ident"]).then_inc(sv_in, 16)
            for i, group in enumerate((SV1, SV2, SV3)):
                r = 0
                for name, n in group:
                    src = w[name]
                    if len(src.shape) == 1:
                        src = src.rearrange("(r n) -> r n", n=P)
                    elif len(src.shape) == 2:
                        src = src.rearrange("a (r n) -> (a r) n", n=P)
                    else:
                        src = src.rearrange("a b (r n) -> (a b r) n", n=P)
                    act.dma_start(svr[r:r + n, i, :], src).then_inc(sv_in, 16)
                    r += n
            act.dma_start(rope1[:, :, :, :], consts["rope1"]).then_inc(small_in, 16)
            act.dma_start(causal[:, :, :], consts["causal"]).then_inc(small_in, 16)
            act.dma_start(lnrow[:, 0, :], w["idx_k_ln_g"][0:1, :].to_broadcast((P, HD))).then_inc(small_in, 16)
            act.dma_start(lnrow[:, 1, :], w["idx_k_ln_b"][0:1, :].to_broadcast((P, HD))).then_inc(small_in, 16)
            act.wait_ge(bd_zero, 1)
            for m, name in ((bda, "rg_w_a"), (bdx, "rg_w_x")):
                v = w[name][0].rearrange("(c b) i j -> b i c j", b=2)
                for b in range(2):
                    act.dma_start(m[b * HD:(b + 1) * HD, :, b * HD:(b + 1) * HD], v[b]).then_inc(bd_in, 16)
            act.dma_start(bc[:, 0, :], w["norm_mix_post"][0:1, :].to_broadcast((P, D))).then_inc(late_in, 16)
            act.dma_start(bc[:, 1, :], w["norm_ffn_post"][0:1, :].to_broadcast((P, D))).then_inc(late_in, 16)
            act.dma_start(cx[:, :, :], w["ctx_2"][0].rearrange("(t p) n -> p t n", p=P)).then_inc(late_in, 16)
            act.dma_start(rope2[:, :, :, :], consts["rope2"]).then_inc(late_in, 16)
            act.dma_start(nsink[:, :], w["wo_sink_2"][0:1, :].to_broadcast((P, 16))).then_inc(late_in, 16)

            def square_sums(name, src, junk):
                k = sums[name]
                if k:
                    act.wait_ge(ss_done, k)
                for t in range(NT):
                    sq = nc.scalar.activation(junk[:, t, :], src[:, t, :], ACT.Square, accum_out=ssb[:, k % 2, t:t + 1])
                sq.then_inc(ss_done, 1)

            def norm_apply(name, src, dst):
                k = sums[name]
                act.wait_ge(rs_done, k + 1)
                nc.scalar.activation(dst[:, 1, :], src[:, 1, :], ACT.Copy, scale=rs[:, k % 2, 1:2]).then_inc(xn_act, 1)

            def turn_evict(name, dst, scale=None, bias=None):
                c0, n = turn[name][0], turn_n[name]
                for i in [i for i in range(n) if i // 2 % 2 == 0]:
                    act.wait_ge(turned, c0 + min(i // 2 * 2 + 2, n))
                    src = T[:, i // 2, (i % 2) * S:(i % 2 + 1) * S]
                    if scale is None:
                        ins = nc.scalar.activation(dst(i), src, ACT.Copy)
                    elif bias is None:
                        ins = nc.scalar.activation(dst(i), src, ACT.Copy, scale=scale(i))
                    else:
                        ins = nc.scalar.activation(dst(i), src, ACT.Identity, scale=scale(i), bias=bias(i))
                    ins.then_inc(turn_act, 1)

            def product_evict(name, dst, total):
                s0, e0 = prod[name]
                for b in range(-(-total // NB)):
                    n = min(NB, total - b * NB)
                    act.wait_ge(slot_read, s0 + 2 * b + 2)
                    nc.scalar.activation(dst[:, 0, b * NB:b * NB + n], G[:, 2 * ((e0 + b) % 2), 0:n], ACT.Copy).then_inc(ev_act, 1)

            def in_loop(name, col0, nblocks):
                s0, e0 = prod[name]
                with act.Fori(0, nblocks // 2) as it:
                    for j in range(2):
                        act.wait_ge(slot_read, it * 4 + (s0 + 2 * j + 2))
                        nc.scalar.activation(proj[:, 0, bass.ds(it * 1024 + (col0 + j * NB), NB)], G[:, 2 * ((e0 + j) % 2), :],
                                             ACT.Copy).then_inc(ev_act, 1)

            def mod_evict(g):
                s0, e0 = prod[f"mod{g}"]
                act.wait_ge(slot_read, s0 + MODG)
                nc.scalar.activation(modrow_of(g), G[:, 2 * (e0 % 2), :], ACT.Copy).then_inc(ev_act, 1)

            def ffn(name):
                f = ffn_i[name]
                s0, e0 = prod["up" + name]
                h0 = FB * f

                def silu(j, it=None):
                    more = 0 if it is None else it
                    act.wait_ge(slot_read, more * 4 + (s0 + 2 * j + 2))
                    act.wait_ge(ev_dve, more * 2 + (e0 + j - 1))
                    p = (e0 + j) % 2
                    nc.scalar.activation(gate[:, j % 2, :, :], G[:, 2 * p:2 * p + 2, 0:S], ACT.Silu).then_inc(ev_act, 1)

                def hid_out(j, it=None):
                    act.wait_ge(hid_turned, (0 if it is None else it * 2) + (h0 + j + 1))
                    dst = hidT[:, 2 * j:2 * j + 2, :] if it is None else hidT[:, bass.ds(it * 4 + 2 * j, 2), :]
                    nc.scalar.activation(dst, T[:, j % 2, :].rearrange("p (c n) -> p c n", c=2), ACT.Copy).then_inc(hidT_ok, 1)

                silu(0)
                with act.Fori(0, FB // 2) as it:
                    silu(1, it)
                    hid_out(0, it)
                    silu(2, it)
                    hid_out(1, it)
                hid_out(FB - 1)
                s0, e0 = prod["down" + name]
                act.wait_ge(slot_read, s0 + FC // 2)

            def down_evict(name, dst):
                e0 = prod["down" + name][1]
                for h in range(2):
                    nc.scalar.activation(dst[:, 0, h * NB:(h + 1) * NB], G[:, 2 * ((e0 + h) % 2), :], ACT.Copy).then_inc(ev_act, 1)

            def attention(name, last_o=False):
                heads, nks = [a[1:] for a in ATTN if a[0] == name][0]
                u0 = att0[name][0]
                n = 2 * heads
                extra = 1 if name == "a1x" else 0

                for u in range(n + 1):
                    if u < n:
                        t = (u // 2) % 2
                        act.wait_ge(a_min, u0 + u + 1)
                        if u >= 4:
                            act.wait_ge(a_o, u0 + u - 3)
                        wv = work[:, u % 4, 0:nks[t] + extra]
                        nc.scalar.activation(wv, wv, ACT.Exp, scale=-1.0, bias=amin[:, u % 4:u % 4 + 1],
                                             accum_out=asum[:, u % 4:u % 4 + 1]).then_inc(a_exp, 1)
                    if u >= 1:
                        t = ((u - 1) // 2) % 2
                        act.wait_ge(a_turned, u0 + u)
                        if u - 1 >= 4:
                            act.wait_ge(a_pv, u0 + u - 4)
                        nc.scalar.activation(pT[:, (u - 1) % 4, 0:nks[t]], T[:, 2, 0:nks[t]], ACT.Copy).then_inc(a_pT, 1)

            act.wait_ge(x_in, 16)
            square_sums("n1", x, Y)
            act.wait_ge(sv_done, 1)
            act.wait_ge(bd_zero, 1)
            for i, name in enumerate(("c_2", "c_ctx_2")):
                ins = nc.scalar.activation(scT[:, :, i], cols[name], ACT.Silu)
            ins.then_inc(c_silu, 1)
            norm_apply("n1", x, Y)
            turn_evict("h1", lambda i: HT[:, i, :], lambda i: cols["norm_mix_pre"][:, i:i + 1])
            act.wait_ge(softp_z, 1)
            nc.scalar.activation(c8[:, 1, :], c8[:, 0, :], ACT.Exp, scale=-1.0).then_inc(softp_e, 1)
            in_loop("in_a", 0, 8)
            s0, e0 = prod["in_tail"]
            act.wait_ge(slot_read, s0 + 2)
            nc.scalar.activation(proj[:, 0, C_IK:C_GA], G[:, 2 * (e0 % 2), 0:C_GA - C_IK], ACT.Copy).then_inc(ev_act, 1)
            in_loop("in_b", C_GA, 4)
            turn_evict("xr", lambda i: xpad[:, i, 3:259])
            act.wait_ge(gelu_in, 1)
            nc.scalar.activation(Y[:, :, :], Y[:, :, :], ACT.Tanh, scale=math.sqrt(2.0 / math.pi)).then_inc(gelu_t, 1)
            act.wait_ge(ev_act, prod["in_b"][1] + 4)
            act.wait_ge(ev_dve, prod["in_b"][1] + 4)
            nc.scalar.activation(proj[:, :, C_GA:N_IN], proj[:, :, C_GA:N_IN], ACT.Sigmoid).then_inc(sg_ready, 1)
            act.wait_ge(softp, 1)
            for c in range(8):
                act.wait_ge(rnn_gate, c + 1)
                nc.scalar.activation(R1[:, c, :], T[:, c % 4, 0:S], ACT.Sigmoid, bias=cols["rg_b_a"][:, c:c + 1])
                nc.scalar.activation(R2[:, c, :], T[:, c % 4, S:2 * S], ACT.Sigmoid, bias=cols["rg_b_x"][:, c:c + 1]).then_inc(rnn_sig, 1)
            act.wait_ge(rnn_sig, 8)
            for c in range(8):
                step(nc.scalar.activation(R3[:, c, :], R1[:, c, :], ACT.Tanh, scale=c8[:, 8, c:c + 1]))
            step.wait()
            for c in range(8):
                ins = nc.scalar.activation(R1[:, c, :], R1[:, c, :], ACT.Exp, scale=c8[:, 9, c:c + 1])
            ins.then_inc(rnn_ta, 1)
            turn_evict("q", lambda i: qT[:, i, :])
            turn_evict("kiq", lambda i: kT[:, i, 0:S] if i < 4 else kT[:, i - 4, S:2 * S])
            turn_evict("ik", lambda i: ikT[:, :])
            for u in range(16):
                nk = P * (u % 2 + 1)
                act.wait_ge(idx_mm, u + 1)
                if u >= 4:
                    act.wait_ge(idx_acc, u - 3)
                nc.scalar.activation(yf[:, (u % 4) * S:(u % 4) * S + nk], T[:, u % 4, 0:nk], ACT.Relu).then_inc(idx_relu, 1)
            act.wait_ge(rnn_sq, 1)
            nc.scalar.activation(R3[:, :, :], R3[:, :, :], ACT.Sqrt).then_inc(rnn_root, 1)
            mod_evict_order = (0, 1, 2)
            act.wait_ge(rnn_scan, 1)
            turn_evict("gr", lambda i: R2[:, i, :])
            act.wait_ge(rnn_y, 1)
            for g in mod_evict_order:
                mod_evict(g)
            attention("a1")
            product_evict("y_a", Y, D)
            turn_evict("o1", lambda i: HT[:, i, :])
            mod_evict(3)
            product_evict("y_b", proj[:, :, C_Q:C_Q + D], D)
            turn_evict("mrg", lambda i: qT[:, i, :])
            product_evict("w_o", Y, D)
            act.wait_ge(ev_act, prod["w_o"][1] + 2)
            act.wait_ge(ev_dve, prod["w_o"][1] + 2)
            square_sums("p1", Y, Z)
            act.wait_ge(x_new, 1)
            square_sums("nf1", x, Y)
            norm_apply("nf1", x, Y)
            act.wait_ge(mod_ok, 1)
            mod_evict(4)
            turn_evict("hf1", lambda i: HT[:, i, :], lambda i: cols["norm_ffn_pre"][:, i:i + 1])
            ffn("1")
            down_evict("1", Y)
            act.wait_ge(ev_act, prod["down1"][1] + 2)
            act.wait_ge(ev_dve, prod["down1"][1] + 2)
            square_sums("pf1", Y, Z)
            act.dma_start(band[:, :, :], consts["band"]).then_inc(band_in, 16)
            act.dma_start(qkgain[:, 0:512].rearrange("p (h n) -> p h n", h=8),
                          w["we_q_gain_2"][0:1, :].unsqueeze(1).to_broadcast((P, 8, HD))).then_inc(band_in, 16)
            act.dma_start(qkgain[:, 512:640].rearrange("p (h n) -> p h n", h=2),
                          w["we_k_gain_2"][0:1, :].unsqueeze(1).to_broadcast((P, 2, HD))).then_inc(band_in, 16)
            act.dma_start(poolm[:, :, :, :], consts["pool"]).then_inc(pool_in, 16)
            act.dma_start(wpool[:, :, :], w["we_pool_2"][0].rearrange("g c d -> c g d")).then_inc(pool_in, 16)
            act.wait_ge(mod_ok, 2)
            mod_evict(5)
            act.wait_ge(late_in, 16 * 5)
            act.wait_ge(x_new, 2)
            square_sums("n_c0", cx, Z)
            norm_apply("n_c0", cx, Z)
            square_sums("n_x0", x, Y)
            norm_apply("n_x0", x, Y)
            act.wait_ge(hs_ok, 1)
            turn_evict("h_c0", lambda i: HC[:, i, :], lambda i: hscale[:, 0, 0, 1, i:i + 1], lambda i: modcol[:, 0, i, 1:2])
            product_evict("qkv_c0", pc, N_EVEN)
            turn_evict("h_x0", lambda i: HT[:, i, :], lambda i: hscale[:, 0, 0, 0, i:i + 1], lambda i: modcol[:, 0, i, 0:1])
            product_evict("qkv_x0", px, N_EVEN)
            turn_evict("q_xc", lambda i: qT[:, i, :])
            turn_evict("k_xc", lambda i: kT[:, i % 2, (i // 2) * S:(i // 2 + 1) * S])
            attention("ax")
            attention("ac")
            for i, dst in enumerate((HT, HC)):
                act.wait_ge(pool_mm, i + 1)
                nc.scalar.activation(qT[:, 4 * i:4 * i + 2, :], T[:, 0, :].rearrange("p (g n) -> p g n", g=2), ACT.Copy).then_inc(pool_d, 1)
                act.wait_ge(pool_y, i + 1)
                for g in range(2):
                    nc.scalar.activation(dst[:, 4 + g, :], T[:, 2, g * S:(g + 1) * S], ACT.Copy,
                                         scale=cols["we_pool_scale_2"][:, g:g + 1]).then_inc(pool_ok, 1)
            turn_evict("o_x", lambda i: HT[:, i, :])
            turn_evict("o_c", lambda i: HC[:, i, :])
            product_evict("out_x0", Y, D)
            act.wait_ge(turn_act, turn["o_c"][1] + 2)
            act.wait_ge(turn_dve, turn["o_c"][2] + 2)
            product_evict("out_c0", Z, D)
            for c, (nm, src) in enumerate((("p_x0", Y), ("p_c0", Z))):
                e = prod["out_x0" if c == 0 else "out_c0"][1] + 2
                act.wait_ge(ev_act, e)
                act.wait_ge(ev_dve, e)
                square_sums(nm, src, kT_junk)
            for nm, src, dst in (("nf_x0", x, Y), ("nf_c0", cx, Z)):
                act.wait_ge(x_new, 4)
                square_sums(nm, src, dst)
                norm_apply(nm, src, dst)
            turn_evict("hf_x0", lambda i: HT[:, i, :], lambda i: hscale[:, 0, 1, 0, i:i + 1], lambda i: modcol[:, 0, 24 + i, 0:1])
            turn_evict("hf_c0", lambda i: HC[:, i, :], lambda i: hscale[:, 0, 1, 1, i:i + 1], lambda i: modcol[:, 0, 24 + i, 1:2])
            ffn("_x0")
            down_evict("_x0", Y)
            act.wait_ge(ev_act, prod["down_x0"][1] + 2)
            act.wait_ge(ev_dve, prod["down_x0"][1] + 2)
            square_sums("pf_x0", Y, kT_junk)
            ffn("_c0")
            down_evict("_c0", Z)
            act.wait_ge(ev_act, prod["down_c0"][1] + 2)
            act.wait_ge(ev_dve, prod["down_c0"][1] + 2)
            square_sums("pf_c0", Z, kT_junk)
            act.wait_ge(x_new, 6)
            for nm, src, dst in (("n_c1", cx, Z), ("n_x1", x, Y)):
                square_sums(nm, src, dst)
                norm_apply(nm, src, dst)
            act.wait_ge(hs_ok, 2)
            turn_evict("h_c1", lambda i: HC[:, i, :], lambda i: hscale[:, 1, 0, 1, i:i + 1], lambda i: modcol[:, 1, i, 1:2])
            product_evict("kv_c1", pc[:, :, D:N_ODD], NB)
            turn_evict("h_x1", lambda i: HT[:, i, :], lambda i: hscale[:, 1, 0, 0, i:i + 1], lambda i: modcol[:, 1, i, 0:1])
            product_evict("qkv_x1", px, N_ODD)
            turn_evict("q_1", lambda i: qT[:, i, :])
            turn_evict("k_1", lambda i: kT[:, i % 4, (i // 4) * S:(i // 4 + 1) * S])
            attention("a1x")
            turn_evict("o_1", lambda i: HT[:, i, :])
            product_evict("out_x1", Y, D)
            act.wait_ge(ev_act, prod["out_x1"][1] + 2)
            act.wait_ge(ev_dve, prod["out_x1"][1] + 2)
            square_sums("p_x1", Y, kT_junk)
            act.wait_ge(x_new, 7)
            square_sums("nf_x1", x, Y)
            norm_apply("nf_x1", x, Y)
            turn_evict("hf_x1", lambda i: HT[:, i, :], lambda i: hscale[:, 1, 1, 0, i:i + 1], lambda i: modcol[:, 1, 24 + i, 0:1])
            ffn("_x1")
            down_evict("_x1", Y)
            act.wait_ge(ev_act, prod["down_x1"][1] + 2)
            act.wait_ge(ev_dve, prod["down_x1"][1] + 2)
            square_sums("pf_x1", Y, kT_junk)

        @block.gpsimd
        def _(pool):
            step = Steps(pool, pstep)
            nc.gpsimd.memset(scT[:, :, :], 0.0)
            nc.gpsimd.memset(ones[:, :], 1.0)
            nc.gpsimd.memset(bd[:, :], 0.0)
            nc.gpsimd.memset(xpad[:, :, 0:3], 0.0).then_inc(bd_zero, 1)
            gr = proj[:, :, C_GR:C_GR + D]
            pool.wait_ge(ev_act, 4)
            pool.wait_ge(ev_dve, 4)
            step(nc.gpsimd.tensor_tensor(Y[:, :, :], gr, gr, ALU.mult))
            step.wait()
            step(nc.gpsimd.tensor_scalar(Y[:, :, :], Y[:, :, :], 0.044715, 1.0, ALU.mult, ALU.add))
            step.wait()
            nc.gpsimd.tensor_tensor(Y[:, :, :], Y[:, :, :], gr, ALU.mult).then_inc(gelu_in, 1)
            pool.wait_ge(gelu_t, 1)
            step(nc.gpsimd.tensor_scalar(Y[:, :, :], Y[:, :, :], 1.0, 1.0, ALU.mult, ALU.add))
            step.wait()
            nc.gpsimd.tensor_tensor(gr, Y[:, :, :], gr, ALU.mult).then_inc(gelu_ok, 1)

        @block.vector
        def _(dve):
            step = Steps(dve, dstep)
            V = nc.vector

            def rsqrt(dst, ss, n, count):
                v, i, y, a = [rq[:, j, 0:n] for j in range(4)]
                step.wait()
                step(V.tensor_scalar(v, ss, 1.0 / count, EPS, ALU.mult, ALU.add))
                step.wait()
                step(V.tensor_scalar(i.bitcast(I32), v.bitcast(I32), 1, None, ALU.logical_shift_right))
                step.wait()
                step(V.tensor_scalar(y.bitcast(I32), i.bitcast(I32), -1.0, float(0x5F3759DF), ALU.mult, ALU.add))
                for r in range(3):
                    step.wait()
                    step(V.tensor_tensor(a, y, y, ALU.mult))
                    step.wait()
                    step(V.scalar_tensor_tensor(a, a, -0.5, v, ALU.mult, ALU.mult))
                    step.wait()
                    if r < 2:
                        step(V.scalar_tensor_tensor(y, a, 1.5, y, ALU.add, ALU.mult))
                return V.scalar_tensor_tensor(dst, a, 1.5, y, ALU.add, ALU.mult)

            def inverse_rms(name):
                k = sums[name]
                dve.wait_ge(ss_done, k + 1)
                rsqrt(rs[:, k % 2, :], ssb[:, k % 2, :], 2, D).then_inc(rs_done, 1)
                dve.wait_ge(rs_done, k + 1)

            def norm(name, src, dst):
                inverse_rms(name)
                V.tensor_scalar(dst[:, 0, :], src[:, 0, :], rs[:, sums[name] % 2, 0:1], None, ALU.mult).then_inc(xn_dve, 1)

            def residual(name, y, row, dst):
                inverse_rms(name)
                for t in range(NT):
                    step(V.scalar_tensor_tensor(y[:, t, :], y[:, t, :], rs[:, sums[name] % 2, t:t + 1], row, ALU.mult, ALU.mult))
                step.wait()
                V.tensor_tensor(dst[:, :, :], dst[:, :, :], y[:, :, :], ALU.add).then_inc(x_new, 1)
                n_x = [n for n in SUMS if n[0] == "p"].index(name) + 1
                dve.wait_ge(x_new, n_x)

            def turn_evict(name, dst, scale=None, bias=None):
                c0, n = turn[name][0], turn_n[name]
                for i in [i for i in range(n) if i // 2 % 2]:
                    dve.wait_ge(turned, c0 + i // 2 * 2 + 2)
                    src = T[:, i // 2, (i % 2) * S:(i % 2 + 1) * S]
                    if scale is None:
                        ins = V.tensor_copy(dst(i), src)
                    elif bias is None:
                        ins = V.tensor_scalar(dst(i), src, scale(i), None, ALU.mult)
                    else:
                        ins = V.tensor_scalar(dst(i), src, scale(i), bias(i), ALU.mult, ALU.add)
                    ins.then_inc(turn_dve, 1)

            def product_evict(name, dst, total):
                s0, e0 = prod[name]
                for b in range(-(-total // NB)):
                    n = min(NB, total - b * NB)
                    dve.wait_ge(slot_read, s0 + 2 * b + 2)
                    V.tensor_copy(dst[:, 1, b * NB:b * NB + n], G[:, 2 * ((e0 + b) % 2) + 1, 0:n]).then_inc(ev_dve, 1)

            def evicted(name):
                e = prod[name][1] + [p for p in PRODUCTS if p[0] == name][0][2]
                dve.wait_ge(ev_act, e)
                dve.wait_ge(ev_dve, e)

            def in_loop(name, col0, nblocks):
                s0, e0 = prod[name]
                with dve.Fori(0, nblocks // 2) as it:
                    for j in range(2):
                        dve.wait_ge(slot_read, it * 4 + (s0 + 2 * j + 2))
                        V.tensor_copy(proj[:, 1, bass.ds(it * 1024 + (col0 + j * NB), NB)],
                                      G[:, 2 * ((e0 + j) % 2) + 1, :]).then_inc(ev_dve, 1)

            def mod_evict(g):
                V.engine_nop().then_inc(ev_dve, 1)

            def mod_columns(g):
                lyr, i0 = g // 3, (g % 3) * 16
                dve.wait_ge(mod_turned, g + 1)
                V.tensor_tensor(modcol[:, lyr, i0:i0 + 16, :].rearrange("p (j c) r -> p c j r", j=4),
                                T[:, g % 4, :].rearrange("p (c j r) -> p c j r", c=4, j=4)[:, :, :, 0:2],
                                cols["b_mod_2"][:, lyr * 48 + i0:lyr * 48 + i0 + 16].rearrange("p (j c) -> p c j", j=4)
                                .unsqueeze(3).to_broadcast((P, 4, 4, 2)), ALU.add).then_inc(mod_ok, 1)

            def mod_scales(lyr):
                dve.wait_ge(mod_ok, 3 * lyr + 3)
                for f, (pre, post) in enumerate((("g_pre_mix_2", "g_post_mix_2"), ("g_pre_ffn_2", "g_post_ffn_2"))):
                    for r in range(2):
                        step(V.scalar_tensor_tensor(hscale[:, lyr, f, r, :], modcol[:, lyr, 24 * f + 8:24 * f + 16, r], 1.0,
                                                    cols[pre][:, 8 * lyr:8 * lyr + 8], ALU.add, ALU.mult))
                        ins = V.tensor_tensor(gtg[:, lyr, f, r, :], modcol[:, lyr, 24 * f + 16:24 * f + 24, r],
                                              cols[post][:, 8 * lyr:8 * lyr + 8], ALU.mult)
                        if (f, r) != (1, 1):
                            step(ins)
                ins.then_inc(hs_ok, 1)
                dve.wait_ge(hs_ok, lyr + 1)

            def broadcast_row(k, col, dst):
                if k >= 1:
                    dve.wait_ge(bc_mm, k)
                for c in range(KC):
                    ins = V.tensor_scalar(diag[:, c, :], ident[:, :], col[:, c:c + 1], None, ALU.mult)
                ins.then_inc(diag_ok, 1)
                dve.wait_ge(bc_mm, k + 1)
                V.tensor_copy(dst.rearrange("p (b n) -> p b n", b=2), T[:, 0:2, :]).then_inc(bc_ok, 1)
                dve.wait_ge(bc_ok, k + 1)

            def rope(first, second, cos, sin, shape):
                n = int(np.prod(shape))
                def tmp(i):
                    v = zf[:, 2048 - (i + 1) * n:2048 - i * n]
                    if len(shape) == 2:
                        return v.rearrange("p (h d) -> p h d", h=shape[0])
                    return v.rearrange("p (h a d) -> p h a d", h=shape[0], a=shape[1])
                step.wait()
                step(V.tensor_tensor(tmp(0), first, cos, ALU.mult))
                step(V.tensor_tensor(tmp(1), second, sin, ALU.mult))
                step(V.tensor_tensor(tmp(2), first, sin, ALU.mult))
                step.wait()
                step(V.tensor_tensor(first, tmp(0), tmp(1), ALU.subtract))
                step.wait()
                step(V.tensor_tensor(tmp(0), second, cos, ALU.mult))
                step.wait()
                step(V.tensor_tensor(second, tmp(0), tmp(2), ALU.add))

            def rope_small(src, t, heads):
                v = src.rearrange("p (h d) -> p h d", h=heads)
                c, s = [rope1[:, t, i, :].unsqueeze(1).to_broadcast((P, heads, 8)) for i in range(2)]
                rope(v[:, :, 0:8], v[:, :, 8:16], c, s, (heads, 8))

            def rope_axial(src, t, heads):
                v = src.rearrange("p (h a b d) -> p h a b d", h=heads, a=2, b=2)
                c, s = [rope2[:, t, i, :].rearrange("p (a d) -> p a d", a=2).unsqueeze(1).to_broadcast((P, heads, 2, 16))
                        for i in range(2)]
                rope(v[:, :, :, 0, :], v[:, :, :, 1, :], c, s, (heads, 2, 16))

            def double_keys(k0, src, groups):
                for b in range(2):
                    ins = V.tensor_copy(kd[:, k0:k0 + NT, 0:groups, b * HD:(b + 1) * HD],
                                        src.rearrange("p t (g d) -> p t g d", g=groups))
                    step(ins)

            def ffn(name):
                f = ffn_i[name]
                e0 = prod["up" + name][1]
                h0 = FB * f

                def hidden(j, it=None):
                    more = 0 if it is None else it
                    dve.wait_ge(ev_act, more * 2 + (e0 + j + 1))
                    if it is not None or j >= 2:
                        dve.wait_ge(hid_turned, more * 2 + (h0 + j - 1))
                    p = (e0 + j) % 2
                    V.tensor_tensor(hid[:, j % 2, :, :], gate[:, j % 2, :, :], G[:, 2 * p:2 * p + 2, S:NB],
                                    ALU.mult).then_inc(ev_dve, 1)

                hidden(0)
                hidden(1)
                hidden(2)
                with dve.Fori(1, FB // 2) as it:
                    hidden(1, it)
                    hidden(2, it)

            def down_evict(name, dst):
                s0, e0 = prod["down" + name]
                dve.wait_ge(slot_read, s0 + FC // 2)
                for h in range(2):
                    V.tensor_copy(dst[:, 1, h * NB:(h + 1) * NB], G[:, 2 * ((e0 + h) % 2) + 1, :]).then_inc(ev_dve, 1)

            def attention(name, mask, o_col):
                heads, nks = [a[1:] for a in ATTN if a[0] == name][0]
                u0 = att0[name][0]
                n = 2 * heads
                step.wait()
                for u in range(n + 3):
                    if u < n:
                        h, t = 2 * (u // 4) + u % 2, (u // 2) % 2
                        b = u % 4
                        dve.wait_ge(a_mm, u0 + u + 1)
                        if u >= 4:
                            dve.wait_ge(a_turned, u0 + u - 3)
                        src, dst, low = T[:, u % 2, 0:nks[t]], work[:, b, 0:nks[t]], amin[:, b:b + 1]
                        if mask is None:
                            ins = V.tensor_scalar(dst, src, -SCALE, None, ALU.mult, ALU.min, accum_out=low)
                        else:
                            ins = V.tensor_tensor_reduce(dst, src, mask[:, t, 0:nks[t]], -SCALE, 3e38, ALU.add, ALU.min, low)
                        if name == "a1x":
                            step(ins)
                            step(V.tensor_copy(work[:, b, nks[t]:nks[t] + 1], nsink[:, h:h + 1]))
                            step.wait(1)
                            ins = V.tensor_tensor(low, low, nsink[:, h:h + 1], ALU.min)
                        ins.then_inc(a_min, 1)
                    if u >= 3:
                        v = u - 3
                        h, t = 2 * (v // 4) + v % 2, (v // 2) % 2
                        dve.wait_ge(a_pv, u0 + v + 1)
                        step(V.reciprocal(arec[:, v % 4:v % 4 + 1], asum[:, v % 4:v % 4 + 1]))
                        step.wait()
                        V.tensor_scalar(Z[:, t, o_col + h * HD:o_col + (h + 1) * HD], T[:, 3, (v % 2) * HD:(v % 2 + 1) * HD],
                                        arec[:, v % 4:v % 4 + 1], None, ALU.mult).then_inc(a_o, 1)

            norm("n1", x, Y)
            dve.wait_ge(sv_turned, 1)
            step(V.tensor_copy(svc[:, 0:164], T[:, 0, 0:164]))
            V.tensor_copy(svc[:, 164:260], T[:, 0, 2 * P:2 * P + 96]).then_inc(sv_done, 1)
            step.wait()
            turn_evict("h1", lambda i: HT[:, i, :], lambda i: cols["norm_mix_pre"][:, i:i + 1])
            lam = cols["rg_lambda"]
            V.scalar_tensor_tensor(c8[:, 0, :], lam, -1.0, lam, ALU.mult, ALU.max).then_inc(softp_z, 1)
            dve.wait_ge(softp_e, 1)
            step(V.tensor_scalar(c8[:, 2, :], c8[:, 1, :], 2.0, None, ALU.add))
            step.wait()
            step(V.reciprocal(c8[:, 3, :], c8[:, 2, :]))
            step.wait()
            step(V.tensor_tensor(c8[:, 4, :], c8[:, 1, :], c8[:, 3, :], ALU.mult))
            step.wait()
            step(V.tensor_tensor(c8[:, 5, :], c8[:, 4, :], c8[:, 4, :], ALU.mult))
            step.wait()
            step(V.tensor_scalar(c8[:, 6, :], c8[:, 5, :], 1.0 / 19, None, ALU.mult))
            for d in (17, 15, 13, 11, 9, 7, 5, 3):
                step.wait()
                step(V.scalar_tensor_tensor(c8[:, 6, :], c8[:, 6, :], 1.0 / d, c8[:, 5, :], ALU.add, ALU.mult))
            step.wait()
            step(V.scalar_tensor_tensor(c8[:, 6, :], c8[:, 6, :], 1.0, c8[:, 4, :], ALU.add, ALU.mult))
            step(V.tensor_scalar(c8[:, 7, :], lam, -8.0, 0.0, ALU.mult, ALU.max))
            step.wait()
            step(V.scalar_tensor_tensor(c8[:, 8, :], c8[:, 6, :], 16.0, c8[:, 7, :], ALU.mult, ALU.add))
            step.wait()
            V.tensor_scalar(c8[:, 9, :], c8[:, 8, :], -1.0, None, ALU.mult).then_inc(softp, 1)
            in_loop("in_a", 0, 8)
            s0, e0 = prod["in_tail"]
            dve.wait_ge(slot_read, s0 + 2)
            V.tensor_copy(proj[:, 1, C_IK:C_GA], G[:, 2 * (e0 % 2) + 1, 0:C_GA - C_IK]).then_inc(ev_dve, 1)
            in_loop("in_b", C_GA, 4)
            turn_evict("xr", lambda i: xpad[:, i, 3:259])
            dve.wait_ge(turn_act, turn["xr"][1] + 4)
            dve.wait_ge(turn_dve, turn["xr"][2] + 4)
            dve.wait_ge(bd_zero, 1)
            cw, cb = cols["conv_w"], cols["conv_b"]
            for c in range(8):
                step(V.tensor_scalar(xc[:, c, :], xpad[:, c, 0:S], cw[:, c:c + 1], cb[:, c:c + 1], ALU.mult, ALU.add))
            for k in range(1, 4):
                for c in range(8):
                    step.wait(7 if k < 3 else 7 - c)
                    ins = V.scalar_tensor_tensor(xc[:, c, :], xpad[:, c, k:k + S], cw[:, 8 * k + c:8 * k + c + 1],
                                                 xc[:, c, :], ALU.mult, ALU.add)
                    if k < 3:
                        step(ins)
                    else:
                        ins.then_inc(rnn_xc, 1)
            dve.wait_ge(small_in, 16 * 4)
            evicted("in_b")
            ik = proj[:, :, C_IK:C_IK + HD]
            step(V.tensor_reduce(rq[:, 4, 0:2], ik, AX.X, ALU.add))
            step.wait()
            step(V.tensor_scalar(rq[:, 4, 2:4], rq[:, 4, 0:2], 1.0 / HD, None, ALU.mult))
            step.wait()
            for t in range(NT):
                step(V.tensor_scalar(ik[:, t, :], ik[:, t, :], rq[:, 4, 2 + t:3 + t], None, ALU.subtract))
            step.wait()
            ik2 = zf[:, 1024:1024 + NT * HD].rearrange("p (t d) -> p t d", t=NT)
            step(V.tensor_tensor(ik2, ik, ik, ALU.mult))
            step.wait()
            step(V.tensor_reduce(rq[:, 4, 4:6], ik2, AX.X, ALU.add))
            step(rsqrt(rq[:, 4, 6:8], rq[:, 4, 4:6], 2, HD))
            step.wait()
            for t in range(NT):
                step(V.scalar_tensor_tensor(ik[:, t, :], ik[:, t, :], rq[:, 4, 6 + t:7 + t], lnrow[:, 0, :], ALU.mult, ALU.mult))
            step.wait()
            step(V.tensor_tensor(ik, ik, lnrow[:, 1, :].unsqueeze(1).to_broadcast((P, NT, HD)), ALU.add))
            step(V.tensor_scalar(iws[:, :, :], proj[:, :, C_IW:C_IW + 8], IDX_SCALE, None, ALU.mult))
            for t in range(NT):
                rope_small(proj[:, t, C_Q:C_V], t, 20)
                rope_small(proj[:, t, C_IQ:C_IW], t, 9)
            step.wait()
            dve.wait_ge(gelu_ok, 1)
            double_keys(0, proj[:, :, C_K:C_V], 4)
            for b in range(2):
                step(V.tensor_copy(ikd[:, :, b * HD:(b + 1) * HD], ik))
            step.wait()
            V.engine_nop().then_inc(qk_ready, 1)
            turn_evict("q", lambda i: qT[:, i, :])
            turn_evict("kiq", lambda i: kT[:, i, 0:S] if i < 4 else kT[:, i - 4, S:2 * S])
            def score(t, b):
                return zf[:, t * NB + b * S:t * NB + b * S + P * (t + 1)]
            for u in range(16):
                h, t = u // 2, u % 2
                nk = P * (t + 1)
                dve.wait_ge(idx_relu, u + 1)
                if u >= 2:
                    dve.wait_ge(idx_acc, u - 1)
                V.scalar_tensor_tensor(score(t, 0), yf[:, (u % 4) * S:(u % 4) * S + nk], iws[:, t, h:h + 1],
                                       causal[:, t, 0:nk] if h == 0 else score(t, 0), ALU.mult, ALU.add).then_inc(idx_acc, 1)
            dve.wait_ge(rnn_ta, 1)
            dve.wait_ge(rnn_sig, 8)
            step(V.tensor_tensor(R2[:, :, :], R2[:, :, :], xc[:, :, :], ALU.mult))
            step.wait()
            step(V.tensor_scalar(xc[:, :, :], R3[:, :, :], 1.0, None, ALU.add))
            step.wait()
            step(V.reciprocal(xc[:, :, :], xc[:, :, :]))
            step.wait()
            step(V.scalar_tensor_tensor(R3[:, :, :], R3[:, :, :], 2.0, xc[:, :, :], ALU.mult, ALU.mult))
            step.wait()
            V.tensor_scalar(R3[:, :, :], R3[:, :, :], 1e-30, None, ALU.max).then_inc(rnn_sq, 1)
            dve.wait_ge(idx_acc, 16)
            for r in range(TOPK // 8):
                for t in range(NT):
                    if r:
                        step.wait(1)
                    step(V.max(top8[:, t, :], score(t, r % 2)))
                for t in range(NT):
                    step.wait(1)
                    step(V.match_replace(score(t, 1 - r % 2), top8[:, t, :], score(t, r % 2), TAKEN))
            step.wait()
            for t in range(NT):
                step(V.tensor_scalar(bias1[:, t, 0:P * (t + 1)], score(t, 0), -2e38, MASKED, ALU.is_gt, ALU.mult))
            step.wait()
            for t in range(NT):
                step(V.tensor_tensor(bias1[:, t, 0:P * (t + 1)], bias1[:, t, 0:P * (t + 1)], causal[:, t, 0:P * (t + 1)], ALU.add))
            dve.wait_ge(rnn_root, 1)
            step(V.tensor_tensor(R2[:, :, :], R2[:, :, :], R3[:, :, :], ALU.mult))
            step.wait()
            for c in range(8):
                ins = V.tensor_tensor_scan(xc[:, c, :], R1[:, c, :], R2[:, c, :], 0.0, ALU.mult, ALU.add)
            ins.then_inc(rnn_scan, 1)
            dve.wait_ge(rnn_scan, 1)
            for c in range(8):
                if c // 2 % 2:
                    dve.wait_ge(turned, turn["gr"][0] + c // 2 * 2 + 2)
                    V.scalar_tensor_tensor(R3[:, c, :], xc[:, c, :], 0.5, T[:, c // 2, (c % 2) * S:(c % 2 + 1) * S],
                                           ALU.mult, ALU.mult).then_inc(turn_dve, 1)
                else:
                    dve.wait_ge(turn_act, turn["gr"][1] + 2 * (c // 4) + c % 2 + 1)
                    step(V.scalar_tensor_tensor(R3[:, c, :], xc[:, c, :], 0.5, R2[:, c, :], ALU.mult, ALU.mult))
            step.wait()
            dve.wait_ge(turn_dve, turn["gr"][2] + 4)
            V.engine_nop().then_inc(rnn_y, 1)
            for g in range(3):
                mod_evict(g)
            attention("a1", bias1, 0)
            dve.wait_ge(sg_ready, 1)
            yb = proj[:, :, C_Q:C_Q + D]

            def gated(name, dst, gcol):
                s0, e0 = prod[name]
                for b in range(2):
                    c = slice(b * NB, (b + 1) * NB)
                    dve.wait_ge(slot_read, s0 + 2 * b + 2)
                    V.tensor_tensor(dst[:, 1, c], G[:, 2 * ((e0 + b) % 2) + 1, :],
                                    proj[:, 1, gcol + b * NB:gcol + (b + 1) * NB], ALU.mult).then_inc(ev_dve, 1)
                evicted(name)
                step(V.tensor_tensor(dst[:, 0, :], dst[:, 0, :], proj[:, 0, gcol:gcol + D], ALU.mult))

            gated("y_a", Y, C_GA)
            turn_evict("o1", lambda i: HT[:, i, :])
            mod_evict(3)
            gated("y_b", yb, C_GB)
            step.wait()
            V.tensor_tensor(Y[:, :, :], Y[:, :, :], yb, ALU.add).then_inc(mrg_ok, 1)
            turn_evict("mrg", lambda i: qT[:, i, :])
            product_evict("w_o", Y, D)
            dve.wait_ge(late_in, 16 * 5)
            evicted("w_o")
            residual("p1", Y, bc[:, 0, :], x)
            for g in range(4):
                mod_columns(g)
            norm("nf1", x, Y)
            mod_evict(4)
            turn_evict("hf1", lambda i: HT[:, i, :], lambda i: cols["norm_ffn_pre"][:, i:i + 1])
            mod_scales(0)
            step(V.tensor_scalar(nsink[:, :], nsink[:, :], -1.0, None, ALU.mult))
            ffn("1")
            down_evict("1", Y)
            evicted("down1")
            residual("pf1", Y, bc[:, 1, :], x)
            mod_evict(5)
            for g in (4, 5):
                mod_columns(g)
            mod_scales(1)
            norm("n_c0", cx, Z)
            norm("n_x0", x, Y)
            turn_evict("h_c0", lambda i: HC[:, i, :], lambda i: hscale[:, 0, 0, 1, i:i + 1], lambda i: modcol[:, 0, i, 1:2])
            product_evict("qkv_c0", pc, N_EVEN)
            turn_evict("h_x0", lambda i: HT[:, i, :], lambda i: hscale[:, 0, 0, 0, i:i + 1], lambda i: modcol[:, 0, i, 0:1])
            product_evict("qkv_x0", px, N_EVEN)
            evicted("qkv_x0")
            dve.wait_ge(band_in, 16 * 3)
            for i, src in enumerate((pc, px)):
                for t in range(NT):
                    qk = src[:, t, 0:640].rearrange("p (h d) -> p h d", h=10)
                    qk2 = zf[:, 0:640].rearrange("p (h d) -> p h d", h=10)
                    step.wait()
                    step(V.tensor_tensor(qk2, qk, qk, ALU.mult))
                    step.wait()
                    step(V.tensor_reduce(rq[:, 4, 0:10], qk2, AX.X, ALU.add))
                    step(rsqrt(rq[:, 5, 0:10], rq[:, 4, 0:10], 10, HD))
                    step.wait()
                    step(V.tensor_tensor(qk, qk, rq[:, 5, 0:10].unsqueeze(2).to_broadcast((P, 10, HD)), ALU.mult))
                    step.wait()
                    step(V.tensor_tensor(qk, qk, qkgain[:, :].rearrange("p (h d) -> p h d", h=10), ALU.mult))
                    if i == 1:
                        rope_axial(src[:, t, 0:640], t, 10)
            step.wait()
            double_keys(0, px[:, :, 512:640], 2)
            double_keys(2, pc[:, :, 512:640], 2)
            step.wait()
            V.engine_nop().then_inc(qk_ready, 1)
            turn_evict("q_xc", lambda i: qT[:, i, :])
            turn_evict("k_xc", lambda i: kT[:, i % 2, (i // 2) * S:(i // 2 + 1) * S])
            attention("ax", None, 0)
            attention("ac", None, NB)
            for i, dst in enumerate((HT, HC)):
                dve.wait_ge(pool_mm, i + 1)
                V.tensor_copy(qT[:, 4 * i + 2:4 * i + 4, :], T[:, 1, :].rearrange("p (g n) -> p g n", g=2)).then_inc(pool_d, 1)
                dve.wait_ge(pool_y, i + 1)
                for g in range(2, 4):
                    V.tensor_scalar(dst[:, 4 + g, :], T[:, 3, (g - 2) * S:(g - 1) * S], cols["we_pool_scale_2"][:, g:g + 1], None,
                                    ALU.mult).then_inc(pool_ok, 1)
            turn_evict("o_x", lambda i: HT[:, i, :])
            turn_evict("o_c", lambda i: HC[:, i, :])
            product_evict("out_x0", Y, D)
            dve.wait_ge(turn_act, turn["o_c"][1] + 2)
            dve.wait_ge(turn_dve, turn["o_c"][2] + 2)
            product_evict("out_c0", Z, D)
            for k, (f, r) in enumerate(((0, 0), (0, 1), (1, 0), (1, 1))):
                broadcast_row(k, gtg[:, 0, f, r, :], (bc if f == 0 else bc2)[:, r, :])
            evicted("out_x0")
            residual("p_x0", Y, bc[:, 0, :], x)
            evicted("out_c0")
            residual("p_c0", Z, bc[:, 1, :], cx)
            norm("nf_x0", x, Y)
            norm("nf_c0", cx, Z)
            turn_evict("hf_x0", lambda i: HT[:, i, :], lambda i: hscale[:, 0, 1, 0, i:i + 1], lambda i: modcol[:, 0, 24 + i, 0:1])
            turn_evict("hf_c0", lambda i: HC[:, i, :], lambda i: hscale[:, 0, 1, 1, i:i + 1], lambda i: modcol[:, 0, 24 + i, 1:2])
            ffn("_x0")
            down_evict("_x0", Y)
            evicted("down_x0")
            residual("pf_x0", Y, bc2[:, 0, :], x)
            ffn("_c0")
            down_evict("_c0", Z)
            evicted("down_c0")
            residual("pf_c0", Z, bc2[:, 1, :], cx)
            norm("n_c1", cx, Z)
            norm("n_x1", x, Y)
            turn_evict("h_c1", lambda i: HC[:, i, :], lambda i: hscale[:, 1, 0, 1, i:i + 1], lambda i: modcol[:, 1, i, 1:2])
            product_evict("kv_c1", pc[:, :, D:N_ODD], NB)
            turn_evict("h_x1", lambda i: HT[:, i, :], lambda i: hscale[:, 1, 0, 0, i:i + 1], lambda i: modcol[:, 1, i, 0:1])
            product_evict("qkv_x1", px, N_ODD)
            for k, f in ((4, 0), (5, 1)):
                broadcast_row(k, gtg[:, 1, f, 0, :], bc[:, f, :])
            evicted("qkv_x1")
            for t in range(NT):
                rope_axial(px[:, t, 0:D + S], t, 20)
            step.wait()
            double_keys(0, px[:, :, D:D + S], 4)
            double_keys(2, pc[:, :, D:D + S], 4)
            step.wait()
            V.engine_nop().then_inc(qk_ready, 1)
            turn_evict("q_1", lambda i: qT[:, i, :])
            turn_evict("k_1", lambda i: kT[:, i % 4, (i // 4) * S:(i // 4 + 1) * S])
            attention("a1x", band, 0)
            turn_evict("o_1", lambda i: HT[:, i, :])
            product_evict("out_x1", Y, D)
            evicted("out_x1")
            residual("p_x1", Y, bc[:, 0, :], x)
            norm("nf_x1", x, Y)
            turn_evict("hf_x1", lambda i: HT[:, i, :], lambda i: hscale[:, 1, 1, 0, i:i + 1], lambda i: modcol[:, 1, 24 + i, 0:1])
            ffn("_x1")
            down_evict("_x1", Y)
            evicted("down_x1")
            residual("pf_x1", Y, bc[:, 1, :], x)


def shape_constants():
    f32 = np.float32
    pos = np.arange(S)
    tile = lambda a: np.ascontiguousarray(a.reshape(NT, P, *a.shape[1:]).swapaxes(0, 1)).astype(f32)
    causal = np.where(pos[None, :] <= pos[:, None], 0.0, MASKED)
    band = np.concatenate([np.where(np.abs(pos[None, :] - pos[:, None]) <= 128, 0.0, MASKED), np.zeros((S, S))], axis=1)

    def angles(at, freq):
        a = at.astype(f32)[:, None] * freq[None, :]
        return np.cos(a).astype(f32), np.sin(a).astype(f32)

    f1 = (f32(500000.0) ** (-np.arange(8, dtype=f32) / f32(8))).astype(f32)
    f2 = (f32(10000.0) ** (-np.arange(16, dtype=f32) / f32(16))).astype(f32)
    rope1 = np.stack(angles(pos, f1), axis=1)
    (cr, sr), (cc, sc) = angles(pos // 64, f2), angles(pos % 64, f2)
    rope2 = np.stack([np.concatenate([cr, cc], 1), np.concatenate([sr, sc], 1)], axis=1)
    pool = np.zeros((4, S, S))
    for g, w in enumerate((2, 4, 8, 16)):
        lo, hi = np.clip(pos - w // 2, 0, S), np.clip(pos + w - w // 2, 0, S)
        inside = (pos[:, None] >= lo[None, :]) & (pos[:, None] < hi[None, :])
        pool[g] = inside / (hi - lo)[None, :] - np.eye(S)
    pool = pool.reshape(4, NT, P, S).transpose(2, 0, 1, 3)
    return {"ident": np.eye(P, dtype=f32), "causal": tile(causal), "band": tile(band), "rope1": tile(rope1),
            "rope2": tile(rope2), "pool": np.ascontiguousarray(pool).astype(f32)}


def kernel(**inputs):
    import numpy as _np
    import concourse.bacc as _bacc
    from concourse import mybir as _mybir
    from concourse.bass_utils import run_bass_kernel_spmd as _run

    nc = _bacc.Bacc("TRN2", target_bir_lowering=False, num_devices=1)
    arrays, t_in, consts = {}, {}, {}
    for name, a in inputs.items():
        a = _np.ascontiguousarray(a)
        arrays[f"in_{name}"] = a
        t_in[name] = nc.dram_tensor(f"in_{name}", a.shape, _mybir.dt.from_np(a.dtype), kind="ExternalInput").ap()
    for name, a in shape_constants().items():
        arrays[f"const_{name}"] = a
        consts[name] = nc.dram_tensor(f"const_{name}", a.shape, _mybir.dt.from_np(a.dtype), kind="ExternalInput").ap()
    out = nc.dram_tensor("out", (1, S, D), F32, kind="ExternalOutput").ap()
    build(nc, t_in, consts, out)
    r = _run(nc, [arrays], core_ids=[0])
    return r.results[0]["out"]
```

```python
import math
from contextlib import ExitStack

import numpy as np
import concourse.bass as bass
from concourse import mybir

F32 = mybir.dt.float32
I32 = mybir.dt.int32
ACT = mybir.ActivationFunctionType
ALU = mybir.AluOpType
AX = mybir.AxisListType

P = 128
S = 256
NT = S // P
D = 1024
KC = D // P
HD = 64
F = 2816
FC = F // P
NB = 512
FB = F // S
N_IN = 6216
C_XR, C_GR, C_Q, C_K, C_V, C_IQ, C_IK, C_IW, C_GA, C_GB = 0, 1024, 2048, 3072, 3328, 3584, 4096, 4160, 4168, 5192
N_EVEN, N_ODD = 1280, 1536
TOPK = 64
EPS = 1e-6
SCALE = HD ** -0.5
IDX_SCALE = (8 ** -0.5) * (64 ** -0.5)
MASKED = -1e30
TAKEN = -3e38
RING = 4

SV1 = [("norm_mix_pre", 8), ("conv_w", 32), ("conv_b", 8), ("rg_b_a", 8), ("rg_b_x", 8), ("rg_lambda", 8),
       ("norm_ffn_pre", 8), ("g_pre_mix_2", 16), ("g_pre_ffn_2", 16), ("c_2", 8), ("c_ctx_2", 8)]
SV2 = [("we_pool_scale_2", 4), ("g_post_mix_2", 16), ("g_post_ffn_2", 16)]
SV3 = [("b_mod_2", 96)]

MODG = 8
PRODUCTS = [("in_a", 16, 8), ("in_tail", 2, 1), ("in_b1", 4, 2), ("in_b2", 4, 2), ("mod0", MODG, 0), ("y_a", 4, 2),
            ("y_b", 4, 2), ("w_o", 4, 2), ("mod1", MODG, 1), ("up1", 22, FB), ("down1", 11, 2),
            ("qkv_c0", 6, 3), ("qkv_x0", 6, 3), ("mod2", MODG, 0), ("mod3", MODG, 0), ("out_x0", 4, 2), ("out_c0", 4, 2),
            ("up_x0", 22, FB), ("down_x0", 11, 2), ("up_c0", 22, FB), ("down_c0", 11, 2),
            ("qkv_x1", 6, 3), ("kv_c1", 2, 1), ("mod4", MODG, 0), ("out_x1", 4, 2), ("mod5", MODG, 1), ("up_x1", 22, FB),
            ("down_x1", 11, 2)]
MOD_IN = {"a1": 0, "ax": 2, "ac": 3, "a1x": 4}
TURNS = [("h1", 8), ("xr", 8), ("q", 8), ("kiq", 8), ("ik", 1), ("gr", 8), ("o1", 8), ("mrg", 8), ("hf1", 8),
         ("h_c0", 8), ("h_x0", 8), ("q_xc", 8), ("k_xc", 4), ("o_x", 4), ("o_c", 4), ("hf_x0", 8), ("hf_c0", 8),
         ("h_x1", 8), ("h_c1", 8), ("q_1", 8), ("k_1", 8), ("o_1", 8), ("hf_x1", 8)]
SUMS = ["n1", "p1", "nf1", "n_c0", "pf1", "n_x0", "p_x0", "nf_x0", "p_c0", "nf_c0", "pf_x0", "n_x1", "pf_c0",
        "n_c1", "p_x1", "nf_x1", "pf_x1"]
ATTN = [("a1", 16, (128, 256)), ("ax", 8, (512, 512)), ("ac", 8, (256, 256)), ("a1x", 16, (512, 512))]
FFNS = ["1", "_x0", "_c0", "_x1"]


def starts(items, *cols):
    at, sums = {}, [0] * len(cols)
    for it in items:
        at[it[0]] = tuple(sums)
        sums = [s + it[c] for s, c in zip(sums, cols)]
    return at


def n_act(n):
    return sum(i // 2 % 2 == 0 for i in range(n))


def build(nc, t_in, consts, out):
    prod = starts(PRODUCTS, 1, 2)
    n_slots = dict((n, s) for n, s, _ in PRODUCTS)
    turn_n = dict(TURNS)
    turn, ca, cd, ct = {}, 0, 0, 0
    for name, n in TURNS:
        turn[name] = (ct, ca, cd)
        ct, ca, cd = ct + n, ca + n_act(n), cd + n - n_act(n)
    sums = dict((n, i) for i, n in enumerate(SUMS))
    att0 = starts([(n, 2 * h) for n, h, _ in ATTN], 1)
    ffn_i = dict((n, i) for i, n in enumerate(FFNS))

    with ExitStack() as ctx:
        def sb(name, *shape):
            return ctx.enter_context(nc.sbuf_tensor(name, [P, *shape], F32))

        def sem(name):
            return ctx.enter_context(nc.semaphore(name))

        G = ctx.enter_context(nc.psum_tensor("G", [P, 4, NB], F32))
        T = ctx.enter_context(nc.psum_tensor("T", [P, 4, NB], F32))

        ring = sb("ring", RING, 2048)
        x = sb("x", NT, D)
        cx = sb("cx", NT, D)
        area = sb("area", NT * N_IN)
        Y = sb("Y", NT, D)
        Z = sb("Z", NT, D)
        HT = sb("HT", KC, S)
        rnn = sb("rnn", 8 * 259 + 4 * 2048)
        qT = sb("qT", 8, S)
        kT = sb("kT", 4, 2 * S)
        ikT = sb("ikT", S)
        bd = sb("bd", 2048 + 512)
        bias1 = sb("bias1", NT, S)
        causal = sb("causal", P)
        modrow = sb("modrow", NB)
        ident = sb("ident", P)
        ones = sb("ones", P)
        svc = sb("svc", 260)
        scT = sb("scT", KC, 32)
        modcol = sb("modcol", 2, 48, 2)
        hscale = sb("hscale", 2, 2, 2, 8)
        gtg = sb("gtg", 2, 2, 2, 8)
        bc = sb("bc", 2, D)
        rope1 = sb("rope1", NT, 2, 8)
        rope2 = sb("rope2", NT, 2, 32)
        lnrow = sb("lnrow", 2, HD)
        nsink = sb("nsink", 16)
        ssb = sb("ssb", 2, 2)
        rs = sb("rs", 2, 2)
        rq = sb("rq", 6, 40)
        c8 = sb("c8", 10, 8)
        amin = sb("amin", 4)
        asum = sb("asum", 4)
        arec = sb("arec", 4)
        top8 = sb("top8", NT, 8)
        iws = sb("iws", NT, 8)

        proj = area[:, :].rearrange("p (t n) -> p t n", t=NT)
        hidT = area[:, 0:FC * S].rearrange("p (c s) -> p c s", c=FC)
        o_ = FC * S
        hid = area[:, o_:o_ + 1024].rearrange("p (b t n) -> p b t n", b=2, t=NT)
        gate = area[:, o_ + 1024:o_ + 2048].rearrange("p (b t n) -> p b t n", b=2, t=NT)
        o_ += 2048
        diag = area[:, o_:o_ + 1024].rearrange("p (c n) -> p c n", c=KC)
        bc2 = area[:, o_ + 1024:o_ + 3072].rearrange("p (r n) -> p r n", r=2)
        band = area[:, o_ + 3072:o_ + 4096].rearrange("p (t n) -> p t n", t=NT)
        qkgain = area[:, o_ + 4096:o_ + 4096 + 10 * HD]
        px = area[:, 0:NT * N_ODD].rearrange("p (t n) -> p t n", t=NT)
        pc = area[:, NT * N_ODD:2 * NT * N_ODD].rearrange("p (t n) -> p t n", t=NT)
        xpad = rnn[:, 0:8 * 259].rearrange("p (c n) -> p c n", c=8)
        o_ = 8 * 259
        xc, R1, R2, R3 = [rnn[:, o_ + 2048 * i:o_ + 2048 * (i + 1)].rearrange("p (c n) -> p c n", c=8) for i in range(4)]
        work = rnn[:, 0:4 * 516].rearrange("p (b n) -> p b n", b=4)
        pT = R1.rearrange("p (b c) n -> p b (c n)", b=4)
        HC = R2
        bda = bd[:, 0:1024].rearrange("p (c n) -> p c n", c=8)
        bdx = bd[:, 1024:2048].rearrange("p (c n) -> p c n", c=8)
        poolm = bd[:, 0:2048].rearrange("p (g k n) -> p g k n", g=4, k=NT)
        wpool = bd[:, 2048:2560].rearrange("p (g n) -> p g n", g=4)
        kd = Y[:, :, :].rearrange("p t n -> p (t n)").rearrange("p (k g n) -> p k g n", k=4, g=4)
        ikd = Z[:, 0, 0:2 * P].rearrange("p (t n) -> p t n", t=NT)
        svr = Z[:, 0, 0:3 * P].rearrange("p (i n) -> p i n", i=3)
        zf = Z[:, :, :].rearrange("p t n -> p (t n)")
        yf = Y[:, :, :].rearrange("p t n -> p (t n)")

        at, cols = 0, {}
        for base, rows in ((0, SV1), (P, SV2), (164, SV3)):
            at = base
            for name, n in rows:
                cols[name] = svc[:, at:at + n]
                at += n

        w_landed = [sem(f"w_landed{i}") for i in range(RING)]
        slot_read = sem("slot_read")
        ev_act = sem("ev_act")
        ev_dve = sem("ev_dve")
        turned = sem("turned")
        turn_act = sem("turn_act")
        turn_dve = sem("turn_dve")
        x_in = sem("x_in")
        sv_in = sem("sv_in")
        small_in = sem("small_in")
        late_in = sem("late_in")
        bd_in = sem("bd_in")
        bd_zero = sem("bd_zero")
        band_in = sem("band_in")
        pool_in = sem("pool_in")
        sv_turned = sem("sv_turned")
        sv_done = sem("sv_done")
        ss_done = sem("ss_done")
        rs_done = sem("rs_done")
        xn_act = sem("xn_act")
        xn_dve = sem("xn_dve")
        x_new = sem("x_new")
        c_silu = sem("c_silu")
        mod_row = sem("mod_row")
        dstep = sem("dstep")
        astep = sem("astep")
        rnn_xc = sem("rnn_xc")
        rnn_gate = sem("rnn_gate")
        rnn_sig = sem("rnn_sig")
        rnn_ta = sem("rnn_ta")
        rnn_sq = sem("rnn_sq")
        rnn_root = sem("rnn_root")
        softp_z = sem("softp_z")
        softp_e = sem("softp_e")
        softp = sem("softp")
        gelu_in = sem("gelu_in")
        gelu_t = sem("gelu_t")
        gelu_ok = sem("gelu_ok")
        qk_ready = sem("qk_ready")
        idx_mm = sem("idx_mm")
        idx_relu = sem("idx_relu")
        idx_acc = sem("idx_acc")
        sg_ready = sem("sg_ready")
        mrg_ok = sem("mrg_ok")
        mod_turned = sem("mod_turned")
        mod_ok = sem("mod_ok")
        diag_ok = sem("diag_ok")
        bc_mm = sem("bc_mm")
        bc_ok = sem("bc_ok")
        pool_mm = sem("pool_mm")
        pool_d = sem("pool_d")
        pool_y = sem("pool_y")
        pool_ok = sem("pool_ok")
        hid_turned = sem("hid_turned")
        hidT_ok = sem("hidT_ok")
        a_mm = sem("a_mm")
        a_min = sem("a_min")
        a_exp = sem("a_exp")
        a_turned = sem("a_turned")
        a_pT = sem("a_pT")
        a_pv = sem("a_pv")
        a_o = sem("a_o")
        stored = sem("stored")

        pstep = sem("pstep")
        rnn_y = sem("rnn_y")
        rnn_scan = sem("rnn_scan")
        hs_ok = sem("hs_ok")
        SV_DMAS = 1 + len(SV1) + len(SV2) + len(SV3)
        kT_flat = kT[:, :, :].rearrange("p g n -> p (g n)")
        kT_junk = kT[:, :, :].rearrange("p g n -> p (g n)").rearrange("p (t n) -> p t n", t=NT)

        def logit_bank(u):
            return (T[:, 0, :], T[:, 1, :], G[:, 2, :])[u % 3]

        bias1_row = bias1[:, :, :].rearrange("p t n -> p (t n)")

        def mod_rows(g):
            return bias1_row if g == 3 else modrow[:, :]

        def mod_rows_done(name):
            return list(MOD_IN).index(name) + 1

        def chunks(w):
            return w.rearrange("(k p) n -> p k n", p=P)

        w = {n: t_in[n] for n in t_in}
        w_in = chunks(w["w_in"][0])
        ring4 = ring[:, :, :].rearrange("p r (k n) -> p r k n", k=4)
        ring2 = ring[:, :, :].rearrange("p r (k n) -> p r k n", k=2)
        up_w = {"1": (chunks(w["w_ffn_gate"][0]), chunks(w["w_ffn_up"][0])),
                "0": tuple(chunks(w["w_ffn_in_2"][0][:, i * F:(i + 1) * F]) for i in range(2)),
                "_x1": tuple(chunks(w["w_ffn_in_2"][1][:, i * F:(i + 1) * F]) for i in range(2))}
        down_w = {"1": chunks(w["w_ffn_down"][0]), "0": chunks(w["w_ffn_out_2"][0]), "_x1": chunks(w["w_ffn_out_2"][1])}
        for n in ("_x0", "_c0"):
            up_w[n], down_w[n] = up_w["0"], down_w["0"]
        plain = {"in_b1": w["w_in"][0][:, C_GA:C_GB], "in_b2": w["w_in"][0][:, C_GB:], "y_a": w["w_rnn_out"][0],
                 "y_b": w["w_att_out"][0], "w_o": w["w_o"][0], "qkv_c0": w["we_in_2"][0],
                 "qkv_x0": w["we_in_2"][0], "out_x0": w["we_out_2"][0], "out_c0": w["we_out_2"][0],
                 "qkv_x1": w["wo_in_2"][0], "kv_c1": w["wo_in_2"][0][:, D:N_ODD], "out_x1": w["wo_out_2"][0]}

        class Steps:

            def __init__(self, eng, s):
                self.eng, self.s, self.n = eng, s, 0

            def __call__(self, ins):
                self.n += 1
                ins.then_inc(self.s, 1)

            def wait(self, back=0):
                self.eng.wait_ge(self.s, self.n - back)

        block = ctx.enter_context(nc.Block())

        @block.sync
        def _(sp):
            def slot_free(s):
                if not isinstance(s, int) or s >= RING:
                    sp.wait_ge(slot_read, s - RING + 1)

            def fill(slot, s, parts):
                slot_free(s)
                for dst, src in parts:
                    sp.dma_start(dst, src).then_inc(w_landed[slot], 16)

            def half_block(slot, s, wv, half, col, n):
                fill(slot, s, [(ring4[:, slot, 2 * i:2 * i + 2, 0:n],
                                wv[:, 4 * half + 2 * i:4 * half + 2 * i + 2, col]) for i in range(2)])

            def product(name):
                s0 = prod[name][0]
                wv = chunks(plain[name])
                total = wv.shape[2]
                for b in range(-(-total // NB)):
                    n = min(NB, total - b * NB)
                    for h in range(2):
                        s = s0 + 2 * b + h
                        half_block(s % RING, s, wv, h, slice(b * NB, b * NB + n), n)

            def in_loop(name, col0, nblocks):
                s0 = prod[name][0]
                for j in range(RING):
                    c = col0 + (j // 2) * NB
                    half_block((s0 + j) % RING, s0 + j, w_in, j % 2, slice(c, c + NB), NB)
                with sp.Fori(1, nblocks // 2) as it:
                    for j in range(RING):
                        half_block((s0 + j) % RING, s0 + j + it * RING, w_in, j % 2,
                                   bass.ds(it * (2 * NB) + (col0 + (j // 2) * NB), NB), NB)

            def mod_group(g):
                s0 = prod[f"mod{g}"][0]
                wv = chunks(w["w_mod_2"][g // 3])
                for j in range(MODG):
                    c = ((g % 3) * 4 + j // 2) * NB
                    half_block((s0 + j) % RING, s0 + j, wv, j % 2, slice(c, c + NB), NB)

            def ffn(name):
                s0 = prod["up" + name][0]
                wg, wu = up_w[name]

                def half_pair(j, s, col):
                    slot, h = (s0 + j) % RING, j % 2
                    fill(slot, s, [(ring4[:, slot, :, S * i:S * i + S], wv[:, 4 * h:4 * h + 4, col])
                                   for i, wv in enumerate((wg, wu))])

                for j in range(2):
                    half_pair(j, s0 + j, slice(0, S))
                with sp.Fori(0, FB // 2) as it:
                    for j in range(2, 6):
                        half_pair(j, s0 + j + it * 4, bass.ds(it * (2 * S) + (j // 2) * S, S))
                s0 = prod["down" + name][0]
                wd = down_w[name]
                for j in range(FC // 2):
                    slot = (s0 + j) % RING
                    fill(slot, s0 + j, [(ring2[:, slot, i:i + 1, :], wd[:, 2 * j + i:2 * j + i + 1, :]) for i in range(2)])

            sp.dma_start(x[:, :, :], w["x"][0].rearrange("(t p) n -> p t n", p=P)).then_inc(x_in, 16)
            in_loop("in_a", 0, 8)
            s0 = prod["in_tail"][0]
            for h in range(2):
                half_block((s0 + h) % RING, s0 + h, w_in, h, slice(C_IK, C_GA), C_GA - C_IK)
            product("in_b1")
            product("in_b2")
            mod_group(0)
            product("y_a")
            product("y_b")
            product("w_o")
            mod_group(1)
            ffn("1")
            product("qkv_c0")
            product("qkv_x0")
            mod_group(2)
            mod_group(3)
            product("out_x0")
            product("out_c0")
            ffn("_x0")
            ffn("_c0")
            product("qkv_x1")
            product("kv_c1")
            mod_group(4)
            product("out_x1")
            mod_group(5)
            ffn("_x1")
            sp.wait_ge(x_new, len([n for n in SUMS if n[0] == "p"]))
            sp.dma_start(out[0].rearrange("(t p) n -> p t n", p=P), x[:, :, :]).then_inc(stored, 16)
            sp.wait_ge(stored, 16)

        @block.tensor
        def _(pe):
            def free(waits):
                for s, v in waits:
                    pe.wait_ge(s, v)

            def pair_free(e):
                if not isinstance(e, int) or e >= 2:
                    pe.wait_ge(ev_act, e - 1)
                    pe.wait_ge(ev_dve, e - 1)

            def landed(s, fills=None):
                pe.wait_ge(w_landed[s % RING], 32 * (s // RING + 1) if fills is None else fills)

            def rows(s, half, e, lhsT, n, fills=None):
                landed(s, fills)
                for t in range(NT):
                    for k in range(4):
                        mm = nc.tensor.matmul(G[:, 2 * (e % 2) + t, 0:n], lhsT[:, 4 * half + k, t * P:(t + 1) * P],
                                              ring4[:, s % RING, k, 0:n], start=(half == 0 and k == 0),
                                              stop=(half == 1 and k == 3))
                mm.then_inc(slot_read, 1)

            def product(name, lhsT, total):
                s0, e0 = prod[name]
                for b in range(-(-total // NB)):
                    pair_free(e0 + b)
                    for h in range(2):
                        rows(s0 + 2 * b + h, h, e0 + b, lhsT, min(NB, total - b * NB))

            def in_loop(name, first, nblocks):
                s0, e0 = prod[name]
                with pe.Fori(first, nblocks // 2) as it:
                    for j in range(4):
                        if j % 2 == 0:
                            pe.wait_ge(ev_act, it * 2 + (e0 + j // 2 - 1))
                            pe.wait_ge(ev_dve, it * 2 + (e0 + j // 2 - 1))
                        rows(s0 + j, j % 2, e0 + j // 2, HT, NB, it * 32 + 32 * ((s0 + j) // RING + 1))

            def mod_slot(g, j, bank):
                s, q = prod[f"mod{g}"][0] + j, j // 2
                if g == 0 and j == 0:
                    pe.wait_ge(c_silu, 1)
                landed(s)
                for k in range(4):
                    mm = nc.tensor.matmul(G[32 * q:32 * q + 32, bank, :], scT[:, 4 * (j % 2) + k, :], ring4[:, s % RING, k, :],
                                          start=(j % 2 == 0 and k == 0), stop=(j % 2 == 1 and k == 3),
                                          tile_position=(0, 32 * q))
                mm.then_inc(slot_read, 1)

            def mod_group(g):
                e0 = prod[f"mod{g}"][1]
                pair_free(e0)
                for j in range(MODG):
                    mod_slot(g, j, 2 * (e0 % 2))

            def mod_turn(g, waits):
                e0 = prod[f"mod{g}"][1]
                free(waits)
                inside = [n for n in MOD_IN if MOD_IN[n] == g]
                if inside:
                    pe.wait_ge(mod_row, mod_rows_done(inside[0]))
                else:
                    pe.wait_ge(ev_act, e0 + 1)
                    pe.wait_ge(ev_dve, e0 + 1)
                for c in range(4):
                    tr = nc.tensor.transpose(T[:, g % 4, c * P:(c + 1) * P],
                                             mod_rows(g)[:, c * P:(c + 1) * P], ident[:, :])
                tr.then_inc(mod_turned, 1)
                return [(mod_ok, g + 1)]

            def turn_stage(name, src, waits, ready=()):
                n, (c0, _, _) = turn_n[name], turn[name]
                free(waits)
                for s, v in ready:
                    pe.wait_ge(s, v)
                for i in range(n):
                    for t in range(NT):
                        tr = nc.tensor.transpose(T[:, i // 2, (i % 2) * S + t * P:(i % 2) * S + (t + 1) * P],
                                                 src(i, t), ident[:, :])
                    tr.then_inc(turned, 1)
                return [(turn_act, turn[name][1] + n_act(n)), (turn_dve, turn[name][2] + n - n_act(n))]

            def norm_turn(name, sname, src, waits):
                k = sums[sname] + 1
                n_x = 1 + [n for n in SUMS[:k] if n[0] == "n"].index(sname)
                return turn_stage(name, lambda i, t: src[:, t, i * P:(i + 1) * P], waits,
                                  [(xn_act, n_x), (xn_dve, n_x)])

            def ffn(name, lhsT, waits):
                f = ffn_i[name]
                s0, e0 = prod["up" + name]
                h0 = FB * f
                free(waits)

                def up_block(j, it=None):
                    more = 0 if it is None else it
                    pe.wait_ge(ev_act, more * 2 + (e0 + j - 1))
                    pe.wait_ge(ev_dve, more * 2 + (e0 + j - 1))
                    for h in range(2):
                        s = s0 + 2 * j + h
                        rows(s, h, e0 + j, lhsT, NB, more * 32 + 32 * (s // RING + 1))

                def turn_hidden(j, it=None):
                    more = 0 if it is None else it
                    pe.wait_ge(ev_dve, more * 2 + (e0 + j + 1))
                    if not (f == 0 and j < 2 and it is None):
                        pe.wait_ge(hidT_ok, more * 2 + (h0 + j - 1))
                    for c in range(2):
                        for t in range(NT):
                            tr = nc.tensor.transpose(T[:, j % 2, c * S + t * P:c * S + (t + 1) * P],
                                                     hid[:, j % 2, t, c * P:(c + 1) * P], ident[:, :])
                    tr.then_inc(hid_turned, 1)

                up_block(0)
                up_block(1)
                turn_hidden(0)
                up_block(2)
                turn_hidden(1)
                with pe.Fori(1, FB // 2) as it:
                    up_block(1, it)
                    turn_hidden(0, it)
                    up_block(2, it)
                    turn_hidden(1, it)
                turn_hidden(FB - 1)
                s0, e0 = prod["down" + name]
                pair_free(e0)
                pair_free(e0 + 1)
                pe.wait_ge(hidT_ok, h0 + FB)
                for j in range(FC // 2):
                    s = s0 + j
                    landed(s)
                    for k in range(2):
                        for t in range(NT):
                            for h in range(2):
                                mm = nc.tensor.matmul(G[:, 2 * ((e0 + h) % 2) + t, :],
                                                      hidT[:, 2 * j + k, t * P:(t + 1) * P],
                                                      ring2[:, s % RING, k, h * NB:(h + 1) * NB],
                                                      start=(j == 0 and k == 0), stop=(j == FC // 2 - 1 and k == 1))
                    mm.then_inc(slot_read, 1)
                return []

            def attention(name, qs, ks, vs, waits, e_next):
                heads, nks = [a[1:] for a in ATTN if a[0] == name][0]
                u0 = att0[name][0]
                n = 2 * heads
                free(waits)
                pe.wait_ge(ev_act, e_next)
                pe.wait_ge(ev_dve, e_next)

                def unit(u):
                    return 2 * (u // 4) + u % 2, (u // 2) % 2

                def scores(u):
                    h, t = unit(u)
                    if u >= 3:
                        pe.wait_ge(a_min, u0 + u - 2)
                    nc.tensor.matmul(logit_bank(u)[:, 0:nks[t]], qs(h, t), ks(h, t), start=True, stop=True).then_inc(a_mm, 1)

                def turn_probs(u):
                    h, t = unit(u)
                    pe.wait_ge(a_exp, u0 + u + 1)
                    if u >= 2:
                        pe.wait_ge(a_pT, u0 + u - 1)
                    for k in range(nks[t] // P):
                        tr = nc.tensor.transpose(T[:, 2 + u % 2, k * P:(k + 1) * P], work[:, u % 4, k * P:(k + 1) * P], ident[:, :])
                    tr.then_inc(a_turned, 1)

                def values(u):
                    h, t = unit(u)
                    pe.wait_ge(a_pT, u0 + u + 1)
                    if u >= 2:
                        pe.wait_ge(a_o, u0 + u - 1)
                    for k in range(nks[t] // P):
                        mm = nc.tensor.matmul(G[:, u % 2, 0:HD], pT[:, u % 4, k * P:(k + 1) * P],
                                              vs(h, k), start=(k == 0), stop=(k == nks[t] // P - 1))
                    mm.then_inc(a_pv, 1)

                g, every = MOD_IN[name], n // MODG
                rows_in = mod_rows_done(name)
                if rows_in > 1:
                    pe.wait_ge(mod_row, rows_in - 1)
                for u in range(n + 3):
                    if u < n:
                        scores(u)
                    if 2 <= u < n + 2:
                        turn_probs(u - 2)
                    if u >= 3:
                        values(u - 3)
                    if u < n and u % every == every - 1:
                        mod_slot(g, u // every, 3)
                return [(a_o, u0 + n), (mod_row, rows_in)]

            def broadcast_row(k, waits):
                free(waits)
                pe.wait_ge(diag_ok, k + 1)
                for c in range(KC):
                    mm = nc.tensor.matmul(T[:, c // 4, (c % 4) * P:(c % 4 + 1) * P], ones[:, :], diag[:, c, :],
                                          start=True, stop=True)
                mm.then_inc(bc_mm, 1)
                return [(bc_ok, k + 1)]

            def half64(h):
                return slice((h % 2) * HD, (h % 2 + 1) * HD)

            pe.wait_ge(sv_in, 16 * SV_DMAS)
            for i, n in enumerate((P, 36, 96)):
                tr = nc.tensor.transpose(T[:, 0, i * P:i * P + n], svr[0:n, i, :], ident[0:n, 0:n])
            tr.then_inc(sv_turned, 1)
            busy = norm_turn("h1", "n1", Y, [(sv_done, 1)])
            free(busy)
            s0, e0 = prod["in_a"]
            for j in range(4):
                if j % 2 == 0:
                    pair_free(e0 + j // 2)
                rows(s0 + j, j % 2, e0 + j // 2, HT, NB)
            busy = turn_stage("xr", lambda i, t: proj[:, t, C_XR + i * P:C_XR + (i + 1) * P], busy,
                              [(ev_act, e0 + 2), (ev_dve, e0 + 2)])
            in_loop("in_a", 1, 8)
            free(busy)
            for c in range(8):
                pe.wait_ge(rnn_xc, c + 1)
                if c == 0:
                    pe.wait_ge(bd_in, 64)
                if c >= 4:
                    pe.wait_ge(rnn_sig, c - 3)
                for i, m in enumerate((bda, bdx)):
                    mm = nc.tensor.matmul(T[:, c % 4, i * S:(i + 1) * S], m[:, c, :], xc[:, c, :], start=True, stop=True)
                mm.then_inc(rnn_gate, 1)
            busy = [(rnn_sig, 8)]
            s0, e0 = prod["in_tail"]
            pair_free(e0)
            for h in range(2):
                rows(s0 + h, h, e0, HT, C_GA - C_IK)
            product("in_b1", HT, D)
            busy = turn_stage("q", lambda i, t: proj[:, t, C_Q + i * P:C_Q + (i + 1) * P], busy, [(qk_ready, 1)])
            busy = turn_stage("kiq", lambda i, t: kd[:, t, i, :] if i < 4 else
                              proj[:, t, C_IQ + (i - 4) * P:C_IQ + (i - 3) * P], busy)
            busy = turn_stage("ik", lambda i, t: ikd[:, t, :], busy)
            free(busy)
            for u in range(16):
                h, t = u // 2, u % 2
                if u >= 4:
                    pe.wait_ge(idx_relu, u - 3)
                nc.tensor.matmul(T[:, u % 4, 0:P * (t + 1)], kT[half64(h), h // 2, S + t * P:S + (t + 1) * P],
                                 ikT[half64(h), 0:P * (t + 1)], start=True, stop=True).then_inc(idx_mm, 1)
            product("in_b2", HT, D)
            busy = [(idx_relu, 16)]
            busy = turn_stage("gr", lambda i, t: proj[:, t, C_GR + i * P:C_GR + (i + 1) * P], busy, [(gelu_ok, 1)])
            busy = attention("a1", lambda h, t: qT[half64(h), h // 2, t * P:(t + 1) * P],
                             lambda h, t: kT[half64(h), h // 4, 0:P * (t + 1)],
                             lambda h, k: proj[:, k, C_V + (h // 4) * HD:C_V + (h // 4 + 1) * HD], busy, prod["y_a"][1])
            free(busy)
            pe.wait_ge(rnn_y, 1)
            product("y_a", R3, D)
            busy = turn_stage("o1", lambda i, t: Z[:, t, i * P:(i + 1) * P], busy)
            free(busy)
            product("y_b", HT, D)
            busy = mod_turn(0, busy)
            busy = turn_stage("mrg", lambda i, t: Y[:, t, i * P:(i + 1) * P], busy, [(mrg_ok, 1)])
            pe.wait_ge(turn_act, turn["mrg"][1] + 4)
            pe.wait_ge(turn_dve, turn["mrg"][2] + 4)
            product("w_o", qT, D)
            mod_group(1)
            busy = norm_turn("hf1", "nf1", Y, busy)
            busy = mod_turn(1, busy)
            busy = norm_turn("h_c0", "n_c0", Z, busy)
            ffn("1", HT, busy)
            product("qkv_c0", HC, N_EVEN)
            busy = broadcast_row(0, [])
            busy = norm_turn("h_x0", "n_x0", Y, busy)
            busy = broadcast_row(1, busy)
            product("qkv_x0", HT, N_EVEN)
            busy = turn_stage("q_xc", lambda i, t: (px, pc)[i // 4][:, t, (i % 4) * P:(i % 4 + 1) * P], busy, [(qk_ready, 2)])
            busy = turn_stage("k_xc", lambda i, t: kd[:, 2 * (i // 2) + t, i % 2, :], busy)
            free(busy)
            vcol = 640
            pe.wait_ge(turn_act, turn["k_xc"][1] + 2)
            pe.wait_ge(turn_dve, turn["k_xc"][2] + 2)
            busy = attention("ax", lambda h, t: qT[half64(h), h // 2, t * P:(t + 1) * P],
                             lambda h, t: kT[half64(h), h // 4, :],
                             lambda h, k: (px, pc)[k // 2][:, k % 2, vcol + (h // 4) * HD:vcol + (h // 4 + 1) * HD], busy,
                             prod["out_x0"][1])
            busy = attention("ac", lambda h, t: qT[half64(h), 4 + h // 2, t * P:(t + 1) * P],
                             lambda h, t: kT[half64(h), h // 4, S:2 * S],
                             lambda h, k: pc[:, k, vcol + (h // 4) * HD:vcol + (h // 4 + 1) * HD], busy, prod["out_x0"][1])
            free(busy)
            pe.wait_ge(pool_in, 16 * 2)
            for i, src in enumerate((px, pc)):
                if i == 1:
                    pe.wait_ge(pool_d, 2)
                for g in range(4):
                    for k in range(NT):
                        mm = nc.tensor.matmul(T[:, g // 2, (g % 2) * S:(g % 2 + 1) * S], src[:, k, 768 + g * P:768 + (g + 1) * P],
                                              poolm[:, g, k, :], start=(k == 0), stop=(k == 1))
                mm.then_inc(pool_mm, 1)
                pe.wait_ge(pool_d, 2 * i + 2)
                if i == 1:
                    pe.wait_ge(pool_ok, 4)
                for g in range(4):
                    mm = nc.tensor.matmul(T[:, 2 + g // 2, (g % 2) * S:(g % 2 + 1) * S], wpool[:, g, :], qT[:, 4 * i + g, :],
                                          start=True, stop=True)
                mm.then_inc(pool_y, 1)
            busy = [(pool_ok, 8)]
            busy = turn_stage("o_x", lambda i, t: Z[:, t, i * P:(i + 1) * P], busy)
            busy = turn_stage("o_c", lambda i, t: Z[:, t, NB + i * P:NB + (i + 1) * P], busy)
            mod_turn(2, busy)
            busy = mod_turn(3, [])
            product("out_x0", HT, D)
            busy = broadcast_row(2, busy)
            product("out_c0", HC, D)
            busy = broadcast_row(3, busy)
            busy = norm_turn("hf_x0", "nf_x0", Y, busy)
            ffn("_x0", HT, busy)
            busy = norm_turn("hf_c0", "nf_c0", Z, [])
            ffn("_c0", HC, busy)
            busy = norm_turn("h_x1", "n_x1", Y, [])
            free(busy)
            product("qkv_x1", HT, N_ODD)
            busy = norm_turn("h_c1", "n_c1", Z, busy)
            free(busy)
            product("kv_c1", HC, NB)
            busy = turn_stage("q_1", lambda i, t: px[:, t, i * P:(i + 1) * P], busy, [(qk_ready, 3)])
            busy = turn_stage("k_1", lambda i, t: kd[:, 2 * (i // 4) + t, i % 4, :], busy)
            vcol1 = 1280
            busy = attention("a1x", lambda h, t: qT[half64(h), h // 2, t * P:(t + 1) * P],
                             lambda h, t: kT[half64(h), h // 4, :],
                             lambda h, k: (px, pc)[k // 2][:, k % 2, vcol1 + (h // 4) * HD:vcol1 + (h // 4 + 1) * HD], busy,
                             prod["out_x1"][1])
            busy = turn_stage("o_1", lambda i, t: Z[:, t, i * P:(i + 1) * P], busy)
            busy = mod_turn(4, busy)
            product("out_x1", HT, D)
            busy = broadcast_row(4, busy)
            mod_group(5)
            busy = mod_turn(5, busy)
            busy = norm_turn("hf_x1", "nf_x1", Y, busy)
            busy = broadcast_row(5, busy)
            ffn("_x1", HT, busy)

        @block.scalar
        def _(act):
            step = Steps(act, astep)

            act.dma_start(ident[:, :], consts["ident"]).then_inc(sv_in, 16)
            for i, group in enumerate((SV1, SV2, SV3)):
                r = 0
                for name, n in group:
                    src = w[name]
                    if len(src.shape) == 1:
                        src = src.rearrange("(r n) -> r n", n=P)
                    elif len(src.shape) == 2:
                        src = src.rearrange("a (r n) -> (a r) n", n=P)
                    else:
                        src = src.rearrange("a b (r n) -> (a b r) n", n=P)
                    act.dma_start(svr[r:r + n, i, :], src).then_inc(sv_in, 16)
                    r += n

            def square_sums(name, src, junk):
                k = sums[name]
                if k:
                    act.wait_ge(ss_done, k)
                for t in range(NT):
                    sq = nc.scalar.activation(junk[:, t, :], src[:, t, :], ACT.Square, accum_out=ssb[:, k % 2, t:t + 1])
                sq.then_inc(ss_done, 1)

            def norm_apply(name, src, dst):
                k = sums[name]
                act.wait_ge(rs_done, k + 1)
                nc.scalar.activation(dst[:, 1, :], src[:, 1, :], ACT.Copy, scale=rs[:, k % 2, 1:2]).then_inc(xn_act, 1)

            def turn_evict(name, dst, scale=None, bias=None):
                c0, n = turn[name][0], turn_n[name]
                for i in [i for i in range(n) if i // 2 % 2 == 0]:
                    act.wait_ge(turned, c0 + min(i // 2 * 2 + 2, n))
                    src = T[:, i // 2, (i % 2) * S:(i % 2 + 1) * S]
                    if scale is None:
                        ins = nc.scalar.activation(dst(i), src, ACT.Copy)
                    elif bias is None:
                        ins = nc.scalar.activation(dst(i), src, ACT.Copy, scale=scale(i))
                    else:
                        ins = nc.scalar.activation(dst(i), src, ACT.Identity, scale=scale(i), bias=bias(i))
                    ins.then_inc(turn_act, 1)

            def product_evict(name, dst, total):
                s0, e0 = prod[name]
                for b in range(-(-total // NB)):
                    n = min(NB, total - b * NB)
                    act.wait_ge(slot_read, s0 + 2 * b + 2)
                    nc.scalar.activation(dst[:, 0, b * NB:b * NB + n], G[:, 2 * ((e0 + b) % 2), 0:n], ACT.Copy).then_inc(ev_act, 1)

            def in_loop(name, col0, first, nblocks):
                s0, e0 = prod[name]
                with act.Fori(first, nblocks // 2) as it:
                    for j in range(2):
                        act.wait_ge(slot_read, it * 4 + (s0 + 2 * j + 2))
                        nc.scalar.activation(proj[:, 0, bass.ds(it * 1024 + (col0 + j * NB), NB)], G[:, 2 * ((e0 + j) % 2), :],
                                             ACT.Copy).then_inc(ev_act, 1)

            def mod_evict(g):
                s0, e0 = prod[f"mod{g}"]
                act.wait_ge(slot_read, s0 + MODG)
                if g >= 1:
                    act.wait_ge(mod_turned, g)
                nc.scalar.activation(modrow[:, :], G[:, 2 * (e0 % 2), :], ACT.Copy).then_inc(ev_act, 1)

            def ffn(name):
                f = ffn_i[name]
                s0, e0 = prod["up" + name]
                h0 = FB * f

                def silu(j, it=None):
                    more = 0 if it is None else it
                    act.wait_ge(slot_read, more * 4 + (s0 + 2 * j + 2))
                    act.wait_ge(ev_dve, more * 2 + (e0 + j - 1))
                    p = (e0 + j) % 2
                    nc.scalar.activation(gate[:, j % 2, :, :], G[:, 2 * p:2 * p + 2, 0:S], ACT.Silu).then_inc(ev_act, 1)

                def hid_out(j, it=None):
                    act.wait_ge(hid_turned, (0 if it is None else it * 2) + (h0 + j + 1))
                    dst = hidT[:, 2 * j:2 * j + 2, :] if it is None else hidT[:, bass.ds(it * 4 + 2 * j, 2), :]
                    nc.scalar.activation(dst, T[:, j % 2, :].rearrange("p (c n) -> p c n", c=2), ACT.Copy).then_inc(hidT_ok, 1)

                silu(0)
                with act.Fori(0, FB // 2) as it:
                    silu(1, it)
                    hid_out(0, it)
                    silu(2, it)
                    hid_out(1, it)
                hid_out(FB - 1)
                s0, e0 = prod["down" + name]
                act.wait_ge(slot_read, s0 + FC // 2)

            def down_evict(name, dst):
                e0 = prod["down" + name][1]
                for h in range(2):
                    nc.scalar.activation(dst[:, 0, h * NB:(h + 1) * NB], G[:, 2 * ((e0 + h) % 2), :], ACT.Copy).then_inc(ev_act, 1)

            def attention(name, last_o=False):
                heads, nks = [a[1:] for a in ATTN if a[0] == name][0]
                u0 = att0[name][0]
                n = 2 * heads
                extra = 1 if name == "a1x" else 0

                g = MOD_IN[name]
                for u in range(n + 2):
                    if u == n:
                        act.wait_ge(slot_read, prod[f"mod{g}"][0] + MODG)
                        if g in (2, 4):
                            act.wait_ge(mod_turned, g)
                        nc.scalar.activation(mod_rows(g), G[:, 3, :], ACT.Copy).then_inc(mod_row, 1)
                    if u < n:
                        t = (u // 2) % 2
                        act.wait_ge(a_min, u0 + u + 1)
                        if u >= 4:
                            act.wait_ge(a_o, u0 + u - 3)
                        wv = work[:, u % 4, 0:nks[t] + extra]
                        nc.scalar.activation(wv, wv, ACT.Exp, scale=-1.0, bias=amin[:, u % 4:u % 4 + 1],
                                             accum_out=asum[:, u % 4:u % 4 + 1]).then_inc(a_exp, 1)
                    if u >= 2:
                        v = u - 2
                        t = (v // 2) % 2
                        act.wait_ge(a_turned, u0 + v + 1)
                        if v >= 4:
                            act.wait_ge(a_pv, u0 + v - 3)
                        nc.scalar.activation(pT[:, v % 4, 0:nks[t]], T[:, 2 + v % 2, 0:nks[t]], ACT.Copy).then_inc(a_pT, 1)

            act.wait_ge(x_in, 16)
            square_sums("n1", x, Y)
            norm_apply("n1", x, Y)
            act.wait_ge(sv_done, 1)
            turn_evict("h1", lambda i: HT[:, i, :], lambda i: cols["norm_mix_pre"][:, i:i + 1])
            act.dma_start(rope1[:, :, :, :], consts["rope1"]).then_inc(small_in, 16)
            act.dma_start(causal[:, :], consts["causal"]).then_inc(small_in, 16)
            act.dma_start(lnrow[:, 0, :], w["idx_k_ln_g"][0:1, :].to_broadcast((P, HD))).then_inc(small_in, 16)
            act.dma_start(lnrow[:, 1, :], w["idx_k_ln_b"][0:1, :].to_broadcast((P, HD))).then_inc(small_in, 16)
            act.wait_ge(bd_zero, 1)
            for m, name in ((bda, "rg_w_a"), (bdx, "rg_w_x")):
                v = w[name][0].rearrange("(c b) i j -> b i c j", b=2)
                for b in range(2):
                    act.dma_start(m[b * HD:(b + 1) * HD, :, b * HD:(b + 1) * HD], v[b]).then_inc(bd_in, 16)
            act.dma_start(bc[:, 0, :], w["norm_mix_post"][0:1, :].to_broadcast((P, D))).then_inc(late_in, 16)
            act.dma_start(bc[:, 1, :], w["norm_ffn_post"][0:1, :].to_broadcast((P, D))).then_inc(late_in, 16)
            act.dma_start(cx[:, :, :], w["ctx_2"][0].rearrange("(t p) n -> p t n", p=P)).then_inc(late_in, 16)
            act.dma_start(rope2[:, :, :, :], consts["rope2"]).then_inc(late_in, 16)
            act.dma_start(nsink[:, :], w["wo_sink_2"][0:1, :].to_broadcast((P, 16))).then_inc(late_in, 16)
            for i, name in enumerate(("c_2", "c_ctx_2")):
                ins = nc.scalar.activation(scT[:, :, i], cols[name], ACT.Silu)
            ins.then_inc(c_silu, 1)
            act.wait_ge(softp_z, 1)
            nc.scalar.activation(c8[:, 1, :], c8[:, 0, :], ACT.Exp, scale=-1.0).then_inc(softp_e, 1)
            s0, e0 = prod["in_a"]
            for b in range(2):
                act.wait_ge(slot_read, s0 + 2 * b + 2)
                nc.scalar.activation(proj[:, 0, b * NB:(b + 1) * NB], G[:, 2 * ((e0 + b) % 2), :], ACT.Copy).then_inc(ev_act, 1)
            turn_evict("xr", lambda i: xpad[:, i, 3:259])
            in_loop("in_a", 0, 1, 8)
            act.wait_ge(gelu_in, 1)
            nc.scalar.activation(Y[:, :, :], Y[:, :, :], ACT.Tanh, scale=math.sqrt(2.0 / math.pi)).then_inc(gelu_t, 1)
            act.wait_ge(softp, 1)
            for c in range(8):
                act.wait_ge(rnn_gate, c + 1)
                nc.scalar.activation(R1[:, c, :], T[:, c % 4, 0:S], ACT.Sigmoid, bias=cols["rg_b_a"][:, c:c + 1])
                nc.scalar.activation(R2[:, c, :], T[:, c % 4, S:2 * S], ACT.Sigmoid, bias=cols["rg_b_x"][:, c:c + 1]).then_inc(rnn_sig, 1)
            act.wait_ge(rnn_sig, 8)
            for c in range(8):
                step(nc.scalar.activation(R3[:, c, :], R1[:, c, :], ACT.Tanh, scale=c8[:, 8, c:c + 1]))
            step.wait()
            for c in range(8):
                ins = nc.scalar.activation(R1[:, c, :], R1[:, c, :], ACT.Exp, scale=c8[:, 9, c:c + 1])
            ins.then_inc(rnn_ta, 1)
            s0, e0 = prod["in_tail"]
            act.wait_ge(slot_read, s0 + 2)
            nc.scalar.activation(proj[:, 0, C_IK:C_GA], G[:, 2 * (e0 % 2), 0:C_GA - C_IK], ACT.Copy).then_inc(ev_act, 1)
            act.wait_ge(rnn_sq, 1)
            nc.scalar.activation(R3[:, :, :], R3[:, :, :], ACT.Sqrt).then_inc(rnn_root, 1)
            product_evict("in_b1", proj[:, :, C_GA:C_GB], D)
            turn_evict("q", lambda i: qT[:, i, :])
            turn_evict("kiq", lambda i: kT[:, i, 0:S] if i < 4 else kT[:, i - 4, S:2 * S])
            turn_evict("ik", lambda i: ikT[:, :])
            for u in range(16):
                nk = P * (u % 2 + 1)
                act.wait_ge(idx_mm, u + 1)
                if u >= 4:
                    act.wait_ge(idx_acc, u - 3)
                nc.scalar.activation(yf[:, (u % 4) * S:(u % 4) * S + nk], T[:, u % 4, 0:nk], ACT.Relu).then_inc(idx_relu, 1)
            product_evict("in_b2", proj[:, :, C_GB:N_IN], D)
            e0 = prod["in_b2"][1]
            act.wait_ge(ev_act, e0 + 2)
            act.wait_ge(ev_dve, e0 + 2)
            nc.scalar.activation(proj[:, :, C_GA:N_IN], proj[:, :, C_GA:N_IN], ACT.Sigmoid).then_inc(sg_ready, 1)
            act.wait_ge(rnn_scan, 1)
            turn_evict("gr", lambda i: R2[:, i, :])
            attention("a1")
            product_evict("y_a", Y, D)
            turn_evict("o1", lambda i: HT[:, i, :])
            product_evict("y_b", proj[:, :, C_Q:C_Q + D], D)
            turn_evict("mrg", lambda i: qT[:, i, :])
            product_evict("w_o", Y, D)
            act.wait_ge(ev_act, prod["w_o"][1] + 2)
            act.wait_ge(ev_dve, prod["w_o"][1] + 2)
            square_sums("p1", Y, Z)
            act.wait_ge(x_new, 1)
            square_sums("nf1", x, Y)
            norm_apply("nf1", x, Y)
            mod_evict(1)
            act.wait_ge(late_in, 16 * 5)
            square_sums("n_c0", cx, Z)
            norm_apply("n_c0", cx, Z)
            turn_evict("hf1", lambda i: HT[:, i, :], lambda i: cols["norm_ffn_pre"][:, i:i + 1])
            act.wait_ge(hs_ok, 1)
            turn_evict("h_c0", lambda i: HC[:, i, :], lambda i: hscale[:, 0, 0, 1, i:i + 1], lambda i: modcol[:, 0, i, 1:2])
            ffn("1")
            down_evict("1", Y)
            act.wait_ge(ev_act, prod["down1"][1] + 2)
            act.wait_ge(ev_dve, prod["down1"][1] + 2)
            square_sums("pf1", Y, Z)
            act.dma_start(band[:, :, :], consts["band"]).then_inc(band_in, 16)
            for name, c0, c1 in (("we_q_gain_2", 0, 512), ("we_k_gain_2", 512, 640)):
                n = (c1 - c0) // HD
                act.dma_start(qkgain[:, c0:c1].rearrange("p (h n) -> p h n", h=n),
                              w[name][0:1, :].unsqueeze(1).to_broadcast((P, n, HD))).then_inc(band_in, 16)
            act.dma_start(poolm[:, :, :, :], consts["pool"]).then_inc(pool_in, 16)
            act.dma_start(wpool[:, :, :], w["we_pool_2"][0].rearrange("g c d -> c g d")).then_inc(pool_in, 16)
            act.wait_ge(x_new, 2)
            square_sums("n_x0", x, Y)
            norm_apply("n_x0", x, Y)
            product_evict("qkv_c0", pc, N_EVEN)
            turn_evict("h_x0", lambda i: HT[:, i, :], lambda i: hscale[:, 0, 0, 0, i:i + 1], lambda i: modcol[:, 0, i, 0:1])
            product_evict("qkv_x0", px, N_EVEN)
            turn_evict("q_xc", lambda i: qT[:, i, :])
            turn_evict("k_xc", lambda i: kT[:, i % 2, (i // 2) * S:(i // 2 + 1) * S])
            attention("ax")
            attention("ac")
            for i, dst in enumerate((HT, HC)):
                act.wait_ge(pool_mm, i + 1)
                nc.scalar.activation(qT[:, 4 * i:4 * i + 2, :], T[:, 0, :].rearrange("p (g n) -> p g n", g=2), ACT.Copy).then_inc(pool_d, 1)
                act.wait_ge(pool_y, i + 1)
                for g in range(2):
                    nc.scalar.activation(dst[:, 4 + g, :], T[:, 2, g * S:(g + 1) * S], ACT.Copy,
                                         scale=cols["we_pool_scale_2"][:, g:g + 1]).then_inc(pool_ok, 1)
            turn_evict("o_x", lambda i: HT[:, i, :])
            turn_evict("o_c", lambda i: HC[:, i, :])
            product_evict("out_x0", Y, D)
            act.wait_ge(ev_act, prod["out_x0"][1] + 2)
            act.wait_ge(ev_dve, prod["out_x0"][1] + 2)
            square_sums("p_x0", Y, kT_junk)
            act.wait_ge(x_new, 3)
            square_sums("nf_x0", x, Y)
            norm_apply("nf_x0", x, Y)
            act.wait_ge(turn_act, turn["o_c"][1] + 2)
            act.wait_ge(turn_dve, turn["o_c"][2] + 2)
            product_evict("out_c0", Z, D)
            act.wait_ge(hs_ok, 2)
            turn_evict("hf_x0", lambda i: HT[:, i, :], lambda i: hscale[:, 0, 1, 0, i:i + 1], lambda i: modcol[:, 0, 24 + i, 0:1])
            act.wait_ge(ev_act, prod["out_c0"][1] + 2)
            act.wait_ge(ev_dve, prod["out_c0"][1] + 2)
            square_sums("p_c0", Z, kT_junk)
            act.wait_ge(x_new, 4)
            square_sums("nf_c0", cx, Z)
            norm_apply("nf_c0", cx, Z)
            ffn("_x0")
            down_evict("_x0", Y)
            turn_evict("hf_c0", lambda i: HC[:, i, :], lambda i: hscale[:, 0, 1, 1, i:i + 1], lambda i: modcol[:, 0, 24 + i, 1:2])
            act.wait_ge(ev_act, prod["down_x0"][1] + 2)
            act.wait_ge(ev_dve, prod["down_x0"][1] + 2)
            square_sums("pf_x0", Y, kT_junk)
            act.wait_ge(x_new, 5)
            square_sums("n_x1", x, Y)
            norm_apply("n_x1", x, Y)
            ffn("_c0")
            down_evict("_c0", Z)
            act.wait_ge(hs_ok, 3)
            turn_evict("h_x1", lambda i: HT[:, i, :], lambda i: hscale[:, 1, 0, 0, i:i + 1], lambda i: modcol[:, 1, i, 0:1])
            act.wait_ge(ev_act, prod["down_c0"][1] + 2)
            act.wait_ge(ev_dve, prod["down_c0"][1] + 2)
            square_sums("pf_c0", Z, kT_junk)
            act.wait_ge(x_new, 6)
            square_sums("n_c1", cx, Z)
            norm_apply("n_c1", cx, Z)
            product_evict("qkv_x1", px, N_ODD)
            turn_evict("h_c1", lambda i: HC[:, i, :], lambda i: hscale[:, 1, 0, 1, i:i + 1], lambda i: modcol[:, 1, i, 1:2])
            product_evict("kv_c1", pc[:, :, D:N_ODD], NB)
            turn_evict("q_1", lambda i: qT[:, i, :])
            turn_evict("k_1", lambda i: kT[:, i % 4, (i // 4) * S:(i // 4 + 1) * S])
            attention("a1x")
            turn_evict("o_1", lambda i: HT[:, i, :])
            product_evict("out_x1", Y, D)
            act.wait_ge(ev_act, prod["out_x1"][1] + 2)
            act.wait_ge(ev_dve, prod["out_x1"][1] + 2)
            square_sums("p_x1", Y, kT_junk)
            act.wait_ge(x_new, 7)
            square_sums("nf_x1", x, Y)
            norm_apply("nf_x1", x, Y)
            mod_evict(5)
            act.wait_ge(hs_ok, 4)
            turn_evict("hf_x1", lambda i: HT[:, i, :], lambda i: hscale[:, 1, 1, 0, i:i + 1], lambda i: modcol[:, 1, 24 + i, 0:1])
            ffn("_x1")
            down_evict("_x1", Y)
            act.wait_ge(ev_act, prod["down_x1"][1] + 2)
            act.wait_ge(ev_dve, prod["down_x1"][1] + 2)
            square_sums("pf_x1", Y, kT_junk)

        @block.gpsimd
        def _(pool):
            step = Steps(pool, pstep)
            nc.gpsimd.memset(scT[:, :, :], 0.0)
            nc.gpsimd.memset(ones[:, :], 1.0)
            nc.gpsimd.memset(bd[:, :], 0.0)
            nc.gpsimd.memset(xpad[:, :, 0:3], 0.0).then_inc(bd_zero, 1)
            gr = proj[:, :, C_GR:C_GR + D]
            e0 = prod["in_a"][1]
            pool.wait_ge(ev_act, e0 + 4)
            pool.wait_ge(ev_dve, e0 + 4)
            step(nc.gpsimd.tensor_tensor(Y[:, :, :], gr, gr, ALU.mult))
            step.wait()
            step(nc.gpsimd.tensor_scalar(Y[:, :, :], Y[:, :, :], 0.044715, 1.0, ALU.mult, ALU.add))
            step.wait()
            nc.gpsimd.tensor_tensor(Y[:, :, :], Y[:, :, :], gr, ALU.mult).then_inc(gelu_in, 1)
            pool.wait_ge(gelu_t, 1)
            step(nc.gpsimd.tensor_scalar(Y[:, :, :], Y[:, :, :], 1.0, 1.0, ALU.mult, ALU.add))
            step.wait()
            nc.gpsimd.tensor_tensor(gr, Y[:, :, :], gr, ALU.mult).then_inc(gelu_ok, 1)

        @block.vector
        def _(dve):
            step = Steps(dve, dstep)
            V = nc.vector

            def rsqrt(dst, ss, n, count):
                v, i, y, a = [rq[:, j, 0:n] for j in range(4)]
                step.wait()
                step(V.tensor_scalar(v, ss, 1.0 / count, EPS, ALU.mult, ALU.add))
                step.wait()
                step(V.tensor_scalar(i.bitcast(I32), v.bitcast(I32), 1, None, ALU.logical_shift_right))
                step.wait()
                step(V.tensor_scalar(y.bitcast(I32), i.bitcast(I32), -1.0, float(0x5F3759DF), ALU.mult, ALU.add))
                for r in range(3):
                    step.wait()
                    step(V.tensor_tensor(a, y, y, ALU.mult))
                    step.wait()
                    step(V.scalar_tensor_tensor(a, a, -0.5, v, ALU.mult, ALU.mult))
                    step.wait()
                    if r < 2:
                        step(V.scalar_tensor_tensor(y, a, 1.5, y, ALU.add, ALU.mult))
                return V.scalar_tensor_tensor(dst, a, 1.5, y, ALU.add, ALU.mult)

            def inverse_rms(name):
                k = sums[name]
                dve.wait_ge(ss_done, k + 1)
                rsqrt(rs[:, k % 2, :], ssb[:, k % 2, :], 2, D).then_inc(rs_done, 1)
                dve.wait_ge(rs_done, k + 1)

            def norm(name, src, dst):
                inverse_rms(name)
                V.tensor_scalar(dst[:, 0, :], src[:, 0, :], rs[:, sums[name] % 2, 0:1], None, ALU.mult).then_inc(xn_dve, 1)

            def residual(name, y, row, dst):
                inverse_rms(name)
                for t in range(NT):
                    step(V.scalar_tensor_tensor(y[:, t, :], y[:, t, :], rs[:, sums[name] % 2, t:t + 1], row, ALU.mult, ALU.mult))
                step.wait()
                V.tensor_tensor(dst[:, :, :], dst[:, :, :], y[:, :, :], ALU.add).then_inc(x_new, 1)
                n_x = [n for n in SUMS if n[0] == "p"].index(name) + 1
                dve.wait_ge(x_new, n_x)

            def turn_evict(name, dst, scale=None, bias=None):
                c0, n = turn[name][0], turn_n[name]
                for i in [i for i in range(n) if i // 2 % 2]:
                    dve.wait_ge(turned, c0 + i // 2 * 2 + 2)
                    src = T[:, i // 2, (i % 2) * S:(i % 2 + 1) * S]
                    if scale is None:
                        ins = V.tensor_copy(dst(i), src)
                    elif bias is None:
                        ins = V.tensor_scalar(dst(i), src, scale(i), None, ALU.mult)
                    else:
                        ins = V.tensor_scalar(dst(i), src, scale(i), bias(i), ALU.mult, ALU.add)
                    ins.then_inc(turn_dve, 1)

            def block_evict(name, b, dst, total):
                s0, e0 = prod[name]
                n = min(NB, total - b * NB)
                dve.wait_ge(slot_read, s0 + 2 * b + 2)
                V.tensor_copy(dst[:, 1, b * NB:b * NB + n], G[:, 2 * ((e0 + b) % 2) + 1, 0:n]).then_inc(ev_dve, 1)

            def blocks_in(name, n):
                dve.wait_ge(ev_act, prod[name][1] + n)
                dve.wait_ge(ev_dve, prod[name][1] + n)

            def product_evict(name, dst, total):
                for b in range(-(-total // NB)):
                    block_evict(name, b, dst, total)

            def evicted(name):
                e = prod[name][1] + [p for p in PRODUCTS if p[0] == name][0][2]
                dve.wait_ge(ev_act, e)
                dve.wait_ge(ev_dve, e)

            def in_loop(name, col0, first, nblocks):
                s0, e0 = prod[name]
                with dve.Fori(first, nblocks // 2) as it:
                    for j in range(2):
                        dve.wait_ge(slot_read, it * 4 + (s0 + 2 * j + 2))
                        V.tensor_copy(proj[:, 1, bass.ds(it * 1024 + (col0 + j * NB), NB)],
                                      G[:, 2 * ((e0 + j) % 2) + 1, :]).then_inc(ev_dve, 1)

            def mod_evict(g):
                V.engine_nop().then_inc(ev_dve, 1)

            def mod_columns(g):
                lyr, i0 = g // 3, (g % 3) * 16
                dve.wait_ge(mod_turned, g + 1)
                V.tensor_tensor(modcol[:, lyr, i0:i0 + 16, :].rearrange("p (j c) r -> p c j r", j=4),
                                T[:, g % 4, :].rearrange("p (c j r) -> p c j r", c=4, j=4)[:, :, :, 0:2],
                                cols["b_mod_2"][:, lyr * 48 + i0:lyr * 48 + i0 + 16].rearrange("p (j c) -> p c j", j=4)
                                .unsqueeze(3).to_broadcast((P, 4, 4, 2)), ALU.add).then_inc(mod_ok, 1)

            def mod_scale(lyr, f):
                pre = ("g_pre_mix_2", "g_pre_ffn_2")[f]
                dve.wait_ge(mod_ok, 3 * lyr + 1 + 2 * f)
                for r in range(2):
                    ins = V.scalar_tensor_tensor(hscale[:, lyr, f, r, :], modcol[:, lyr, 24 * f + 8:24 * f + 16, r], 1.0,
                                                 cols[pre][:, 8 * lyr:8 * lyr + 8], ALU.add, ALU.mult)
                ins.then_inc(hs_ok, 1)
                dve.wait_ge(hs_ok, 2 * lyr + f + 1)

            def mod_gate(lyr, f):
                post = ("g_post_mix_2", "g_post_ffn_2")[f]
                dve.wait_ge(mod_ok, 3 * lyr + 2 + f)
                for r in range(2):
                    step(V.tensor_tensor(gtg[:, lyr, f, r, :], modcol[:, lyr, 24 * f + 16:24 * f + 24, r],
                                         cols[post][:, 8 * lyr:8 * lyr + 8], ALU.mult))
                step.wait()

            def diagonal(k, col):
                if k >= 1:
                    dve.wait_ge(bc_mm, k)
                for c in range(KC):
                    ins = V.tensor_scalar(diag[:, c, :], ident[:, :], col[:, c:c + 1], None, ALU.mult)
                ins.then_inc(diag_ok, 1)

            def spread_row(k, dst):
                dve.wait_ge(bc_mm, k + 1)
                V.tensor_copy(dst.rearrange("p (b n) -> p b n", b=2), T[:, 0:2, :]).then_inc(bc_ok, 1)
                dve.wait_ge(bc_ok, k + 1)

            def rope(first, second, cos, sin, shape, scratch):
                n = int(np.prod(shape))

                def tmp(i):
                    v = scratch[:, 2048 - (i + 1) * n:2048 - i * n]
                    if len(shape) == 2:
                        return v.rearrange("p (h d) -> p h d", h=shape[0])
                    return v.rearrange("p (h a d) -> p h a d", h=shape[0], a=shape[1])
                step.wait()
                step(V.tensor_tensor(tmp(0), first, cos, ALU.mult))
                step(V.tensor_tensor(tmp(1), second, sin, ALU.mult))
                step(V.tensor_tensor(tmp(2), first, sin, ALU.mult))
                step.wait()
                step(V.tensor_tensor(first, tmp(0), tmp(1), ALU.subtract))
                step.wait()
                step(V.tensor_tensor(tmp(0), second, cos, ALU.mult))
                step.wait()
                step(V.tensor_tensor(second, tmp(0), tmp(2), ALU.add))

            def rope_small(src, t, heads):
                v = src.rearrange("p (h d) -> p h d", h=heads)
                c, s = [rope1[:, t, i, :].unsqueeze(1).to_broadcast((P, heads, 8)) for i in range(2)]
                rope(v[:, :, 0:8], v[:, :, 8:16], c, s, (heads, 8), zf)

            def rope_axial(src, t, heads):
                v = src.rearrange("p (h a b d) -> p h a b d", h=heads, a=2, b=2)
                c, s = [rope2[:, t, i, :].rearrange("p (a d) -> p a d", a=2).unsqueeze(1).to_broadcast((P, heads, 2, 16))
                        for i in range(2)]
                rope(v[:, :, :, 0, :], v[:, :, :, 1, :], c, s, (heads, 2, 16), kT_flat)

            def double_keys(k0, src, groups):
                for b in range(2):
                    ins = V.tensor_copy(kd[:, k0:k0 + NT, 0:groups, b * HD:(b + 1) * HD],
                                        src.rearrange("p t (g d) -> p t g d", g=groups))
                    step(ins)

            def ffn(name):
                f = ffn_i[name]
                e0 = prod["up" + name][1]
                h0 = FB * f

                def hidden(j, it=None):
                    more = 0 if it is None else it
                    dve.wait_ge(ev_act, more * 2 + (e0 + j + 1))
                    if it is not None or j >= 2:
                        dve.wait_ge(hid_turned, more * 2 + (h0 + j - 1))
                    p = (e0 + j) % 2
                    V.tensor_tensor(hid[:, j % 2, :, :], gate[:, j % 2, :, :], G[:, 2 * p:2 * p + 2, S:NB],
                                    ALU.mult).then_inc(ev_dve, 1)

                hidden(0)
                hidden(1)
                hidden(2)
                with dve.Fori(1, FB // 2) as it:
                    hidden(1, it)
                    hidden(2, it)

            def down_evict(name, dst):
                s0, e0 = prod["down" + name]
                dve.wait_ge(slot_read, s0 + FC // 2)
                for h in range(2):
                    V.tensor_copy(dst[:, 1, h * NB:(h + 1) * NB], G[:, 2 * ((e0 + h) % 2) + 1, :]).then_inc(ev_dve, 1)

            def attention(name, mask, o_col):
                heads, nks = [a[1:] for a in ATTN if a[0] == name][0]
                u0 = att0[name][0]
                n = 2 * heads
                step.wait()
                for u in range(n + 4):
                    if u < n:
                        h, t = 2 * (u // 4) + u % 2, (u // 2) % 2
                        b = u % 4
                        dve.wait_ge(a_mm, u0 + u + 1)
                        if u >= 4:
                            dve.wait_ge(a_turned, u0 + u - 3)
                        src, dst, low = logit_bank(u)[:, 0:nks[t]], work[:, b, 0:nks[t]], amin[:, b:b + 1]
                        if mask is None:
                            ins = V.tensor_scalar(dst, src, -SCALE, None, ALU.mult, ALU.min, accum_out=low)
                        else:
                            ins = V.tensor_tensor_reduce(dst, src, mask[:, t, 0:nks[t]], -SCALE, 3e38, ALU.add, ALU.min, low)
                        if name == "a1x":
                            step(ins)
                            step(V.tensor_copy(work[:, b, nks[t]:nks[t] + 1], nsink[:, h:h + 1]))
                            step.wait(1)
                            ins = V.tensor_tensor(low, low, nsink[:, h:h + 1], ALU.min)
                        ins.then_inc(a_min, 1)
                    if u >= 4:
                        v = u - 4
                        h, t = 2 * (v // 4) + v % 2, (v // 2) % 2
                        dve.wait_ge(a_pv, u0 + v + 1)
                        step(V.reciprocal(arec[:, v % 4:v % 4 + 1], asum[:, v % 4:v % 4 + 1]))
                        step.wait()
                        V.tensor_scalar(Z[:, t, o_col + h * HD:o_col + (h + 1) * HD], G[:, v % 2, 0:HD],
                                        arec[:, v % 4:v % 4 + 1], None, ALU.mult).then_inc(a_o, 1)

            def qk_norm(src, t, c0, heads):
                qk = src[:, t, c0:c0 + heads * HD].rearrange("p (h d) -> p h d", h=heads)
                qk2 = zf[:, 0:heads * HD].rearrange("p (h d) -> p h d", h=heads)
                step.wait()
                step(V.tensor_tensor(qk2, qk, qk, ALU.mult))
                step.wait()
                step(V.tensor_reduce(rq[:, 4, 0:heads], qk2, AX.X, ALU.add))
                step(rsqrt(rq[:, 5, 0:heads], rq[:, 4, 0:heads], heads, HD))
                step.wait()
                step(V.tensor_tensor(qk, qk, rq[:, 5, 0:heads].unsqueeze(2).to_broadcast((P, heads, HD)), ALU.mult))
                step.wait()
                step(V.tensor_tensor(qk, qk, qkgain[:, c0:c0 + heads * HD].rearrange("p (h d) -> p h d", h=heads), ALU.mult))

            dve.wait_ge(sv_turned, 1)
            step(V.tensor_copy(svc[:, 0:164], T[:, 0, 0:164]))
            V.tensor_copy(svc[:, 164:260], T[:, 0, 2 * P:2 * P + 96]).then_inc(sv_done, 1)
            norm("n1", x, Y)
            dve.wait_ge(sv_done, 1)
            turn_evict("h1", lambda i: HT[:, i, :], lambda i: cols["norm_mix_pre"][:, i:i + 1])
            lam = cols["rg_lambda"]
            V.scalar_tensor_tensor(c8[:, 0, :], lam, -1.0, lam, ALU.mult, ALU.max).then_inc(softp_z, 1)
            dve.wait_ge(softp_e, 1)
            step(V.tensor_scalar(c8[:, 2, :], c8[:, 1, :], 2.0, None, ALU.add))
            step.wait()
            step(V.reciprocal(c8[:, 3, :], c8[:, 2, :]))
            step.wait()
            step(V.tensor_tensor(c8[:, 4, :], c8[:, 1, :], c8[:, 3, :], ALU.mult))
            step.wait()
            step(V.tensor_tensor(c8[:, 5, :], c8[:, 4, :], c8[:, 4, :], ALU.mult))
            step.wait()
            step(V.tensor_scalar(c8[:, 6, :], c8[:, 5, :], 1.0 / 19, None, ALU.mult))
            for d in (17, 15, 13, 11, 9, 7, 5, 3):
                step.wait()
                step(V.scalar_tensor_tensor(c8[:, 6, :], c8[:, 6, :], 1.0 / d, c8[:, 5, :], ALU.add, ALU.mult))
            step.wait()
            step(V.scalar_tensor_tensor(c8[:, 6, :], c8[:, 6, :], 1.0, c8[:, 4, :], ALU.add, ALU.mult))
            step(V.tensor_scalar(c8[:, 7, :], lam, -8.0, 0.0, ALU.mult, ALU.max))
            step.wait()
            step(V.scalar_tensor_tensor(c8[:, 8, :], c8[:, 6, :], 16.0, c8[:, 7, :], ALU.mult, ALU.add))
            step.wait()
            V.tensor_scalar(c8[:, 9, :], c8[:, 8, :], -1.0, None, ALU.mult).then_inc(softp, 1)
            for b in range(2):
                block_evict("in_a", b, proj, N_IN)
            turn_evict("xr", lambda i: xpad[:, i, 3:259])
            dve.wait_ge(turn_act, turn["xr"][1] + 4)
            dve.wait_ge(turn_dve, turn["xr"][2] + 4)
            dve.wait_ge(bd_zero, 1)
            cw, cb = cols["conv_w"], cols["conv_b"]
            for c in range(8):
                step(V.tensor_scalar(xc[:, c, :], xpad[:, c, 0:S], cw[:, c:c + 1], cb[:, c:c + 1], ALU.mult, ALU.add))
            for k in range(1, 4):
                for c in range(8):
                    step.wait(7 if k < 3 else 7 - c)
                    ins = V.scalar_tensor_tensor(xc[:, c, :], xpad[:, c, k:k + S], cw[:, 8 * k + c:8 * k + c + 1],
                                                 xc[:, c, :], ALU.mult, ALU.add)
                    if k < 3:
                        step(ins)
                    else:
                        ins.then_inc(rnn_xc, 1)
            in_loop("in_a", 0, 1, 8)
            dve.wait_ge(small_in, 16 * 4)
            blocks_in("in_a", 8)
            for t in range(NT):
                rope_small(proj[:, t, C_Q:C_V], t, 20)
            s0, e0 = prod["in_tail"]
            dve.wait_ge(slot_read, s0 + 2)
            V.tensor_copy(proj[:, 1, C_IK:C_GA], G[:, 2 * (e0 % 2) + 1, 0:C_GA - C_IK]).then_inc(ev_dve, 1)
            dve.wait_ge(rnn_sig, 8)
            step(V.tensor_tensor(R2[:, :, :], R2[:, :, :], xc[:, :, :], ALU.mult))
            dve.wait_ge(rnn_ta, 1)
            step.wait()
            step(V.tensor_scalar(xc[:, :, :], R3[:, :, :], 1.0, None, ALU.add))
            step.wait()
            step(V.reciprocal(xc[:, :, :], xc[:, :, :]))
            step.wait()
            step(V.scalar_tensor_tensor(R3[:, :, :], R3[:, :, :], 2.0, xc[:, :, :], ALU.mult, ALU.mult))
            step.wait()
            V.tensor_scalar(R3[:, :, :], R3[:, :, :], 1e-30, None, ALU.max).then_inc(rnn_sq, 1)
            blocks_in("in_tail", 1)
            ik = proj[:, :, C_IK:C_IK + HD]
            step(V.tensor_reduce(rq[:, 4, 0:2], ik, AX.X, ALU.add))
            step.wait()
            step(V.tensor_scalar(rq[:, 4, 2:4], rq[:, 4, 0:2], 1.0 / HD, None, ALU.mult))
            step.wait()
            for t in range(NT):
                step(V.tensor_scalar(ik[:, t, :], ik[:, t, :], rq[:, 4, 2 + t:3 + t], None, ALU.subtract))
            step.wait()
            ik2 = zf[:, 1024:1024 + NT * HD].rearrange("p (t d) -> p t d", t=NT)
            step(V.tensor_tensor(ik2, ik, ik, ALU.mult))
            step.wait()
            step(V.tensor_reduce(rq[:, 4, 4:6], ik2, AX.X, ALU.add))
            step(rsqrt(rq[:, 4, 6:8], rq[:, 4, 4:6], 2, HD))
            step.wait()
            for t in range(NT):
                step(V.scalar_tensor_tensor(ik[:, t, :], ik[:, t, :], rq[:, 4, 6 + t:7 + t], lnrow[:, 0, :], ALU.mult, ALU.mult))
            step.wait()
            step(V.tensor_tensor(ik, ik, lnrow[:, 1, :].unsqueeze(1).to_broadcast((P, NT, HD)), ALU.add))
            step(V.tensor_scalar(iws[:, :, :], proj[:, :, C_IW:C_IW + 8], IDX_SCALE, None, ALU.mult))
            for t in range(NT):
                rope_small(proj[:, t, C_IQ:C_IW], t, 9)
            step.wait()
            dve.wait_ge(gelu_ok, 1)
            double_keys(0, proj[:, :, C_K:C_V], 4)
            for b in range(2):
                step(V.tensor_copy(ikd[:, :, b * HD:(b + 1) * HD], ik))
            step.wait()
            V.engine_nop().then_inc(qk_ready, 1)
            product_evict("in_b1", proj[:, :, C_GA:C_GB], D)
            turn_evict("q", lambda i: qT[:, i, :])
            turn_evict("kiq", lambda i: kT[:, i, 0:S] if i < 4 else kT[:, i - 4, S:2 * S])

            def score(t, b):
                return zf[:, t * NB + b * S:t * NB + b * S + P * (t + 1)]

            for u in range(16):
                h, t = u // 2, u % 2
                nk = P * (t + 1)
                dve.wait_ge(idx_relu, u + 1)
                src = yf[:, (u % 4) * S:(u % 4) * S + nk]
                if h == 0:
                    ins = V.tensor_scalar(score(t, 0), src, iws[:, t, h:h + 1], None, ALU.mult)
                else:
                    dve.wait_ge(idx_acc, u - 1)
                    ins = V.scalar_tensor_tensor(score(t, 0), src, iws[:, t, h:h + 1], score(t, 0), ALU.mult, ALU.add)
                ins.then_inc(idx_acc, 1)
            dve.wait_ge(idx_acc, 16)
            for t in range(NT):
                late = score(t, 0)[:, t * P:(t + 1) * P]
                step(V.tensor_tensor(late, late, causal[:, :], ALU.add))
            dve.wait_ge(rnn_root, 1)
            step(V.tensor_tensor(R2[:, :, :], R2[:, :, :], R3[:, :, :], ALU.mult))
            step.wait()
            for c in range(8):
                ins = V.tensor_tensor_scan(xc[:, c, :], R1[:, c, :], R2[:, c, :], 0.0, ALU.mult, ALU.add)
            ins.then_inc(rnn_scan, 1)
            dve.wait_ge(rnn_scan, 1)
            for r in range(TOPK // 8):
                for t in range(NT):
                    if r:
                        step.wait(1)
                    step(V.max(top8[:, t, :], score(t, r % 2)))
                for t in range(NT):
                    step.wait(1)
                    step(V.match_replace(score(t, 1 - r % 2), top8[:, t, :], score(t, r % 2), TAKEN))
            step.wait()
            for t in range(NT):
                step(V.tensor_scalar(bias1[:, t, 0:P * (t + 1)], score(t, 0), -2e38, MASKED, ALU.is_gt, ALU.mult))
            step.wait()
            for t in range(NT):
                late = bias1[:, t, t * P:(t + 1) * P]
                step(V.tensor_tensor(late, late, causal[:, :], ALU.add))
            product_evict("in_b2", proj[:, :, C_GB:N_IN], D)
            for c in range(8):
                if c // 2 % 2:
                    dve.wait_ge(turned, turn["gr"][0] + c // 2 * 2 + 2)
                    V.scalar_tensor_tensor(R3[:, c, :], xc[:, c, :], 0.5, T[:, c // 2, (c % 2) * S:(c % 2 + 1) * S],
                                           ALU.mult, ALU.mult).then_inc(turn_dve, 1)
                else:
                    dve.wait_ge(turn_act, turn["gr"][1] + 2 * (c // 4) + c % 2 + 1)
                    step(V.scalar_tensor_tensor(R3[:, c, :], xc[:, c, :], 0.5, R2[:, c, :], ALU.mult, ALU.mult))
            step.wait()
            dve.wait_ge(turn_dve, turn["gr"][2] + 4)
            V.engine_nop().then_inc(rnn_y, 1)
            attention("a1", bias1, 0)
            dve.wait_ge(sg_ready, 1)
            yb = proj[:, :, C_Q:C_Q + D]

            def gated(name, dst, gcol):
                s0, e0 = prod[name]
                for b in range(2):
                    c = slice(b * NB, (b + 1) * NB)
                    dve.wait_ge(slot_read, s0 + 2 * b + 2)
                    V.tensor_tensor(dst[:, 1, c], G[:, 2 * ((e0 + b) % 2) + 1, :],
                                    proj[:, 1, gcol + b * NB:gcol + (b + 1) * NB], ALU.mult).then_inc(ev_dve, 1)
                evicted(name)
                step(V.tensor_tensor(dst[:, 0, :], dst[:, 0, :], proj[:, 0, gcol:gcol + D], ALU.mult))

            gated("y_a", Y, C_GA)
            turn_evict("o1", lambda i: HT[:, i, :])
            gated("y_b", yb, C_GB)
            step.wait()
            V.tensor_tensor(Y[:, :, :], Y[:, :, :], yb, ALU.add).then_inc(mrg_ok, 1)
            mod_columns(0)
            turn_evict("mrg", lambda i: qT[:, i, :])
            product_evict("w_o", Y, D)
            dve.wait_ge(late_in, 16 * 5)
            evicted("w_o")
            residual("p1", Y, bc[:, 0, :], x)
            norm("nf1", x, Y)
            mod_evict(1)
            norm("n_c0", cx, Z)
            turn_evict("hf1", lambda i: HT[:, i, :], lambda i: cols["norm_ffn_pre"][:, i:i + 1])
            mod_columns(1)
            mod_scale(0, 0)
            turn_evict("h_c0", lambda i: HC[:, i, :], lambda i: hscale[:, 0, 0, 1, i:i + 1], lambda i: modcol[:, 0, i, 1:2])
            step(V.tensor_scalar(nsink[:, :], nsink[:, :], -1.0, None, ALU.mult))
            ffn("1")
            down_evict("1", Y)
            evicted("down1")
            residual("pf1", Y, bc[:, 1, :], x)
            norm("n_x0", x, Y)
            mod_gate(0, 0)
            diagonal(0, gtg[:, 0, 0, 0, :])
            product_evict("qkv_c0", pc, N_EVEN)
            spread_row(0, bc[:, 0, :])
            diagonal(1, gtg[:, 0, 0, 1, :])
            turn_evict("h_x0", lambda i: HT[:, i, :], lambda i: hscale[:, 0, 0, 0, i:i + 1], lambda i: modcol[:, 0, i, 0:1])
            spread_row(1, bc[:, 1, :])
            evicted("qkv_c0")
            dve.wait_ge(band_in, 16 * 3)
            for t in range(NT):
                qk_norm(pc, t, 0, 10)
            for b, c0, heads in ((0, 0, 8), (1, 512, 2)):
                block_evict("qkv_x0", b, px, N_EVEN)
                blocks_in("qkv_x0", b + 1)
                for t in range(NT):
                    qk_norm(px, t, c0, heads)
                    rope_axial(px[:, t, c0:c0 + heads * HD], t, heads)
            block_evict("qkv_x0", 2, px, N_EVEN)
            step.wait()
            double_keys(0, px[:, :, 512:640], 2)
            double_keys(2, pc[:, :, 512:640], 2)
            step.wait()
            V.engine_nop().then_inc(qk_ready, 1)
            turn_evict("q_xc", lambda i: qT[:, i, :])
            turn_evict("k_xc", lambda i: kT[:, i % 2, (i // 2) * S:(i // 2 + 1) * S])
            attention("ax", None, 0)
            attention("ac", None, NB)
            for i, dst in enumerate((HT, HC)):
                dve.wait_ge(pool_mm, i + 1)
                V.tensor_copy(qT[:, 4 * i + 2:4 * i + 4, :], T[:, 1, :].rearrange("p (g n) -> p g n", g=2)).then_inc(pool_d, 1)
                dve.wait_ge(pool_y, i + 1)
                for g in range(2, 4):
                    V.tensor_scalar(dst[:, 4 + g, :], T[:, 3, (g - 2) * S:(g - 1) * S], cols["we_pool_scale_2"][:, g:g + 1], None,
                                    ALU.mult).then_inc(pool_ok, 1)
            turn_evict("o_x", lambda i: HT[:, i, :])
            turn_evict("o_c", lambda i: HC[:, i, :])
            mod_columns(2)
            mod_columns(3)
            mod_gate(0, 1)
            diagonal(2, gtg[:, 0, 1, 0, :])
            mod_scale(0, 1)
            mod_scale(1, 0)
            product_evict("out_x0", Y, D)
            spread_row(2, bc2[:, 0, :])
            diagonal(3, gtg[:, 0, 1, 1, :])
            evicted("out_x0")
            residual("p_x0", Y, bc[:, 0, :], x)
            norm("nf_x0", x, Y)
            dve.wait_ge(turn_act, turn["o_c"][1] + 2)
            dve.wait_ge(turn_dve, turn["o_c"][2] + 2)
            product_evict("out_c0", Z, D)
            spread_row(3, bc2[:, 1, :])
            turn_evict("hf_x0", lambda i: HT[:, i, :], lambda i: hscale[:, 0, 1, 0, i:i + 1], lambda i: modcol[:, 0, 24 + i, 0:1])
            evicted("out_c0")
            residual("p_c0", Z, bc[:, 1, :], cx)
            norm("nf_c0", cx, Z)
            ffn("_x0")
            down_evict("_x0", Y)
            turn_evict("hf_c0", lambda i: HC[:, i, :], lambda i: hscale[:, 0, 1, 1, i:i + 1], lambda i: modcol[:, 0, 24 + i, 1:2])
            evicted("down_x0")
            residual("pf_x0", Y, bc2[:, 0, :], x)
            norm("n_x1", x, Y)
            ffn("_c0")
            down_evict("_c0", Z)
            turn_evict("h_x1", lambda i: HT[:, i, :], lambda i: hscale[:, 1, 0, 0, i:i + 1], lambda i: modcol[:, 1, i, 0:1])
            evicted("down_c0")
            residual("pf_c0", Z, bc2[:, 1, :], cx)
            norm("n_c1", cx, Z)
            for b in range(2):
                block_evict("qkv_x1", b, px, N_ODD)
            blocks_in("qkv_x1", 2)
            for t in range(NT):
                rope_axial(px[:, t, 0:D], t, 16)
            block_evict("qkv_x1", 2, px, N_ODD)
            blocks_in("qkv_x1", 3)
            turn_evict("h_c1", lambda i: HC[:, i, :], lambda i: hscale[:, 1, 0, 1, i:i + 1], lambda i: modcol[:, 1, i, 1:2])
            for t in range(NT):
                rope_axial(px[:, t, D:D + S], t, 4)
            step.wait()
            double_keys(0, px[:, :, D:D + S], 4)
            product_evict("kv_c1", pc[:, :, D:N_ODD], NB)
            evicted("kv_c1")
            double_keys(2, pc[:, :, D:D + S], 4)
            step.wait()
            V.engine_nop().then_inc(qk_ready, 1)
            turn_evict("q_1", lambda i: qT[:, i, :])
            turn_evict("k_1", lambda i: kT[:, i % 4, (i // 4) * S:(i // 4 + 1) * S])
            attention("a1x", band, 0)
            turn_evict("o_1", lambda i: HT[:, i, :])
            mod_columns(4)
            mod_gate(1, 0)
            diagonal(4, gtg[:, 1, 0, 0, :])
            product_evict("out_x1", Y, D)
            spread_row(4, bc[:, 0, :])
            evicted("out_x1")
            residual("p_x1", Y, bc[:, 0, :], x)
            norm("nf_x1", x, Y)
            mod_evict(5)
            mod_columns(5)
            mod_scale(1, 1)
            mod_gate(1, 1)
            turn_evict("hf_x1", lambda i: HT[:, i, :], lambda i: hscale[:, 1, 1, 0, i:i + 1], lambda i: modcol[:, 1, 24 + i, 0:1])
            diagonal(5, gtg[:, 1, 1, 0, :])
            spread_row(5, bc[:, 1, :])
            ffn("_x1")
            down_evict("_x1", Y)
            evicted("down_x1")
            residual("pf_x1", Y, bc[:, 1, :], x)


def shape_constants():
    f32 = np.float32
    pos = np.arange(S)
    tile = lambda a: np.ascontiguousarray(a.reshape(NT, P, *a.shape[1:]).swapaxes(0, 1)).astype(f32)
    causal = np.where(pos[None, :P] <= pos[:P, None], 0.0, MASKED)
    band = np.concatenate([np.where(np.abs(pos[None, :] - pos[:, None]) <= 128, 0.0, MASKED), np.zeros((S, S))], axis=1)

    def angles(at, freq):
        a = at.astype(f32)[:, None] * freq[None, :]
        return np.cos(a).astype(f32), np.sin(a).astype(f32)

    f1 = (f32(500000.0) ** (-np.arange(8, dtype=f32) / f32(8))).astype(f32)
    f2 = (f32(10000.0) ** (-np.arange(16, dtype=f32) / f32(16))).astype(f32)
    rope1 = np.stack(angles(pos, f1), axis=1)
    (cr, sr), (cc, sc) = angles(pos // 64, f2), angles(pos % 64, f2)
    rope2 = np.stack([np.concatenate([cr, cc], 1), np.concatenate([sr, sc], 1)], axis=1)
    pool = np.zeros((4, S, S))
    for g, w in enumerate((2, 4, 8, 16)):
        lo, hi = np.clip(pos - w // 2, 0, S), np.clip(pos + w - w // 2, 0, S)
        inside = (pos[:, None] >= lo[None, :]) & (pos[:, None] < hi[None, :])
        pool[g] = inside / (hi - lo)[None, :] - np.eye(S)
    pool = pool.reshape(4, NT, P, S).transpose(2, 0, 1, 3)
    return {"ident": np.eye(P, dtype=f32), "causal": causal.astype(f32), "band": tile(band), "rope1": tile(rope1),
            "rope2": tile(rope2), "pool": np.ascontiguousarray(pool).astype(f32)}


def kernel(**inputs):
    import numpy as _np
    import concourse.bacc as _bacc
    from concourse import mybir as _mybir
    from concourse.bass_utils import run_bass_kernel_spmd as _run

    nc = _bacc.Bacc("TRN2", target_bir_lowering=False, num_devices=1)
    arrays, t_in, consts = {}, {}, {}
    for name, a in inputs.items():
        a = _np.ascontiguousarray(a)
        arrays[f"in_{name}"] = a
        t_in[name] = nc.dram_tensor(f"in_{name}", a.shape, _mybir.dt.from_np(a.dtype), kind="ExternalInput").ap()
    for name, a in shape_constants().items():
        arrays[f"const_{name}"] = a
        consts[name] = nc.dram_tensor(f"const_{name}", a.shape, _mybir.dt.from_np(a.dtype), kind="ExternalInput").ap()
    out = nc.dram_tensor("out", (1, S, D), F32, kind="ExternalOutput").ap()
    build(nc, t_in, consts, out)
    r = _run(nc, [arrays], core_ids=[0])
    return r.results[0]["out"]
```

```python
import math
from contextlib import ExitStack

import numpy as np
import concourse.bass as bass
from concourse import mybir

F32 = mybir.dt.float32
F32R = mybir.dt.float32r
I32 = mybir.dt.int32
ACT = mybir.ActivationFunctionType
ALU = mybir.AluOpType
AX = mybir.AxisListType

P = 128
S = 256
NT = S // P
D = 1024
KC = D // P
HD = 64
F = 2816
FC = F // P
NB = 512
FB = F // S
N_IN = 6216
C_XR, C_GR, C_Q, C_K, C_V, C_IQ, C_IK, C_IW, C_GA, C_GB = 0, 1024, 2048, 3072, 3328, 3584, 4096, 4160, 4168, 5192
N_EVEN, N_ODD = 1280, 1536
TOPK = 64
EPS = 1e-6
SCALE = HD ** -0.5
IDX_SCALE = (8 ** -0.5) * (64 ** -0.5)
MASKED = -1e30
TAKEN = -3e38
RING = 4

SV1 = [("norm_mix_pre", 8), ("conv_w", 32), ("conv_b", 8), ("rg_b_a", 8), ("rg_b_x", 8), ("rg_lambda", 8),
       ("norm_ffn_pre", 8), ("g_pre_mix_2", 16), ("g_pre_ffn_2", 16), ("c_2", 8), ("c_ctx_2", 8)]
SV2 = [("we_pool_scale_2", 4), ("g_post_mix_2", 16), ("g_post_ffn_2", 16)]
SV3 = [("b_mod_2", 96)]

MODG = 8
PRODUCTS = [("in_a", 16, 8), ("in_tail", 2, 1), ("in_b1", 4, 2), ("in_b2", 4, 2), ("mod0", MODG, 0), ("y_a", 4, 2),
            ("y_b", 4, 2), ("w_o", 4, 2), ("mod1", MODG, 1), ("up1", 22, FB), ("down1", 11, 2),
            ("qkv_c0", 6, 3), ("qkv_x0", 6, 3), ("mod2", MODG, 0), ("mod3", MODG, 0), ("out_x0", 4, 2), ("out_c0", 4, 2),
            ("up_x0", 22, FB), ("down_x0", 11, 2), ("up_c0", 22, FB), ("down_c0", 11, 2),
            ("qkv_x1", 6, 3), ("kv_c1", 2, 1), ("mod4", MODG, 0), ("out_x1", 4, 2), ("mod5", MODG, 1), ("up_x1", 22, FB),
            ("down_x1", 11, 2)]
MOD_IN = {"a1": 0, "ax": 2, "ac": 3, "a1x": 4}
TURNS = [("h1", 8), ("xr", 8), ("q", 8), ("kiq", 8), ("ik", 1), ("gr", 8), ("o1", 8), ("mrg", 8), ("hf1", 8),
         ("h_c0", 8), ("h_x0", 8), ("q_xc", 8), ("k_xc", 4), ("o_x", 4), ("o_c", 4), ("hf_x0", 8), ("hf_c0", 8),
         ("h_x1", 8), ("h_c1", 8), ("q_1", 8), ("k_1", 8), ("o_1", 8), ("hf_x1", 8)]
SUMS = ["n1", "n_c0", "p1", "nf1", "pf1", "n_x0", "p_x0", "nf_x0", "p_c0", "nf_c0", "pf_x0", "n_x1", "pf_c0",
        "n_c1", "p_x1", "nf_x1", "pf_x1"]
ATTN = [("a1", 16, (128, 256)), ("ax", 8, (512, 512)), ("ac", 8, (256, 256)), ("a1x", 16, (512, 512))]
FFNS = ["1", "_x0", "_c0", "_x1"]
NF = 2 * FB + FC // 2
NA = 16
F0 = [NA + NF * i for i in range(len(FFNS) + 1)]


def starts(items, *cols):
    at, sums = {}, [0] * len(cols)
    for it in items:
        at[it[0]] = tuple(sums)
        sums = [s + it[c] for s, c in zip(sums, cols)]
    return at


def n_act(n):
    return sum(i // 2 % 2 == 0 for i in range(n))


def build(nc, t_in, consts, out):
    prod = starts(PRODUCTS, 1, 2)
    is_split = lambda n: n == "in_a" or n.startswith(("up", "down"))
    reads = dict((n, v[0]) for n, v in starts([(n, 0 if is_split(n) else k) for n, k, _ in PRODUCTS], 1).items())
    turn_n = dict(TURNS)
    turn, ca, cd, ct = {}, 0, 0, 0
    for name, n in TURNS:
        turn[name] = (ct, ca, cd)
        ct, ca, cd = ct + n, ca + n_act(n), cd + n - n_act(n)
    sums = dict((n, i) for i, n in enumerate(SUMS))
    att0 = starts([(n, 2 * h) for n, h, _ in ATTN], 1)
    ffn_i = dict((n, i) for i, n in enumerate(FFNS))

    with ExitStack() as ctx:
        def sb(name, *shape):
            return ctx.enter_context(nc.sbuf_tensor(name, [P, *shape], F32))

        def sem(name):
            return ctx.enter_context(nc.semaphore(name))

        G = ctx.enter_context(nc.psum_tensor("G", [P, 4, NB], F32))
        T = ctx.enter_context(nc.psum_tensor("T", [P, 4, NB], F32))

        with ExitStack() as under:
            def sbr(name, n):
                return under.enter_context(nc.sbuf_tensor(name, [P, n], F32R))

            hidT_h = sbr("hidT_h", FC * S)[:, :].rearrange("p (c s) -> p c s", c=FC)
            sbr("under_hid", 4096)
            xT_l = sbr("xT_l", KC * S)[:, :].rearrange("p (c s) -> p c s", c=KC)
            sbr("under_gain", NT * N_IN - FC * S - 4096 - KC * S)
            hidT_l = sbr("hidT_l", FC * S)[:, :].rearrange("p (c s) -> p c s", c=FC)
            w0_h, w0_l = sbr("w0_h", 2048), sbr("w0_l", 2048)
            sbr("under_rnn", 8 * 259 + 4 * 2048 - FC * S - 4096)
            w1_h, w1_l = sbr("w1_h", 2048), sbr("w1_l", 2048)
            xT_h = sbr("xT_h", KC * S)[:, :].rearrange("p (c s) -> p c s", c=KC)
            sbr("under_ring", RING * 2048 + NT * D)
            x1_h = sbr("x1_h", KC * S)[:, :].rearrange("p (c s) -> p c s", c=KC)
            x1_l = sbr("x1_l", KC * S)[:, :].rearrange("p (c s) -> p c s", c=KC)
        area = sb("area", NT * N_IN)
        rnn = sb("rnn", 8 * 259 + 4 * 2048)
        qT = sb("qT", 8, S)
        kT = sb("kT", 4, 2 * S)
        HT = sb("HT", KC, S)
        ring = sb("ring", RING, 2048)
        x = sb("x", NT, D)
        cx = sb("cx", NT, D)
        bc = sb("bc", 2, D)
        Y = sb("Y", NT, D)
        Z = sb("Z", NT, D)
        ikT = sb("ikT", S)
        bd = sb("bd", 2048 + 512)
        bias1 = sb("bias1", NT, S)
        causal = sb("causal", P)
        modrow = sb("modrow", NB)
        ident = sb("ident", P)
        ones = sb("ones", P)
        svc = sb("svc", 260)
        scT = sb("scT", KC, 32)
        modcol = sb("modcol", 2, 48, 2)
        hscale = sb("hscale", 2, 2, 2, 8)
        gtg = sb("gtg", 2, 2, 2, 8)
        rope1 = sb("rope1", NT, 2, 8)
        rope2 = sb("rope2", NT, 2, 32)
        lnrow = sb("lnrow", 2, HD)
        nsink = sb("nsink", 16)
        ssb = sb("ssb", 2, 2)
        rs = sb("rs", 2, 2)
        rq = sb("rq", 6, 40)
        c8 = sb("c8", 10, 8)
        amin = sb("amin", 4)
        asum = sb("asum", 4)
        arec = sb("arec", 4)
        top8 = sb("top8", NT, 8)
        iws = sb("iws", NT, 8)

        proj = area[:, :].rearrange("p (t n) -> p t n", t=NT)
        o_ = FC * S
        hid = area[:, o_:o_ + 1024].rearrange("p (b t n) -> p b t n", b=2, t=NT)
        gate = area[:, o_ + 1024:o_ + 2048].rearrange("p (b t n) -> p b t n", b=2, t=NT)
        o_ += 2048
        bc2 = area[:, o_:o_ + 2048].rearrange("p (r n) -> p r n", r=2)
        diag = area[:, o_ + 2048:o_ + 3072].rearrange("p (c n) -> p c n", c=KC)
        diag_last = area[:, 0:1024].rearrange("p (c n) -> p c n", c=KC)
        band = area[:, o_ + 3072:o_ + 4096].rearrange("p (t n) -> p t n", t=NT)
        qkgain = area[:, o_ + 4096:o_ + 4096 + 10 * HD]
        px = area[:, 0:NT * N_ODD].rearrange("p (t n) -> p t n", t=NT)
        pc = area[:, NT * N_ODD:2 * NT * N_ODD].rearrange("p (t n) -> p t n", t=NT)
        xpad = rnn[:, 0:8 * 259].rearrange("p (c n) -> p c n", c=8)
        o_ = 8 * 259
        xc, R1, R2, R3 = [rnn[:, o_ + 2048 * i:o_ + 2048 * (i + 1)].rearrange("p (c n) -> p c n", c=8) for i in range(4)]
        work = rnn[:, 0:4 * 516].rearrange("p (b n) -> p b n", b=4)
        pT = R1.rearrange("p (b c) n -> p b (c n)", b=4)
        HC = R2
        bda = bd[:, 0:1024].rearrange("p (c n) -> p c n", c=8)
        bdx = bd[:, 1024:2048].rearrange("p (c n) -> p c n", c=8)
        poolm = bd[:, 0:2048].rearrange("p (g k n) -> p g k n", g=4, k=NT)
        wpool = bd[:, 2048:2560].rearrange("p (g n) -> p g n", g=4)
        kd = Y[:, :, :].rearrange("p t n -> p (t n)").rearrange("p (k g n) -> p k g n", k=4, g=4)
        kd1 = rnn[:, 0:1024].rearrange("p (k g n) -> p k g n", k=NT, g=4)
        ikd = Z[:, 0, 0:2 * P].rearrange("p (t n) -> p t n", t=NT)
        svr = Z[:, 0, 0:3 * P].rearrange("p (i n) -> p i n", i=3)
        zf = Z[:, :, :].rearrange("p t n -> p (t n)")
        yf = Y[:, :, :].rearrange("p t n -> p (t n)")

        at, cols = 0, {}
        for base, rows in ((0, SV1), (P, SV2), (164, SV3)):
            at = base
            for name, n in rows:
                cols[name] = svc[:, at:at + n]
                at += n

        w_landed = [sem(f"w_landed{i}") for i in range(RING)]
        slot_read = sem("slot_read")
        ev_act = sem("ev_act")
        ev_dve = sem("ev_dve")
        turned = sem("turned")
        turn_act = sem("turn_act")
        turn_dve = sem("turn_dve")
        x_in = sem("x_in")
        first_in = sem("first_in")
        sv_in = sem("sv_in")
        small_in = sem("small_in")
        late_in = sem("late_in")
        bd_in = sem("bd_in")
        bd_zero = sem("bd_zero")
        band_in = sem("band_in")
        pool_in = sem("pool_in")
        sv_turned = sem("sv_turned")
        sv_done = sem("sv_done")
        ss_done = sem("ss_done")
        rs_done = sem("rs_done")
        xn_act = sem("xn_act")
        xn_dve = sem("xn_dve")
        x_new = sem("x_new")
        c_silu = sem("c_silu")
        mod_row = sem("mod_row")
        dstep = sem("dstep")
        astep = sem("astep")
        rnn_xc = sem("rnn_xc")
        rnn_gate = sem("rnn_gate")
        rnn_sig = sem("rnn_sig")
        rnn_ta = sem("rnn_ta")
        rnn_sq = sem("rnn_sq")
        rnn_u = sem("rnn_u")
        rnn_root = sem("rnn_root")
        softp_z = sem("softp_z")
        softp_e = sem("softp_e")
        softp = sem("softp")
        gelu_in = sem("gelu_in")
        gelu_t = sem("gelu_t")
        gelu_ok = sem("gelu_ok")
        qk_ready = sem("qk_ready")
        idx_mm = sem("idx_mm")
        idx_relu = sem("idx_relu")
        idx_acc = sem("idx_acc")
        sg_ready = sem("sg_ready")
        mrg_ok = sem("mrg_ok")
        mod_turned = sem("mod_turned")
        mod_ok = sem("mod_ok")
        diag_ok = sem("diag_ok")
        bc_mm = sem("bc_mm")
        bc_ok = sem("bc_ok")
        pool_mm = sem("pool_mm")
        pool_d = sem("pool_d")
        pool_y = sem("pool_y")
        pool_ok = sem("pool_ok")
        hid_turned = sem("hid_turned")
        hidT_hi = sem("hidT_hi")
        hidT_ok = sem("hidT_ok")
        split_mm = sem("split_mm")
        w_hi = sem("w_hi")
        w_lo_pool = sem("w_lo_pool")
        w_lo_dve = sem("w_lo_dve")
        xT_hi = sem("xT_hi")
        xT_ok = sem("xT_ok")
        gain_in = sem("gain_in")
        a_mm = sem("a_mm")
        a_min = sem("a_min")
        a_exp = sem("a_exp")
        a_turned = sem("a_turned")
        a_pT = sem("a_pT")
        a_pv = sem("a_pv")
        a_o = sem("a_o")
        stored = sem("stored")

        pstep = sem("pstep")
        rnn_y = sem("rnn_y")
        rnn_scan = sem("rnn_scan")
        hs_ok = sem("hs_ok")
        SV_DMAS = len(SV1) + len(SV2) + len(SV3) - 1
        kT_flat = kT[:, :, :].rearrange("p g n -> p (g n)")
        junk = bd[:, 0:2048].rearrange("p (t n) -> p t n", t=NT)
        HF = bd[:, 0:2048].rearrange("p (c n) -> p c n", c=KC)
        split_h = (w0_h[:, :], w1_h[:, :])
        split_l = (w0_l[:, :], w1_l[:, :])
        ring1 = ring[:, :, :]

        def logit_bank(u):
            return (T[:, 0, :], T[:, 1, :], G[:, 2, :])[u % 3]

        bias1_row = bias1[:, :, :].rearrange("p t n -> p (t n)")

        def mod_rows(g):
            return bias1_row if g == 3 else modrow[:, :]

        def mod_rows_done(name):
            return list(MOD_IN).index(name) + 1

        def chunks(w):
            return w.rearrange("(k p) n -> p k n", p=P)

        w = {n: t_in[n] for n in t_in}
        w_in = chunks(w["w_in"][0])
        ring4 = ring[:, :, :].rearrange("p r (k n) -> p r k n", k=4)
        ring2 = ring[:, :, :].rearrange("p r (k n) -> p r k n", k=2)
        up_w = {"1": (chunks(w["w_ffn_gate"][0]), chunks(w["w_ffn_up"][0])),
                "0": tuple(chunks(w["w_ffn_in_2"][0][:, i * F:(i + 1) * F]) for i in range(2)),
                "_x1": tuple(chunks(w["w_ffn_in_2"][1][:, i * F:(i + 1) * F]) for i in range(2))}
        down_w = {"1": chunks(w["w_ffn_down"][0]), "0": chunks(w["w_ffn_out_2"][0]), "_x1": chunks(w["w_ffn_out_2"][1])}
        for n in ("_x0", "_c0"):
            up_w[n], down_w[n] = up_w["0"], down_w["0"]
        plain = {"in_b1": w["w_in"][0][:, C_GA:C_GB], "in_b2": w["w_in"][0][:, C_GB:], "y_a": w["w_rnn_out"][0],
                 "y_b": w["w_att_out"][0], "w_o": w["w_o"][0], "qkv_c0": w["we_in_2"][0],
                 "qkv_x0": w["we_in_2"][0], "out_x0": w["we_out_2"][0], "out_c0": w["we_out_2"][0],
                 "qkv_x1": w["wo_in_2"][0], "kv_c1": w["wo_in_2"][0][:, D:N_ODD], "out_x1": w["wo_out_2"][0]}

        class Steps:

            def __init__(self, eng, s):
                self.eng, self.s, self.n = eng, s, 0

            def __call__(self, ins):
                self.n += 1
                ins.then_inc(self.s, 1)

            def wait(self, back=0):
                self.eng.wait_ge(self.s, self.n - back)

        block = ctx.enter_context(nc.Block())

        @block.sync
        def _(sp):
            def split_free(n):
                sp.wait_ge(w_lo_pool, n + 1)
                sp.wait_ge(w_lo_dve, n + 1)

            def slot_free(s):
                if s >= RING:
                    name = [n for n, k, _ in PRODUCTS if prod[n][0] <= s - RING < prod[n][0] + k][0]
                    at = s - RING - prod[name][0]
                    if name == "in_a":
                        split_free(s - RING)
                    elif is_split(name):
                        f = [n for n in FFNS if name in ("up" + n, "down" + n)][0]
                        split_free(F0[ffn_i[f]] + s - RING - prod["up" + f][0])
                    else:
                        sp.wait_ge(slot_read, reads[name] + at + 1)

            def fill(slot, s, parts):
                if s is not None:
                    slot_free(s)
                for dst, src in parts:
                    sp.dma_start(dst, src).then_inc(w_landed[slot], 16)

            def half_block(slot, s, wv, half, col, n):
                fill(slot, s, [(ring4[:, slot, 2 * i:2 * i + 2, 0:n],
                                wv[:, 4 * half + 2 * i:4 * half + 2 * i + 2, col]) for i in range(2)])

            def product(name):
                s0 = prod[name][0]
                wv = chunks(plain[name])
                total = wv.shape[2]
                for b in range(-(-total // NB)):
                    n = min(NB, total - b * NB)
                    for h in range(2):
                        s = s0 + 2 * b + h
                        half_block(s % RING, s, wv, h, slice(b * NB, b * NB + n), n)

            def in_pair(it):
                for j in range(RING):
                    c = (2 * it + j // 2) * NB
                    half_block(j, it * RING + j, w_in, j % 2, slice(c, c + NB), NB)

            def mod_group(g):
                s0 = prod[f"mod{g}"][0]
                wv = chunks(w["w_mod_2"][g // 3])
                for j in range(MODG):
                    c = ((g % 3) * 4 + j // 2) * NB
                    half_block((s0 + j) % RING, s0 + j, wv, j % 2, slice(c, c + NB), NB)

            def ffn(name):
                s0 = prod["up" + name][0]
                wg, wu = up_w[name]

                def half_pair(j, s, col):
                    slot, h = (s0 + j) % RING, j % 2
                    fill(slot, s, [(ring4[:, slot, :, S * i:S * i + S], wv[:, 4 * h:4 * h + 4, col])
                                   for i, wv in enumerate((wg, wu))])

                for j in range(6):
                    half_pair(j, s0 + j, slice(j // 2 * S, j // 2 * S + S))
                with sp.Fori(1, FB // 2) as it:
                    for j in range(2, 6):
                        split_free(it * 4 + (F0[ffn_i[name]] + j - RING))
                        half_pair(j, None, bass.ds(it * (2 * S) + (j // 2) * S, S))
                s0 = prod["down" + name][0]
                wd = down_w[name]
                for j in range(FC // 2):
                    slot = (s0 + j) % RING
                    fill(slot, s0 + j, [(ring2[:, slot, i:i + 1, :], wd[:, 2 * j + i:2 * j + i + 1, :]) for i in range(2)])

            sp.dma_start(x[:, :, :], w["x"][0].rearrange("(t p) n -> p t n", p=P)).then_inc(x_in, 16)
            in_pair(0)
            for i, group in enumerate((SV1, SV2, SV3)):
                r = 0
                for name, n in group:
                    src = w[name]
                    if len(src.shape) == 1:
                        src = src.rearrange("(r n) -> r n", n=P)
                    elif len(src.shape) == 2:
                        src = src.rearrange("a (r n) -> (a r) n", n=P)
                    else:
                        src = src.rearrange("a b (r n) -> (a b r) n", n=P)
                    if name != "norm_mix_pre":
                        sp.dma_start(svr[r:r + n, i, :], src).then_inc(sv_in, 16)
                    r += n
            in_pair(1)
            sp.dma_start(rope1[:, :, :, :], consts["rope1"]).then_inc(small_in, 16)
            sp.dma_start(causal[:, :], consts["causal"]).then_inc(small_in, 16)
            sp.dma_start(lnrow[:, 0, :], w["idx_k_ln_g"][0:1, :].to_broadcast((P, HD))).then_inc(small_in, 16)
            sp.dma_start(lnrow[:, 1, :], w["idx_k_ln_b"][0:1, :].to_broadcast((P, HD))).then_inc(small_in, 16)
            sp.wait_ge(bd_zero, 1)
            for m, name in ((bda, "rg_w_a"), (bdx, "rg_w_x")):
                v = w[name][0].rearrange("(c b) i j -> b i c j", b=2)
                for b in range(2):
                    sp.dma_start(m[b * HD:(b + 1) * HD, :, b * HD:(b + 1) * HD], v[b]).then_inc(bd_in, 16)
            with sp.Fori(2, 4) as it:
                for j in range(RING):
                    split_free(it * RING + (j - RING))
                    half_block(j, None, w_in, j % 2, bass.ds(it * (2 * NB) + (j // 2) * NB, NB), NB)
            s0 = prod["in_tail"][0]
            for h in range(2):
                half_block((s0 + h) % RING, s0 + h, w_in, h, slice(C_IK, C_GA), C_GA - C_IK)
            product("in_b1")
            product("in_b2")
            sp.wait_ge(split_mm, NA)
            sp.dma_start(bc[:, 0, :], w["norm_mix_post"][0:1, :].to_broadcast((P, D))).then_inc(late_in, 16)
            sp.dma_start(bc[:, 1, :], w["norm_ffn_post"][0:1, :].to_broadcast((P, D))).then_inc(late_in, 16)
            sp.dma_start(cx[:, :, :], w["ctx_2"][0].rearrange("(t p) n -> p t n", p=P)).then_inc(late_in, 16)
            sp.dma_start(rope2[:, :, :, :], consts["rope2"]).then_inc(late_in, 16)
            sp.dma_start(nsink[:, :], w["wo_sink_2"][0:1, :].to_broadcast((P, 16))).then_inc(late_in, 16)
            mod_group(0)
            product("y_a")
            product("y_b")
            product("w_o")
            mod_group(1)
            ffn("1")
            product("qkv_c0")
            product("qkv_x0")
            mod_group(2)
            mod_group(3)
            product("out_x0")
            product("out_c0")
            ffn("_x0")
            ffn("_c0")
            product("qkv_x1")
            product("kv_c1")
            mod_group(4)
            product("out_x1")
            mod_group(5)
            ffn("_x1")
            sp.wait_ge(x_new, NT * len([n for n in SUMS if n[0] == "p"]))
            sp.dma_start(out[0].rearrange("(t p) n -> p t n", p=P), x[:, :, :]).then_inc(stored, 16)
            sp.wait_ge(stored, 16)

        @block.tensor
        def _(pe):
            def free(waits):
                for s, v in waits:
                    pe.wait_ge(s, v)

            def pair_free(e):
                if not isinstance(e, int) or e >= 2:
                    pe.wait_ge(ev_act, e - 1)
                    pe.wait_ge(ev_dve, e - 1)

            def landed(s, fills=None):
                pe.wait_ge(w_landed[s % RING], 32 * (s // RING + 1) if fills is None else fills)

            def rows(s, half, e, lhsT, n, fills=None):
                landed(s, fills)
                for t in range(NT):
                    for k in range(4):
                        mm = nc.tensor.matmul(G[:, 2 * (e % 2) + t, 0:n], lhsT[:, 4 * half + k, t * P:(t + 1) * P],
                                              ring4[:, s % RING, k, 0:n], start=(half == 0 and k == 0),
                                              stop=(half == 1 and k == 3))
                mm.then_inc(slot_read, 1)

            def product(name, lhsT, total, first=0, last=None):
                s0, e0 = prod[name]
                for b in range(first, last or -(-total // NB)):
                    pair_free(e0 + b)
                    for h in range(2):
                        rows(s0 + 2 * b + h, h, e0 + b, lhsT, min(NB, total - b * NB))

            def split_ready(n):
                pe.wait_ge(w_lo_pool, n)
                pe.wait_ge(w_lo_dve, n)

            def three(dst, a, b, w_h, w_l, start, stop):
                nc.tensor.matmul(dst, a, w_h, start=start, stop=False)
                nc.tensor.matmul(dst, a, w_l, start=False, stop=False)
                return nc.tensor.matmul(dst, b, w_h, start=False, stop=stop)

            def split_rows(h, buf, bank, x_h, x_l):
                w_h, w_l = [v[buf].rearrange("p (k n) -> p k n", k=4) for v in (split_h, split_l)]
                for t in range(NT):
                    for k in range(4):
                        c, tok = 4 * h + k, slice(t * P, (t + 1) * P)
                        mm = three(G[:, bank + t, :], x_h[:, c, tok], x_l[:, c, tok], w_h[:, k, :], w_l[:, k, :],
                                   c == 0, c == KC - 1)
                mm.then_inc(split_mm, 1)

            def in_block(b, it=None):
                if it is not None:
                    pe.wait_ge(ev_act, it * 2 + (b - 1))
                    pe.wait_ge(ev_dve, it * 2 + (b - 1))
                for h in range(2):
                    if it is None and b == 0:
                        pe.wait_ge(xT_ok, h + 1)
                    split_ready((0 if it is None else it * 4) + (2 * b + h + 1))
                    split_rows(h, h, 2 * b, x1_h, x1_l)

            def mod_slot(g, j, bank):
                s, q = prod[f"mod{g}"][0] + j, j // 2
                if g == 0 and j == 0:
                    pe.wait_ge(c_silu, 1)
                landed(s)
                for k in range(4):
                    mm = nc.tensor.matmul(G[32 * q:32 * q + 32, bank, :], scT[:, 4 * (j % 2) + k, :], ring4[:, s % RING, k, :],
                                          start=(j % 2 == 0 and k == 0), stop=(j % 2 == 1 and k == 3),
                                          tile_position=(0, 32 * q))
                mm.then_inc(slot_read, 1)

            def mod_group(g):
                e0 = prod[f"mod{g}"][1]
                pair_free(e0)
                for j in range(MODG):
                    mod_slot(g, j, 2 * (e0 % 2))

            def mod_turn(g, waits):
                e0 = prod[f"mod{g}"][1]
                free(waits)
                inside = [n for n in MOD_IN if MOD_IN[n] == g]
                if inside:
                    pe.wait_ge(mod_row, mod_rows_done(inside[0]))
                else:
                    pe.wait_ge(ev_act, e0 + 1)
                    pe.wait_ge(ev_dve, e0 + 1)
                for c in range(4):
                    tr = nc.tensor.transpose(T[:, 2 + g % 2, c * P:(c + 1) * P],
                                             mod_rows(g)[:, c * P:(c + 1) * P], ident[:, :])
                tr.then_inc(mod_turned, 1)
                return [(mod_ok, g + 1)]

            def turn_stage(name, src, waits, ready=()):
                n, (c0, _, _) = turn_n[name], turn[name]
                free(waits)
                for s, v in ready:
                    pe.wait_ge(s, v)
                for i in range(n):
                    for t in range(NT):
                        tr = nc.tensor.transpose(T[:, i // 2, (i % 2) * S + t * P:(i % 2) * S + (t + 1) * P],
                                                 src(i, t), ident[:, :])
                    tr.then_inc(turned, 1)
                return [(turn_act, turn[name][1] + n_act(n)), (turn_dve, turn[name][2] + n - n_act(n))]

            def norm_turn(name, sname, src, waits):
                k = sums[sname] + 1
                n_x = 1 + [n for n in SUMS[:k] if n[0] == "n"].index(sname)
                return turn_stage(name, lambda i, t: src[:, t, i * P:(i + 1) * P], waits,
                                  [(xn_act, n_x), (xn_dve, n_x)])

            def ffn(name, waits, after_block0=None, in_down=None):
                f = ffn_i[name]
                e0 = prod["up" + name][1]
                h0 = FB * f
                free(waits)

                def up_block(j, it=None):
                    more = 0 if it is None else it
                    pe.wait_ge(ev_act, more * 2 + (e0 + j - 1))
                    pe.wait_ge(ev_dve, more * 2 + (e0 + j - 1))
                    for h in range(2):
                        if j == 0:
                            pe.wait_ge(xT_ok, 2 * (f + 1) + h + 1)
                        split_ready(more * 4 + (F0[f] + 2 * j + h + 1))
                        split_rows(h, (f + h) % 2, 2 * ((e0 + j) % 2), xT_h, xT_l)

                def turn_hidden(j, it=None):
                    more = 0 if it is None else it
                    pe.wait_ge(ev_dve, more * 2 + (e0 + j + 1))
                    if not (f == 0 and j < 2 and it is None):
                        pe.wait_ge(hidT_ok, more * 2 + (h0 + j - 1))
                    for c in range(2):
                        for t in range(NT):
                            tr = nc.tensor.transpose(T[:, j % 2, c * S + t * P:c * S + (t + 1) * P],
                                                     hid[:, j % 2, t, c * P:(c + 1) * P], ident[:, :])
                    tr.then_inc(hid_turned, 1)

                up_block(0)
                if after_block0:
                    after_block0()
                up_block(1)
                turn_hidden(0)
                up_block(2)
                turn_hidden(1)
                with pe.Fori(1, FB // 2) as it:
                    up_block(1, it)
                    turn_hidden(0, it)
                    up_block(2, it)
                    turn_hidden(1, it)
                e0d = prod["down" + name][1]
                pair_free(e0d)
                pair_free(e0d + 1)
                for j in range(FC // 2):
                    split_ready(F0[f] + 2 * FB + j + 1)
                    if j == 1:
                        turn_hidden(FB - 1)
                    if j == 4 and in_down:
                        in_down()
                    pe.wait_ge(hidT_ok, h0 + j + 1)
                    w_h, w_l = [v[(f + j) % 2].rearrange("p (k n) -> p k n", k=2) for v in (split_h, split_l)]
                    for k in range(2):
                        for t in range(NT):
                            for h in range(2):
                                c, tok, col = 2 * j + k, slice(t * P, (t + 1) * P), slice(h * NB, (h + 1) * NB)
                                mm = three(G[:, 2 * ((e0d + h) % 2) + t, :], hidT_h[:, c, tok], hidT_l[:, c, tok],
                                           w_h[:, k, col], w_l[:, k, col], c == 0, c == FC - 1)
                    mm.then_inc(split_mm, 1)
                return []

            def attention(name, qs, ks, vs, waits, e_next):
                heads, nks = [a[1:] for a in ATTN if a[0] == name][0]
                u0 = att0[name][0]
                n = 2 * heads
                free(waits)
                pe.wait_ge(ev_act, e_next)
                pe.wait_ge(ev_dve, e_next)

                def unit(u):
                    return 2 * (u // 4) + u % 2, (u // 2) % 2

                def scores(u):
                    h, t = unit(u)
                    if u >= 3:
                        pe.wait_ge(a_min, u0 + u - 2)
                    nc.tensor.matmul(logit_bank(u)[:, 0:nks[t]], qs(h, t), ks(h, t), start=True, stop=True).then_inc(a_mm, 1)

                def turn_probs(u):
                    h, t = unit(u)
                    pe.wait_ge(a_exp, u0 + u + 1)
                    if u >= 2:
                        pe.wait_ge(a_pT, u0 + u - 1)
                    for k in range(nks[t] // P):
                        tr = nc.tensor.transpose(T[:, 2 + u % 2, k * P:(k + 1) * P], work[:, u % 4, k * P:(k + 1) * P], ident[:, :])
                    tr.then_inc(a_turned, 1)

                def values(u):
                    h, t = unit(u)
                    pe.wait_ge(a_pT, u0 + u + 1)
                    if u >= 2:
                        pe.wait_ge(a_o, u0 + u - 1)
                    for k in range(nks[t] // P):
                        mm = nc.tensor.matmul(G[:, u % 2, 0:HD], pT[:, u % 4, k * P:(k + 1) * P],
                                              vs(h, k), start=(k == 0), stop=(k == nks[t] // P - 1))
                    mm.then_inc(a_pv, 1)

                g, every = MOD_IN[name], n // MODG
                rows_in = mod_rows_done(name)
                if rows_in > 1:
                    pe.wait_ge(mod_row, rows_in - 1)
                for u in range(n + 4):
                    if u < n:
                        scores(u)
                    if 3 <= u < n + 3:
                        turn_probs(u - 3)
                    if u >= 4:
                        values(u - 4)
                    if u < n and u % every == every - 1:
                        mod_slot(g, u // every, 3)
                return [(a_o, u0 + n), (mod_row, rows_in)]

            def broadcast_row(k, waits, bank=0):
                free(waits)
                pe.wait_ge(diag_ok, k + 1)
                for c in range(KC):
                    mm = nc.tensor.matmul(T[:, bank + c // 4, (c % 4) * P:(c % 4 + 1) * P], ones[:, :],
                                          (diag_last if k == 5 else diag)[:, c, :],
                                          start=True, stop=True)
                mm.then_inc(bc_mm, 1)
                return [(bc_ok, k + 1)]

            def half64(h):
                return slice((h % 2) * HD, (h % 2 + 1) * HD)

            pe.wait_ge(first_in, 16 * 2)
            nc.tensor.transpose(T[:, 0, 0:8], svr[0:8, 0, :], ident[0:8, 0:8]).then_inc(sv_turned, 1)
            busy = norm_turn("h1", "n1", Y, [(sv_done, 1)])
            free(busy)
            in_block(0)
            e0 = prod["in_a"][1]
            pe.wait_ge(sv_in, 16 * SV_DMAS)
            for i, n in enumerate((P, 36, 96)):
                tr = nc.tensor.transpose(T[:, 0, i * P:i * P + n], svr[0:n, i, :], ident[0:n, 0:n])
            tr.then_inc(sv_turned, 1)
            in_block(1)
            free([(sv_done, 2)])
            busy = turn_stage("xr", lambda i, t: proj[:, t, C_XR + i * P:C_XR + (i + 1) * P], busy,
                              [(ev_act, e0 + 2), (ev_dve, e0 + 2)])
            with pe.Fori(1, 4) as it:
                for b in range(2):
                    in_block(b, it)
            free(busy)
            for c in range(8):
                pe.wait_ge(rnn_xc, c + 1)
                if c == 0:
                    pe.wait_ge(bd_in, 64)
                if c >= 4:
                    pe.wait_ge(rnn_sig, c - 3)
                for i, m in enumerate((bda, bdx)):
                    mm = nc.tensor.matmul(T[:, c % 4, i * S:(i + 1) * S], m[:, c, :], xc[:, c, :], start=True, stop=True)
                mm.then_inc(rnn_gate, 1)
            busy = [(rnn_sig, 8)]
            s0, e0 = prod["in_tail"]
            pair_free(e0)
            for h in range(2):
                rows(s0 + h, h, e0, HT, C_GA - C_IK)
            product("in_b1", HT, D)
            busy = turn_stage("q", lambda i, t: proj[:, t, C_Q + i * P:C_Q + (i + 1) * P], busy, [(qk_ready, 1)])
            busy = turn_stage("kiq", lambda i, t: kd1[:, t, i, :] if i < 4 else
                              proj[:, t, C_IQ + (i - 4) * P:C_IQ + (i - 3) * P], busy)
            busy = turn_stage("ik", lambda i, t: ikd[:, t, :], busy)
            free(busy)
            for u in range(16):
                h, t = u // 2, u % 2
                if u >= 4:
                    pe.wait_ge(idx_relu, u - 3)
                nc.tensor.matmul(T[:, u % 4, 0:P * (t + 1)], kT[half64(h), h // 2, S + t * P:S + (t + 1) * P],
                                 ikT[half64(h), 0:P * (t + 1)], start=True, stop=True).then_inc(idx_mm, 1)
            product("in_b2", HT, D)
            busy = [(idx_relu, 16)]
            busy = turn_stage("gr", lambda i, t: proj[:, t, C_GR + i * P:C_GR + (i + 1) * P], busy, [(gelu_ok, 1)])
            busy = attention("a1", lambda h, t: qT[half64(h), h // 2, t * P:(t + 1) * P],
                             lambda h, t: kT[half64(h), h // 4, 0:P * (t + 1)],
                             lambda h, k: proj[:, k, C_V + (h // 4) * HD:C_V + (h // 4 + 1) * HD], busy, prod["y_a"][1])
            free(busy)
            pe.wait_ge(rnn_y, 1)
            product("y_a", R3, D)
            busy = turn_stage("o1", lambda i, t: Z[:, t, i * P:(i + 1) * P], busy)
            free(busy)
            product("y_b", HT, D)
            busy = mod_turn(0, busy)
            busy = turn_stage("mrg", lambda i, t: Y[:, t, i * P:(i + 1) * P], busy, [(mrg_ok, 1)])
            pe.wait_ge(turn_act, turn["mrg"][1] + 4)
            pe.wait_ge(turn_dve, turn["mrg"][2] + 4)
            product("w_o", qT, D)
            mod_group(1)
            busy = norm_turn("hf1", "nf1", Y, busy)
            ffn("1", busy, after_block0=lambda: mod_turn(1, []))
            busy = norm_turn("h_c0", "n_c0", Z, [])
            free(busy)
            product("qkv_c0", HC, N_EVEN)
            busy = broadcast_row(0, busy)
            busy = norm_turn("h_x0", "n_x0", Y, busy)
            busy = broadcast_row(1, busy)
            product("qkv_x0", HT, N_EVEN)
            busy = turn_stage("q_xc", lambda i, t: (px, pc)[i // 4][:, t, (i % 4) * P:(i % 4 + 1) * P], busy, [(qk_ready, 2)])
            busy = turn_stage("k_xc", lambda i, t: kd[:, 2 * (i // 2) + t, i % 2, :], busy)
            free(busy)
            vcol = 640
            pe.wait_ge(turn_act, turn["k_xc"][1] + 2)
            pe.wait_ge(turn_dve, turn["k_xc"][2] + 2)
            busy = attention("ax", lambda h, t: qT[half64(h), h // 2, t * P:(t + 1) * P],
                             lambda h, t: kT[half64(h), h // 4, :],
                             lambda h, k: (px, pc)[k // 2][:, k % 2, vcol + (h // 4) * HD:vcol + (h // 4 + 1) * HD], busy,
                             prod["out_x0"][1])
            busy = attention("ac", lambda h, t: qT[half64(h), 4 + h // 2, t * P:(t + 1) * P],
                             lambda h, t: kT[half64(h), h // 4, S:2 * S],
                             lambda h, k: pc[:, k, vcol + (h // 4) * HD:vcol + (h // 4 + 1) * HD], busy, prod["out_x0"][1])
            free(busy)
            pe.wait_ge(pool_in, 16 * 2)
            for i, src in enumerate((px, pc)):
                if i == 1:
                    pe.wait_ge(pool_d, 2)
                for g in range(4):
                    for k in range(NT):
                        mm = nc.tensor.matmul(T[:, g // 2, (g % 2) * S:(g % 2 + 1) * S], src[:, k, 768 + g * P:768 + (g + 1) * P],
                                              poolm[:, g, k, :], start=(k == 0), stop=(k == 1))
                mm.then_inc(pool_mm, 1)
                pe.wait_ge(pool_d, 2 * i + 2)
                if i == 1:
                    pe.wait_ge(pool_ok, 4)
                for g in range(4):
                    mm = nc.tensor.matmul(T[:, 2 + g // 2, (g % 2) * S:(g % 2 + 1) * S], wpool[:, g, :], qT[:, 4 * i + g, :],
                                          start=True, stop=True)
                mm.then_inc(pool_y, 1)
            busy = [(pool_ok, 8)]
            busy = turn_stage("o_x", lambda i, t: Z[:, t, i * P:(i + 1) * P], busy)
            busy = turn_stage("o_c", lambda i, t: Z[:, t, NB + i * P:NB + (i + 1) * P], busy)
            mod_turn(2, busy)
            busy = mod_turn(3, [])
            product("out_x0", HT, D)
            busy = broadcast_row(2, busy)
            product("out_c0", HC, D, 0, 1)
            busy = broadcast_row(3, busy)
            busy = norm_turn("hf_x0", "nf_x0", Y, busy)
            product("out_c0", HC, D, 1)
            ffn("_x0", busy, in_down=lambda: norm_turn("hf_c0", "nf_c0", Z, [(hidT_ok, FB * (ffn_i["_x0"] + 1))]))
            ffn("_c0", [(turn_act, turn["hf_c0"][1] + 4), (turn_dve, turn["hf_c0"][2] + 4)])
            busy = norm_turn("h_x1", "n_x1", Y, [])
            free(busy)
            product("qkv_x1", HT, N_ODD)
            busy = norm_turn("h_c1", "n_c1", Z, busy)
            free(busy)
            product("kv_c1", HC, NB)
            busy = turn_stage("q_1", lambda i, t: px[:, t, i * P:(i + 1) * P], busy, [(qk_ready, 3)])
            busy = turn_stage("k_1", lambda i, t: kd[:, 2 * (i // 4) + t, i % 4, :], busy)
            vcol1 = 1280
            busy = attention("a1x", lambda h, t: qT[half64(h), h // 2, t * P:(t + 1) * P],
                             lambda h, t: kT[half64(h), h // 4, :],
                             lambda h, k: (px, pc)[k // 2][:, k % 2, vcol1 + (h // 4) * HD:vcol1 + (h // 4 + 1) * HD], busy,
                             prod["out_x1"][1])
            busy = turn_stage("o_1", lambda i, t: Z[:, t, i * P:(i + 1) * P], busy)
            busy = mod_turn(4, busy)
            product("out_x1", HT, D)
            busy = broadcast_row(4, busy)
            mod_group(5)
            busy = mod_turn(5, busy)
            busy = norm_turn("hf_x1", "nf_x1", Y, busy)
            ffn("_x1", busy, after_block0=lambda: broadcast_row(5, [], 2))

        @block.scalar
        def _(act):
            step = Steps(act, astep)

            act.dma_start(ident[:, :], consts["ident"]).then_inc(first_in, 16)
            act.dma_start(svr[0:8, 0, :], w["norm_mix_pre"].rearrange("a (r n) -> (a r) n", n=P)).then_inc(first_in, 16)

            def square_sums(name, src, junk):
                k = sums[name]
                if k:
                    act.wait_ge(ss_done, k)
                nc.scalar.activation(junk[:, 0, :], src[:, 0, :], ACT.Square, accum_out=ssb[:, k % 2, 0:1]).then_inc(ss_done, 1)

            def norm_apply(name, src, dst):
                k = sums[name]
                act.wait_ge(rs_done, k + 1)
                nc.scalar.activation(dst[:, 1, :], src[:, 1, :], ACT.Copy, scale=rs[:, k % 2, 1:2]).then_inc(xn_act, 1)

            def turn_evict(name, dst, scale=None, bias=None):
                c0, n = turn[name][0], turn_n[name]
                for i in [i for i in range(n) if i // 2 % 2 == 0]:
                    act.wait_ge(turned, c0 + min(i // 2 * 2 + 2, n))
                    src = T[:, i // 2, (i % 2) * S:(i % 2 + 1) * S]
                    if scale is None:
                        ins = nc.scalar.activation(dst(i), src, ACT.Copy)
                    elif bias is None:
                        ins = nc.scalar.activation(dst(i), src, ACT.Copy, scale=scale(i))
                    else:
                        ins = nc.scalar.activation(dst(i), src, ACT.Identity, scale=scale(i), bias=bias(i))
                    ins.then_inc(turn_act, 1)

            def product_evict(name, dst, total, first=0, last=None):
                s0, e0 = reads[name], prod[name][1]
                for b in range(first, last or -(-total // NB)):
                    n = min(NB, total - b * NB)
                    act.wait_ge(slot_read, s0 + 2 * b + 2)
                    nc.scalar.activation(dst[:, 0, b * NB:b * NB + n], G[:, 2 * ((e0 + b) % 2), 0:n], ACT.Copy).then_inc(ev_act, 1)

            def in_block(b, it=None, last=False):
                more = 0 if it is None else it
                if not last:
                    w_high("in_a", 2 * b + 2, it)
                act.wait_ge(split_mm, more * 4 + (2 * b + 2))
                c = slice(b * NB, (b + 1) * NB) if it is None else bass.ds(it * (2 * NB) + b * NB, NB)
                nc.scalar.activation(proj[:, 0, c], G[:, 2 * (b % 2), :], ACT.Copy).then_inc(ev_act, 1)
                if not last:
                    w_high("in_a", 2 * b + 3, it)

            def mod_evict(g):
                s0, e0 = reads[f"mod{g}"], prod[f"mod{g}"][1]
                act.wait_ge(slot_read, s0 + MODG)
                if g >= 1:
                    act.wait_ge(mod_turned, g)
                nc.scalar.activation(modrow[:, :], G[:, 2 * (e0 % 2), :], ACT.Copy).then_inc(ev_act, 1)

            def w_high(name, i, it=None):
                s, n = (i, i) if name == "in_a" else (prod["up" + name][0] + i, F0[ffn_i[name]] + i)
                more = 0 if it is None else it
                act.wait_ge(w_landed[s % RING], more * 32 + 32 * (s // RING + 1))
                if n >= 2:
                    act.wait_ge(split_mm, more * 4 + (n - 1))
                nc.scalar.activation(split_h[n % 2], ring1[:, s % RING, :], ACT.Copy).then_inc(w_hi, 1)

            def x_split(name, turned_as, scale, bias=None):
                c0, a0, d0 = turn[turned_as]
                whole, high = (HT, x1_h) if name == "in_a" else (HF, xT_h)
                for h in range(2):
                    for i in (4 * h, 4 * h + 1):
                        act.wait_ge(turned, c0 + 4 * h + 2)
                        src = T[:, i // 2, (i % 2) * S:(i % 2 + 1) * S]
                        if bias is None:
                            ins = nc.scalar.activation(whole[:, i, :], src, ACT.Copy, scale=scale(i))
                        else:
                            ins = nc.scalar.activation(whole[:, i, :], src, ACT.Identity, scale=scale(i), bias=bias(i))
                        ins.then_inc(turn_act, 1)
                    act.wait_ge(turn_act, a0 + 2 * h + 2)
                    act.wait_ge(turn_dve, d0 + 2 * h + 2)
                    nc.scalar.activation(high[:, 4 * h:4 * h + 4, :], whole[:, 4 * h:4 * h + 4, :], ACT.Copy).then_inc(xT_hi, 1)

            def up_block(name, j, it=None):
                f, e0, more = ffn_i[name], prod["up" + name][1], 0 if it is None else it
                w_high(name, 2 * j + 2, it)
                act.wait_ge(split_mm, more * 4 + (F0[f] + 2 * j + 2))
                act.wait_ge(ev_dve, more * 2 + (e0 + j - 1))
                p = (e0 + j) % 2
                nc.scalar.activation(gate[:, j % 2, :, :], G[:, 2 * p:2 * p + 2, 0:S], ACT.Silu).then_inc(ev_act, 1)
                w_high(name, 2 * j + 3, it)
                if j:
                    hid_high(name, j - 1, it)

            def hid_high(name, j, it=None):
                act.wait_ge(hid_turned, (0 if it is None else it * 2) + (FB * ffn_i[name] + j + 1))
                dst = hidT_h[:, 2 * j:2 * j + 2, :] if it is None else hidT_h[:, bass.ds(it * 4 + 2 * j, 2), :]
                nc.scalar.activation(dst, T[:, j % 2, :].rearrange("p (c n) -> p c n", c=2), ACT.Copy).then_inc(hidT_hi, 1)

            def up_loop(name, first):
                with act.Fori(first, FB // 2) as it:
                    up_block(name, 1, it)
                    up_block(name, 2, it)
                hid_high(name, FB - 1)

            def down_weights(name, first=2 * FB + 2, last=NF):
                for i in range(first, last):
                    w_high(name, i)

            def down_done(name):
                act.wait_ge(split_mm, F0[ffn_i[name] + 1])

            def down_evict(name, dst):
                e0 = prod["down" + name][1]
                for h in range(2):
                    nc.scalar.activation(dst[:, 0, h * NB:(h + 1) * NB], G[:, 2 * ((e0 + h) % 2), :], ACT.Copy).then_inc(ev_act, 1)

            def attention(name, last_o=False):
                heads, nks = [a[1:] for a in ATTN if a[0] == name][0]
                u0 = att0[name][0]
                n = 2 * heads
                extra = 1 if name == "a1x" else 0

                g = MOD_IN[name]
                for u in range(n + 3):
                    if u == n:
                        act.wait_ge(slot_read, reads[f"mod{g}"] + MODG)
                        if g in (2, 4):
                            act.wait_ge(mod_turned, g)
                        nc.scalar.activation(mod_rows(g), G[:, 3, :], ACT.Copy).then_inc(mod_row, 1)
                    if u >= 3:
                        v = u - 3
                        t = (v // 2) % 2
                        act.wait_ge(a_turned, u0 + v + 1)
                        if v >= 4:
                            act.wait_ge(a_pv, u0 + v - 3)
                        nc.scalar.activation(pT[:, v % 4, 0:nks[t]], T[:, 2 + v % 2, 0:nks[t]], ACT.Copy).then_inc(a_pT, 1)
                    if u < n:
                        t = (u // 2) % 2
                        act.wait_ge(a_min, u0 + u + 1)
                        if u >= 4:
                            act.wait_ge(a_o, u0 + u - 3)
                        wv = work[:, u % 4, 0:nks[t] + extra]
                        nc.scalar.activation(wv, wv, ACT.Exp, scale=-1.0, bias=amin[:, u % 4:u % 4 + 1],
                                             accum_out=asum[:, u % 4:u % 4 + 1]).then_inc(a_exp, 1)

            def out_gate(name, col):
                act.wait_ge(ev_act, prod[name][1] + 2)
                act.wait_ge(ev_dve, prod[name][1] + 2)
                nc.scalar.activation(proj[:, :, col:col + D], proj[:, :, col:col + D], ACT.Sigmoid).then_inc(sg_ready, 1)

            act.wait_ge(x_in, 16)
            square_sums("n1", x, Y)
            norm_apply("n1", x, Y)
            act.wait_ge(sv_done, 1)
            w_high("in_a", 0)
            x_split("in_a", "h1", lambda i: cols["norm_mix_pre"][:, i:i + 1])
            w_high("in_a", 1)
            for b in range(2):
                in_block(b)
            turn_evict("xr", lambda i: xpad[:, i, 3:259])
            act.wait_ge(sv_done, 2)
            for i, name in enumerate(("c_2", "c_ctx_2")):
                ins = nc.scalar.activation(scT[:, :, i], cols[name], ACT.Silu)
            ins.then_inc(c_silu, 1)
            act.wait_ge(softp_z, 1)
            nc.scalar.activation(c8[:, 1, :], c8[:, 0, :], ACT.Exp, scale=-1.0).then_inc(softp_e, 1)
            with act.Fori(1, 3) as it:
                for b in range(2):
                    in_block(b, it)
            in_block(6)
            in_block(7, last=True)
            act.wait_ge(softp, 1)
            for c in range(8):
                act.wait_ge(rnn_gate, c + 1)
                nc.scalar.activation(R1[:, c, :], T[:, c % 4, 0:S], ACT.Sigmoid, bias=cols["rg_b_a"][:, c:c + 1])
                nc.scalar.activation(R2[:, c, :], T[:, c % 4, S:2 * S], ACT.Sigmoid, bias=cols["rg_b_x"][:, c:c + 1]).then_inc(rnn_sig, 1)
            act.wait_ge(gelu_in, 1)
            nc.scalar.activation(Y[:, :, :], Y[:, :, :], ACT.Tanh, scale=math.sqrt(2.0 / math.pi)).then_inc(gelu_t, 1)
            act.wait_ge(rnn_sig, 8)
            for c in range(8):
                step(nc.scalar.activation(R3[:, c, :], R1[:, c, :], ACT.Tanh, scale=c8[:, 8, c:c + 1]))
            step.wait()
            for c in range(8):
                ins = nc.scalar.activation(R1[:, c, :], R1[:, c, :], ACT.Exp, scale=c8[:, 9, c:c + 1])
            ins.then_inc(rnn_ta, 1)
            s0, e0 = reads["in_tail"], prod["in_tail"][1]
            act.wait_ge(slot_read, s0 + 2)
            nc.scalar.activation(proj[:, 0, C_IK:C_GA], G[:, 2 * (e0 % 2), 0:C_GA - C_IK], ACT.Copy).then_inc(ev_act, 1)
            product_evict("in_b1", proj[:, :, C_GA:C_GB], D)
            turn_evict("q", lambda i: qT[:, i, :])
            turn_evict("kiq", lambda i: kT[:, i, 0:S] if i < 4 else kT[:, i - 4, S:2 * S])
            turn_evict("ik", lambda i: ikT[:, :])
            act.wait_ge(rnn_sq, 1)
            nc.scalar.activation(R3[:, :, :], R3[:, :, :], ACT.Sqrt).then_inc(rnn_root, 1)
            for u in range(16):
                nk = P * (u % 2 + 1)
                act.wait_ge(idx_mm, u + 1)
                if u >= 4:
                    act.wait_ge(idx_acc, u - 3)
                nc.scalar.activation(yf[:, (u % 4) * S:(u % 4) * S + nk], T[:, u % 4, 0:nk], ACT.Relu).then_inc(idx_relu, 1)
            out_gate("in_b1", C_GA)
            product_evict("in_b2", proj[:, :, C_GB:N_IN], D)
            act.wait_ge(rnn_scan, 1)
            turn_evict("gr", lambda i: R2[:, i, :])
            attention("a1")
            out_gate("in_b2", C_GB)
            product_evict("y_a", Y, D)
            turn_evict("o1", lambda i: HT[:, i, :])
            product_evict("y_b", proj[:, :, C_Q:C_Q + D], D)
            turn_evict("mrg", lambda i: qT[:, i, :])
            act.wait_ge(late_in, 16 * 5)
            square_sums("n_c0", cx, Z)
            norm_apply("n_c0", cx, Z)
            product_evict("w_o", Y, D)
            act.wait_ge(ev_act, prod["w_o"][1] + 2)
            square_sums("p1", Y, junk)
            act.wait_ge(x_new, 1)
            square_sums("nf1", x, Y)
            norm_apply("nf1", x, Y)
            mod_evict(1)
            w_high("1", 0)
            x_split("1", "hf1", lambda i: cols["norm_ffn_pre"][:, i:i + 1])
            w_high("1", 1)
            up_block("1", 0)
            up_loop("1", 0)
            down_weights("1")
            down_done("1")
            down_evict("1", Y)
            act.wait_ge(ev_act, prod["down1"][1] + 2)
            square_sums("pf1", Y, junk)
            act.wait_ge(hs_ok, 1)
            turn_evict("h_c0", lambda i: HC[:, i, :], lambda i: hscale[:, 0, 0, 1, i:i + 1], lambda i: modcol[:, 0, i, 1:2])
            act.wait_ge(x_new, 3)
            square_sums("n_x0", x, Y)
            norm_apply("n_x0", x, Y)
            for name, c0, c1 in (("we_q_gain_2", 0, 512), ("we_k_gain_2", 512, 640)):
                n = (c1 - c0) // HD
                act.dma_start(qkgain[:, c0:c1].rearrange("p (h n) -> p h n", h=n),
                              w[name][0:1, :].unsqueeze(1).to_broadcast((P, n, HD))).then_inc(gain_in, 16)
            act.dma_start(poolm[:, :, :, :], consts["pool"]).then_inc(pool_in, 16)
            act.dma_start(wpool[:, :, :], w["we_pool_2"][0].rearrange("g c d -> c g d")).then_inc(pool_in, 16)
            product_evict("qkv_c0", pc, N_EVEN)
            turn_evict("h_x0", lambda i: HT[:, i, :], lambda i: hscale[:, 0, 0, 0, i:i + 1], lambda i: modcol[:, 0, i, 0:1])
            product_evict("qkv_x0", px, N_EVEN)
            turn_evict("q_xc", lambda i: qT[:, i, :])
            turn_evict("k_xc", lambda i: kT[:, i % 2, (i // 2) * S:(i // 2 + 1) * S])
            attention("ax")
            attention("ac")
            for i, dst in enumerate((HT, HC)):
                act.wait_ge(pool_mm, i + 1)
                nc.scalar.activation(qT[:, 4 * i:4 * i + 2, :], T[:, 0, :].rearrange("p (g n) -> p g n", g=2), ACT.Copy).then_inc(pool_d, 1)
                act.wait_ge(pool_y, i + 1)
                for g in range(2):
                    nc.scalar.activation(dst[:, 4 + g, :], T[:, 2, g * S:(g + 1) * S], ACT.Copy,
                                         scale=cols["we_pool_scale_2"][:, g:g + 1]).then_inc(pool_ok, 1)
            turn_evict("o_x", lambda i: HT[:, i, :])
            turn_evict("o_c", lambda i: HC[:, i, :])
            product_evict("out_x0", Y, D)
            act.wait_ge(ev_act, prod["out_x0"][1] + 2)
            square_sums("p_x0", Y, junk)
            act.wait_ge(x_new, 5)
            square_sums("nf_x0", x, Y)
            norm_apply("nf_x0", x, Y)
            act.wait_ge(turn_act, turn["o_c"][1] + 2)
            act.wait_ge(turn_dve, turn["o_c"][2] + 2)
            product_evict("out_c0", Z, D, 0, 1)
            w_high("_x0", 0)
            act.wait_ge(hs_ok, 2)
            x_split("_x0", "hf_x0", lambda i: hscale[:, 0, 1, 0, i:i + 1], lambda i: modcol[:, 0, 24 + i, 0:1])
            product_evict("out_c0", Z, D, 1)
            w_high("_x0", 1)
            up_block("_x0", 0)
            act.wait_ge(xT_ok, 2 * ffn_i["_x0"] + 4)
            square_sums("p_c0", Z, junk)
            for j in range(1, 4):
                up_block("_x0", j)
            act.wait_ge(x_new, 7)
            square_sums("nf_c0", cx, Z)
            up_block("_x0", 4)
            norm_apply("nf_c0", cx, Z)
            up_loop("_x0", 2)
            down_weights("_x0", last=2 * FB + 6)
            act.wait_ge(hs_ok, 2)
            x_split("_c0", "hf_c0", lambda i: hscale[:, 0, 1, 1, i:i + 1], lambda i: modcol[:, 0, 24 + i, 1:2])
            down_weights("_x0", 2 * FB + 6)
            w_high("_c0", 0)
            down_done("_x0")
            down_evict("_x0", Y)
            w_high("_c0", 1)
            up_block("_c0", 0)
            act.wait_ge(xT_ok, 2 * ffn_i["_c0"] + 4)
            square_sums("pf_x0", Y, junk)
            for j in range(1, 4):
                up_block("_c0", j)
            act.wait_ge(x_new, 9)
            square_sums("n_x1", x, Y)
            up_block("_c0", 4)
            norm_apply("n_x1", x, Y)
            up_loop("_c0", 2)
            down_weights("_c0")
            down_done("_c0")
            down_evict("_c0", Z)
            act.wait_ge(hs_ok, 3)
            turn_evict("h_x1", lambda i: HT[:, i, :], lambda i: hscale[:, 1, 0, 0, i:i + 1], lambda i: modcol[:, 1, i, 0:1])
            act.wait_ge(ev_act, prod["down_c0"][1] + 2)
            square_sums("pf_c0", Z, junk)
            act.dma_start(band[:, :, :], consts["band"]).then_inc(band_in, 16)
            act.wait_ge(x_new, 11)
            square_sums("n_c1", cx, Z)
            norm_apply("n_c1", cx, Z)
            product_evict("qkv_x1", px, N_ODD)
            turn_evict("h_c1", lambda i: HC[:, i, :], lambda i: hscale[:, 1, 0, 1, i:i + 1], lambda i: modcol[:, 1, i, 1:2])
            product_evict("kv_c1", pc[:, :, D:N_ODD], NB)
            turn_evict("q_1", lambda i: qT[:, i, :])
            turn_evict("k_1", lambda i: kT[:, i % 4, (i // 4) * S:(i // 4 + 1) * S])
            attention("a1x")
            turn_evict("o_1", lambda i: HT[:, i, :])
            product_evict("out_x1", Y, D)
            act.wait_ge(ev_act, prod["out_x1"][1] + 2)
            square_sums("p_x1", Y, junk)
            act.wait_ge(x_new, 13)
            square_sums("nf_x1", x, Y)
            norm_apply("nf_x1", x, Y)
            mod_evict(5)
            act.wait_ge(hs_ok, 4)
            w_high("_x1", 0)
            x_split("_x1", "hf_x1", lambda i: hscale[:, 1, 1, 0, i:i + 1], lambda i: modcol[:, 1, 24 + i, 0:1])
            w_high("_x1", 1)
            up_block("_x1", 0)
            up_loop("_x1", 0)
            down_weights("_x1")
            down_done("_x1")
            down_evict("_x1", Y)
            act.wait_ge(ev_act, prod["down_x1"][1] + 2)
            square_sums("pf_x1", Y, junk)

        @block.gpsimd
        def _(pool):
            step = Steps(pool, pstep)
            nc.gpsimd.memset(scT[:, :, :], 0.0)
            nc.gpsimd.memset(ones[:, :], 1.0)
            nc.gpsimd.memset(bd[:, :], 0.0)
            nc.gpsimd.memset(xpad[:, :, 0:3], 0.0).then_inc(bd_zero, 1)
            half = slice(0, 1024)

            def w_low(first, n, i, it=None):
                pool.wait_ge(w_hi, (0 if it is None else it * 4) + (n + i + 1))
                b = (n + i) % 2
                nc.gpsimd.tensor_tensor(split_l[b][:, half], ring1[:, (first + i) % RING, half],
                                        split_h[b][:, half].bitcast(F32), ALU.subtract).then_inc(w_lo_pool, 1)

            with pool.Fori(0, NA // 4) as it:
                for i in range(4):
                    w_low(0, 0, i, it)
            gr = proj[:, :, C_GR:C_GR + D]
            e0 = prod["in_a"][1]
            pool.wait_ge(ev_act, e0 + 4)
            pool.wait_ge(ev_dve, e0 + 4)
            step(nc.gpsimd.tensor_tensor(Y[:, :, :], gr, gr, ALU.mult))
            step.wait()
            step(nc.gpsimd.tensor_scalar(Y[:, :, :], Y[:, :, :], 0.044715, 1.0, ALU.mult, ALU.add))
            step.wait()
            nc.gpsimd.tensor_tensor(Y[:, :, :], Y[:, :, :], gr, ALU.mult).then_inc(gelu_in, 1)
            pool.wait_ge(gelu_t, 1)
            step(nc.gpsimd.tensor_scalar(Y[:, :, :], Y[:, :, :], 1.0, 1.0, ALU.mult, ALU.add))
            step.wait()
            nc.gpsimd.tensor_tensor(gr, Y[:, :, :], gr, ALU.mult).then_inc(gelu_ok, 1)
            pool.wait_ge(rnn_sig, 8)
            step(nc.gpsimd.tensor_tensor(R2[:, :, :], R2[:, :, :], xc[:, :, :], ALU.mult))
            pool.wait_ge(rnn_ta, 1)
            step.wait()
            step(nc.gpsimd.tensor_tensor(xc[:, :, :], R1[:, :, :], R1[:, :, :], ALU.mult))
            step.wait()
            step(nc.gpsimd.tensor_scalar(xc[:, :, :], xc[:, :, :], 1.0, None, ALU.add))
            step.wait()
            step(nc.gpsimd.tensor_tensor(R3[:, :, :], R3[:, :, :], xc[:, :, :], ALU.mult))
            step.wait()
            nc.gpsimd.tensor_scalar(R3[:, :, :], R3[:, :, :], 1e-30, None, ALU.max).then_inc(rnn_sq, 1)
            pool.wait_ge(rnn_root, 1)
            nc.gpsimd.tensor_tensor(R2[:, :, :], R2[:, :, :], R3[:, :, :], ALU.mult).then_inc(rnn_u, 1)
            for f, name in enumerate(FFNS):
                s0 = prod["up" + name][0]
                w_low(s0, F0[f], 0)
                with pool.Fori(0, NF // 4) as it:
                    for i in range(1, 5):
                        w_low(s0, F0[f], i, it)

        @block.vector
        def _(dve):
            step = Steps(dve, dstep)
            V = nc.vector

            def rsqrt(dst, ss, n, count):
                v, i, y, a = [rq[:, j, 0:n] for j in range(4)]
                step.wait()
                step(V.tensor_scalar(v, ss, 1.0 / count, EPS, ALU.mult, ALU.add))
                step.wait()
                step(V.tensor_scalar(i.bitcast(I32), v.bitcast(I32), 1, None, ALU.logical_shift_right))
                step.wait()
                step(V.tensor_scalar(y.bitcast(I32), i.bitcast(I32), -1.0, float(0x5F3759DF), ALU.mult, ALU.add))
                for r in range(3):
                    step.wait()
                    step(V.tensor_tensor(a, y, y, ALU.mult))
                    step.wait()
                    step(V.scalar_tensor_tensor(a, a, -0.5, v, ALU.mult, ALU.mult))
                    step.wait()
                    if r < 2:
                        step(V.scalar_tensor_tensor(y, a, 1.5, y, ALU.add, ALU.mult))
                return V.scalar_tensor_tensor(dst, a, 1.5, y, ALU.add, ALU.mult)

            def inverse_rms(name, src, junk):
                k = sums[name]
                step.wait()
                step(V.tensor_tensor_reduce(junk[:, 1, :], src[:, 1, :], src[:, 1, :], 1.0, 0.0, ALU.mult, ALU.add,
                                            ssb[:, k % 2, 1:2]))
                dve.wait_ge(ss_done, k + 1)
                rsqrt(rs[:, k % 2, :], ssb[:, k % 2, :], 2, D).then_inc(rs_done, 1)
                dve.wait_ge(rs_done, k + 1)

            def norm(name, src, dst):
                inverse_rms(name, src, dst)
                norm_tile(name, src, dst)

            def norm_tile(name, src, dst):
                V.tensor_scalar(dst[:, 0, :], src[:, 0, :], rs[:, sums[name] % 2, 0:1], None, ALU.mult).then_inc(xn_dve, 1)

            def residual(name, y, row, dst):
                inverse_rms(name, y, junk)
                for t in range(NT):
                    residual_tile(name, y, row, dst, t)

            def residual_tile(name, y, row, dst, t):
                step(V.scalar_tensor_tensor(y[:, t, :], y[:, t, :], rs[:, sums[name] % 2, t:t + 1], row, ALU.mult, ALU.mult))
                step.wait()
                V.tensor_tensor(dst[:, t, :], dst[:, t, :], y[:, t, :], ALU.add).then_inc(x_new, 1)
                if t == NT - 1:
                    dve.wait_ge(x_new, NT * ([n for n in SUMS if n[0] == "p"].index(name) + 1))

            def turn_evict(name, dst, scale=None, bias=None):
                c0, n = turn[name][0], turn_n[name]
                for i in [i for i in range(n) if i // 2 % 2]:
                    dve.wait_ge(turned, c0 + i // 2 * 2 + 2)
                    src = T[:, i // 2, (i % 2) * S:(i % 2 + 1) * S]
                    if scale is None:
                        ins = V.tensor_copy(dst(i), src)
                    elif bias is None:
                        ins = V.tensor_scalar(dst(i), src, scale(i), None, ALU.mult)
                    else:
                        ins = V.tensor_scalar(dst(i), src, scale(i), bias(i), ALU.mult, ALU.add)
                    ins.then_inc(turn_dve, 1)

            def block_evict(name, b, dst, total):
                s0, e0 = reads[name], prod[name][1]
                n = min(NB, total - b * NB)
                dve.wait_ge(slot_read, s0 + 2 * b + 2)
                V.tensor_copy(dst[:, 1, b * NB:b * NB + n], G[:, 2 * ((e0 + b) % 2) + 1, 0:n]).then_inc(ev_dve, 1)

            def blocks_in(name, n):
                dve.wait_ge(ev_act, prod[name][1] + n)
                dve.wait_ge(ev_dve, prod[name][1] + n)

            def product_evict(name, dst, total, first=0, last=None):
                for b in range(first, last or -(-total // NB)):
                    block_evict(name, b, dst, total)

            def evicted(name):
                e = prod[name][1] + [p for p in PRODUCTS if p[0] == name][0][2]
                dve.wait_ge(ev_act, e)
                dve.wait_ge(ev_dve, e)

            def in_block(b, last=False):
                if not last:
                    w_low("in_a", 2 * b + 2)
                dve.wait_ge(split_mm, 2 * b + 2)
                V.tensor_copy(proj[:, 1, b * NB:(b + 1) * NB], G[:, 2 * (b % 2) + 1, :]).then_inc(ev_dve, 1)
                if not last:
                    w_low("in_a", 2 * b + 3)

            def mod_evict(g):
                V.engine_nop().then_inc(ev_dve, 1)

            def mod_columns(g):
                lyr, i0 = g // 3, (g % 3) * 16
                dve.wait_ge(mod_turned, g + 1)
                V.tensor_tensor(modcol[:, lyr, i0:i0 + 16, :].rearrange("p (j c) r -> p c j r", j=4),
                                T[:, 2 + g % 2, :].rearrange("p (c j r) -> p c j r", c=4, j=4)[:, :, :, 0:2],
                                cols["b_mod_2"][:, lyr * 48 + i0:lyr * 48 + i0 + 16].rearrange("p (j c) -> p c j", j=4)
                                .unsqueeze(3).to_broadcast((P, 4, 4, 2)), ALU.add).then_inc(mod_ok, 1)

            def mod_scale(lyr, f):
                pre = ("g_pre_mix_2", "g_pre_ffn_2")[f]
                dve.wait_ge(mod_ok, 3 * lyr + 1 + 2 * f)
                for r in range(2):
                    ins = V.scalar_tensor_tensor(hscale[:, lyr, f, r, :], modcol[:, lyr, 24 * f + 8:24 * f + 16, r], 1.0,
                                                 cols[pre][:, 8 * lyr:8 * lyr + 8], ALU.add, ALU.mult)
                ins.then_inc(hs_ok, 1)
                dve.wait_ge(hs_ok, 2 * lyr + f + 1)

            def mod_gate(lyr, f):
                post = ("g_post_mix_2", "g_post_ffn_2")[f]
                dve.wait_ge(mod_ok, 3 * lyr + 2 + f)
                for r in range(2):
                    step(V.tensor_tensor(gtg[:, lyr, f, r, :], modcol[:, lyr, 24 * f + 16:24 * f + 24, r],
                                         cols[post][:, 8 * lyr:8 * lyr + 8], ALU.mult))
                step.wait()

            def diagonal(k, col):
                if k >= 1:
                    dve.wait_ge(bc_mm, k)
                for c in range(KC):
                    ins = V.tensor_scalar((diag_last if k == 5 else diag)[:, c, :], ident[:, :], col[:, c:c + 1], None, ALU.mult)
                ins.then_inc(diag_ok, 1)

            def spread_row(k, dst, bank=0):
                dve.wait_ge(bc_mm, k + 1)
                V.tensor_copy(dst.rearrange("p (b n) -> p b n", b=2), T[:, bank:bank + 2, :]).then_inc(bc_ok, 1)
                dve.wait_ge(bc_ok, k + 1)

            def rope(first, second, cos, sin, shape, scratch):
                n = int(np.prod(shape))

                def tmp(i):
                    v = scratch[:, 2048 - (i + 1) * n:2048 - i * n]
                    if len(shape) == 2:
                        return v.rearrange("p (h d) -> p h d", h=shape[0])
                    return v.rearrange("p (h a d) -> p h a d", h=shape[0], a=shape[1])
                step.wait()
                step(V.tensor_tensor(tmp(0), first, cos, ALU.mult))
                step(V.tensor_tensor(tmp(1), second, sin, ALU.mult))
                step(V.tensor_tensor(tmp(2), first, sin, ALU.mult))
                step.wait()
                step(V.tensor_tensor(first, tmp(0), tmp(1), ALU.subtract))
                step.wait()
                step(V.tensor_tensor(tmp(0), second, cos, ALU.mult))
                step.wait()
                step(V.tensor_tensor(second, tmp(0), tmp(2), ALU.add))

            def rope_small(src, t, heads):
                v = src.rearrange("p (h d) -> p h d", h=heads)
                c, s = [rope1[:, t, i, :].unsqueeze(1).to_broadcast((P, heads, 8)) for i in range(2)]
                rope(v[:, :, 0:8], v[:, :, 8:16], c, s, (heads, 8), zf)

            def rope_axial(src, t, heads):
                v = src.rearrange("p (h a b d) -> p h a b d", h=heads, a=2, b=2)
                c, s = [rope2[:, t, i, :].rearrange("p (a d) -> p a d", a=2).unsqueeze(1).to_broadcast((P, heads, 2, 16))
                        for i in range(2)]
                rope(v[:, :, :, 0, :], v[:, :, :, 1, :], c, s, (heads, 2, 16), kT_flat)

            def double_keys(k0, src, groups, kd=kd):
                for b in range(2):
                    ins = V.tensor_copy(kd[:, k0:k0 + NT, 0:groups, b * HD:(b + 1) * HD],
                                        src.rearrange("p t (g d) -> p t g d", g=groups))
                    step(ins)

            def w_low(name, i, it=None):
                s, n = (i, i) if name == "in_a" else (prod["up" + name][0] + i, F0[ffn_i[name]] + i)
                half = slice(1024, 2048)
                dve.wait_ge(w_hi, (0 if it is None else it * 4) + (n + 1))
                V.tensor_tensor(split_l[n % 2][:, half], ring1[:, s % RING, half], split_h[n % 2][:, half].bitcast(F32),
                                ALU.subtract).then_inc(w_lo_dve, 1)

            def x_split(name, turned_as, scale, bias=None):
                f = -1 if name == "in_a" else ffn_i[name]
                whole, high, low = (HT, x1_h, x1_l) if name == "in_a" else (HF, xT_h, xT_l)
                c0 = turn[turned_as][0]
                for h in range(2):
                    for i in (4 * h + 2, 4 * h + 3):
                        dve.wait_ge(turned, c0 + 4 * h + 4)
                        src = T[:, i // 2, (i % 2) * S:(i % 2 + 1) * S]
                        if bias is None:
                            ins = V.tensor_scalar(whole[:, i, :], src, scale(i), None, ALU.mult)
                        else:
                            ins = V.tensor_scalar(whole[:, i, :], src, scale(i), bias(i), ALU.mult, ALU.add)
                        ins.then_inc(turn_dve, 1)
                    c = slice(4 * h, 4 * h + 4)
                    dve.wait_ge(xT_hi, 2 * (f + 1) + h + 1)
                    V.tensor_tensor(low[:, c, :], whole[:, c, :], high[:, c, :].bitcast(F32), ALU.subtract).then_inc(xT_ok, 1)

            def up_block(name, j, it=None):
                f, e0, more = ffn_i[name], prod["up" + name][1], 0 if it is None else it
                w_low(name, 2 * j + 2, it)
                dve.wait_ge(ev_act, more * 2 + (e0 + j + 1))
                if it is not None or j >= 2:
                    dve.wait_ge(hid_turned, more * 2 + (FB * f + j - 1))
                p = (e0 + j) % 2
                V.tensor_tensor(hid[:, j % 2, :, :], gate[:, j % 2, :, :], G[:, 2 * p:2 * p + 2, S:NB],
                                ALU.mult).then_inc(ev_dve, 1)
                w_low(name, 2 * j + 3, it)
                if j:
                    hid_low(name, j - 1, it)

            def hid_low(name, j, it=None):
                dve.wait_ge(hidT_hi, (0 if it is None else it * 2) + (FB * ffn_i[name] + j + 1))
                c = slice(2 * j, 2 * j + 2) if it is None else bass.ds(it * 4 + 2 * j, 2)
                V.tensor_tensor(hidT_l[:, c, :], T[:, j % 2, :].rearrange("p (c n) -> p c n", c=2),
                                hidT_h[:, c, :].bitcast(F32), ALU.subtract).then_inc(hidT_ok, 1)

            def up_loop(name, first):
                with dve.Fori(first, FB // 2) as it:
                    up_block(name, 1, it)
                    up_block(name, 2, it)
                hid_low(name, FB - 1)

            def down_weights(name, first=2 * FB + 2, last=NF):
                for i in range(first, last):
                    w_low(name, i)

            def down_evict(name, dst):
                e0 = prod["down" + name][1]
                dve.wait_ge(split_mm, F0[ffn_i[name] + 1])
                for h in range(2):
                    V.tensor_copy(dst[:, 1, h * NB:(h + 1) * NB], G[:, 2 * ((e0 + h) % 2) + 1, :]).then_inc(ev_dve, 1)

            def attention(name, mask, o_col):
                heads, nks = [a[1:] for a in ATTN if a[0] == name][0]
                u0 = att0[name][0]
                n = 2 * heads
                step.wait()
                for u in range(n + 4):
                    if u < n:
                        h, t = 2 * (u // 4) + u % 2, (u // 2) % 2
                        b = u % 4
                        dve.wait_ge(a_mm, u0 + u + 1)
                        if u >= 4:
                            dve.wait_ge(a_turned, u0 + u - 3)
                        src, dst, low = logit_bank(u)[:, 0:nks[t]], work[:, b, 0:nks[t]], amin[:, b:b + 1]
                        if mask is None:
                            ins = V.tensor_scalar(dst, src, -SCALE, None, ALU.mult, ALU.min, accum_out=low)
                        else:
                            ins = V.tensor_tensor_reduce(dst, src, mask[:, t, 0:nks[t]], -SCALE, 3e38, ALU.add, ALU.min, low)
                        if name == "a1x":
                            step(ins)
                            step(V.tensor_copy(work[:, b, nks[t]:nks[t] + 1], nsink[:, h:h + 1]))
                            step.wait(1)
                            ins = V.tensor_tensor(low, low, nsink[:, h:h + 1], ALU.min)
                        ins.then_inc(a_min, 1)
                    if u >= 4:
                        v = u - 4
                        h, t = 2 * (v // 4) + v % 2, (v // 2) % 2
                        dve.wait_ge(a_pv, u0 + v + 1)
                        step(V.reciprocal(arec[:, v % 4:v % 4 + 1], asum[:, v % 4:v % 4 + 1]))
                        step.wait()
                        V.tensor_scalar(Z[:, t, o_col + h * HD:o_col + (h + 1) * HD], G[:, v % 2, 0:HD],
                                        arec[:, v % 4:v % 4 + 1], None, ALU.mult).then_inc(a_o, 1)

            def qk_norm(src, c0, heads):
                n = NT * heads
                qk = src[:, :, c0:c0 + heads * HD].rearrange("p t (h d) -> p t h d", h=heads)
                qk2 = zf[:, 0:n * HD].rearrange("p (t h d) -> p t h d", t=NT, h=heads)
                step.wait()
                step(V.tensor_tensor(qk2, qk, qk, ALU.mult))
                step.wait()
                step(V.tensor_reduce(rq[:, 4, 0:n], qk2, AX.X, ALU.add))
                step(rsqrt(rq[:, 5, 0:n], rq[:, 4, 0:n], n, HD))
                step.wait()
                inv = rq[:, 5, 0:n].rearrange("p (t h) -> p t h", t=NT).unsqueeze(3).to_broadcast((P, NT, heads, HD))
                step(V.tensor_tensor(qk, qk, inv, ALU.mult))
                gain = qkgain[:, c0:c0 + heads * HD].rearrange("p (h d) -> p h d", h=heads)
                step.wait()
                step(V.tensor_tensor(qk, qk, gain.unsqueeze(1).to_broadcast((P, NT, heads, HD)), ALU.mult))

            dve.wait_ge(sv_turned, 1)
            V.tensor_copy(svc[:, 0:8], T[:, 0, 0:8]).then_inc(sv_done, 1)
            dve.wait_ge(x_in, 16)
            norm("n1", x, Y)
            dve.wait_ge(sv_done, 1)
            w_low("in_a", 0)
            x_split("in_a", "h1", lambda i: cols["norm_mix_pre"][:, i:i + 1])
            w_low("in_a", 1)
            in_block(0)
            dve.wait_ge(sv_turned, 2)
            step(V.tensor_copy(svc[:, 8:164], T[:, 0, 8:164]))
            step.wait()
            V.tensor_copy(svc[:, 164:260], T[:, 0, 2 * P:2 * P + 96]).then_inc(sv_done, 1)
            dve.wait_ge(sv_done, 2)
            in_block(1)
            turn_evict("xr", lambda i: xpad[:, i, 3:259])
            lam = cols["rg_lambda"]
            V.scalar_tensor_tensor(c8[:, 0, :], lam, -1.0, lam, ALU.mult, ALU.max).then_inc(softp_z, 1)
            dve.wait_ge(turn_act, turn["xr"][1] + 4)
            dve.wait_ge(turn_dve, turn["xr"][2] + 4)
            dve.wait_ge(bd_zero, 1)
            cw, cb = cols["conv_w"], cols["conv_b"]
            for c in range(8):
                step(V.tensor_scalar(xc[:, c, :], xpad[:, c, 0:S], cw[:, c:c + 1], cb[:, c:c + 1], ALU.mult, ALU.add))
            for k in range(1, 4):
                in_block(k + 1)
                step.wait()
                for c in range(8):
                    ins = V.scalar_tensor_tensor(xc[:, c, :], xpad[:, c, k:k + S], cw[:, 8 * k + c:8 * k + c + 1],
                                                 xc[:, c, :], ALU.mult, ALU.add)
                    if k < 3:
                        step(ins)
                    else:
                        ins.then_inc(rnn_xc, 1)
            in_block(5)
            dve.wait_ge(softp_e, 1)
            step(V.tensor_scalar(c8[:, 2, :], c8[:, 1, :], 2.0, None, ALU.add))
            step.wait()
            step(V.reciprocal(c8[:, 3, :], c8[:, 2, :]))
            step.wait()
            step(V.tensor_tensor(c8[:, 4, :], c8[:, 1, :], c8[:, 3, :], ALU.mult))
            step.wait()
            step(V.tensor_tensor(c8[:, 5, :], c8[:, 4, :], c8[:, 4, :], ALU.mult))
            step.wait()
            step(V.tensor_scalar(c8[:, 6, :], c8[:, 5, :], 1.0 / 19, None, ALU.mult))
            for d in (17, 15, 13, 11, 9, 7, 5, 3):
                step.wait()
                step(V.scalar_tensor_tensor(c8[:, 6, :], c8[:, 6, :], 1.0 / d, c8[:, 5, :], ALU.add, ALU.mult))
            step.wait()
            step(V.scalar_tensor_tensor(c8[:, 6, :], c8[:, 6, :], 1.0, c8[:, 4, :], ALU.add, ALU.mult))
            step(V.tensor_scalar(c8[:, 7, :], lam, -8.0, 0.0, ALU.mult, ALU.max))
            step.wait()
            step(V.scalar_tensor_tensor(c8[:, 8, :], c8[:, 6, :], 16.0, c8[:, 7, :], ALU.mult, ALU.add))
            step.wait()
            V.tensor_scalar(c8[:, 9, :], c8[:, 8, :], -1.0, None, ALU.mult).then_inc(softp, 1)
            in_block(6)
            in_block(7, last=True)
            dve.wait_ge(small_in, 16 * 4)
            blocks_in("in_a", 8)
            for t in range(NT):
                rope_small(proj[:, t, C_Q:C_V], t, 20)
            s0, e0 = reads["in_tail"], prod["in_tail"][1]
            dve.wait_ge(slot_read, s0 + 2)
            V.tensor_copy(proj[:, 1, C_IK:C_GA], G[:, 2 * (e0 % 2) + 1, 0:C_GA - C_IK]).then_inc(ev_dve, 1)
            blocks_in("in_tail", 1)
            ik = proj[:, :, C_IK:C_IK + HD]
            step(V.tensor_reduce(rq[:, 4, 0:2], ik, AX.X, ALU.add))
            step.wait()
            step(V.tensor_scalar(rq[:, 4, 2:4], rq[:, 4, 0:2], 1.0 / HD, None, ALU.mult))
            step.wait()
            for t in range(NT):
                step(V.tensor_scalar(ik[:, t, :], ik[:, t, :], rq[:, 4, 2 + t:3 + t], None, ALU.subtract))
            step.wait()
            ik2 = zf[:, 1024:1024 + NT * HD].rearrange("p (t d) -> p t d", t=NT)
            step(V.tensor_tensor(ik2, ik, ik, ALU.mult))
            step.wait()
            step(V.tensor_reduce(rq[:, 4, 4:6], ik2, AX.X, ALU.add))
            step(rsqrt(rq[:, 4, 6:8], rq[:, 4, 4:6], 2, HD))
            step.wait()
            for t in range(NT):
                step(V.scalar_tensor_tensor(ik[:, t, :], ik[:, t, :], rq[:, 4, 6 + t:7 + t], lnrow[:, 0, :], ALU.mult, ALU.mult))
            step.wait()
            step(V.tensor_tensor(ik, ik, lnrow[:, 1, :].unsqueeze(1).to_broadcast((P, NT, HD)), ALU.add))
            step(V.tensor_scalar(iws[:, :, :], proj[:, :, C_IW:C_IW + 8], IDX_SCALE, None, ALU.mult))
            for t in range(NT):
                rope_small(proj[:, t, C_IQ:C_IW], t, 9)
            step.wait()
            double_keys(0, proj[:, :, C_K:C_V], 4, kd1)
            for b in range(2):
                step(V.tensor_copy(ikd[:, :, b * HD:(b + 1) * HD], ik))
            step.wait()
            V.engine_nop().then_inc(qk_ready, 1)
            product_evict("in_b1", proj[:, :, C_GA:C_GB], D)
            turn_evict("q", lambda i: qT[:, i, :])
            turn_evict("kiq", lambda i: kT[:, i, 0:S] if i < 4 else kT[:, i - 4, S:2 * S])

            def score(t, b):
                return zf[:, t * NB + b * S:t * NB + b * S + P * (t + 1)]

            for u in range(16):
                h, t = u // 2, u % 2
                nk = P * (t + 1)
                dve.wait_ge(idx_relu, u + 1)
                src = yf[:, (u % 4) * S:(u % 4) * S + nk]
                if h == 0:
                    ins = V.tensor_scalar(score(t, 0), src, iws[:, t, h:h + 1], None, ALU.mult)
                else:
                    dve.wait_ge(idx_acc, u - 1)
                    ins = V.scalar_tensor_tensor(score(t, 0), src, iws[:, t, h:h + 1], score(t, 0), ALU.mult, ALU.add)
                ins.then_inc(idx_acc, 1)
            dve.wait_ge(idx_acc, 16)
            for t in range(NT):
                late = score(t, 0)[:, t * P:(t + 1) * P]
                step(V.tensor_tensor(late, late, causal[:, :], ALU.add))
            dve.wait_ge(rnn_u, 1)
            for c in range(8):
                ins = V.tensor_tensor_scan(xc[:, c, :], R1[:, c, :], R2[:, c, :], 0.0, ALU.mult, ALU.add)
            ins.then_inc(rnn_scan, 1)
            dve.wait_ge(rnn_scan, 1)
            step.wait()
            for r in range(TOPK // 8):
                for t in range(NT):
                    if r:
                        step.wait(1)
                    step(V.max(top8[:, t, :], score(t, r % 2)))
                for t in range(NT):
                    step.wait(1)
                    step(V.match_replace(score(t, 1 - r % 2), top8[:, t, :], score(t, r % 2), TAKEN))
            step.wait()
            for t in range(NT):
                step(V.tensor_scalar(bias1[:, t, 0:P * (t + 1)], score(t, 0), -2e38, MASKED, ALU.is_gt, ALU.mult))
            step.wait()
            for t in range(NT):
                late = bias1[:, t, t * P:(t + 1) * P]
                step(V.tensor_tensor(late, late, causal[:, :], ALU.add))
            product_evict("in_b2", proj[:, :, C_GB:N_IN], D)
            for c in range(8):
                if c // 2 % 2:
                    dve.wait_ge(turned, turn["gr"][0] + c // 2 * 2 + 2)
                    V.scalar_tensor_tensor(R3[:, c, :], xc[:, c, :], 0.5, T[:, c // 2, (c % 2) * S:(c % 2 + 1) * S],
                                           ALU.mult, ALU.mult).then_inc(turn_dve, 1)
                else:
                    dve.wait_ge(turn_act, turn["gr"][1] + 2 * (c // 4) + c % 2 + 1)
                    step(V.scalar_tensor_tensor(R3[:, c, :], xc[:, c, :], 0.5, R2[:, c, :], ALU.mult, ALU.mult))
            step.wait()
            dve.wait_ge(turn_dve, turn["gr"][2] + 4)
            V.engine_nop().then_inc(rnn_y, 1)
            attention("a1", bias1, 0)
            dve.wait_ge(sg_ready, 1)
            yb = proj[:, :, C_Q:C_Q + D]

            def gated(name, dst, gcol):
                s0, e0 = reads[name], prod[name][1]
                for b in range(2):
                    c = slice(b * NB, (b + 1) * NB)
                    dve.wait_ge(slot_read, s0 + 2 * b + 2)
                    V.tensor_tensor(dst[:, 1, c], G[:, 2 * ((e0 + b) % 2) + 1, :],
                                    proj[:, 1, gcol + b * NB:gcol + (b + 1) * NB], ALU.mult).then_inc(ev_dve, 1)
                evicted(name)
                step(V.tensor_tensor(dst[:, 0, :], dst[:, 0, :], proj[:, 0, gcol:gcol + D], ALU.mult))

            gated("y_a", Y, C_GA)
            turn_evict("o1", lambda i: HT[:, i, :])
            dve.wait_ge(sg_ready, 2)
            gated("y_b", yb, C_GB)
            step.wait()
            V.tensor_tensor(Y[:, :, :], Y[:, :, :], yb, ALU.add).then_inc(mrg_ok, 1)
            mod_columns(0)
            turn_evict("mrg", lambda i: qT[:, i, :])
            mod_scale(0, 0)
            dve.wait_ge(late_in, 16 * 5)
            norm("n_c0", cx, Z)
            product_evict("w_o", Y, D)
            evicted("w_o")
            residual("p1", Y, bc[:, 0, :], x)
            norm("nf1", x, Y)
            mod_evict(1)
            w_low("1", 0)
            x_split("1", "hf1", lambda i: cols["norm_ffn_pre"][:, i:i + 1])
            w_low("1", 1)
            step(V.tensor_scalar(nsink[:, :], nsink[:, :], -1.0, None, ALU.mult))
            up_block("1", 0)
            mod_columns(1)
            up_block("1", 1)
            up_block("1", 2)
            up_loop("1", 1)
            down_weights("1")
            down_evict("1", Y)
            turn_evict("h_c0", lambda i: HC[:, i, :], lambda i: hscale[:, 0, 0, 1, i:i + 1], lambda i: modcol[:, 0, i, 1:2])
            evicted("down1")
            residual("pf1", Y, bc[:, 1, :], x)
            norm("n_x0", x, Y)
            mod_gate(0, 0)
            diagonal(0, gtg[:, 0, 0, 0, :])
            product_evict("qkv_c0", pc, N_EVEN)
            spread_row(0, bc[:, 0, :])
            diagonal(1, gtg[:, 0, 0, 1, :])
            turn_evict("h_x0", lambda i: HT[:, i, :], lambda i: hscale[:, 0, 0, 0, i:i + 1], lambda i: modcol[:, 0, i, 0:1])
            spread_row(1, bc[:, 1, :])
            evicted("qkv_c0")
            dve.wait_ge(gain_in, 16 * 2)
            qk_norm(pc, 0, 10)
            for b, c0, heads in ((0, 0, 8), (1, 512, 2)):
                block_evict("qkv_x0", b, px, N_EVEN)
                blocks_in("qkv_x0", b + 1)
                qk_norm(px, c0, heads)
                for t in range(NT):
                    rope_axial(px[:, t, c0:c0 + heads * HD], t, heads)
            block_evict("qkv_x0", 2, px, N_EVEN)
            step.wait()
            double_keys(0, px[:, :, 512:640], 2)
            double_keys(2, pc[:, :, 512:640], 2)
            step.wait()
            V.engine_nop().then_inc(qk_ready, 1)
            turn_evict("q_xc", lambda i: qT[:, i, :])
            turn_evict("k_xc", lambda i: kT[:, i % 2, (i // 2) * S:(i // 2 + 1) * S])
            attention("ax", None, 0)
            attention("ac", None, NB)
            for i, dst in enumerate((HT, HC)):
                dve.wait_ge(pool_mm, i + 1)
                V.tensor_copy(qT[:, 4 * i + 2:4 * i + 4, :], T[:, 1, :].rearrange("p (g n) -> p g n", g=2)).then_inc(pool_d, 1)
                dve.wait_ge(pool_y, i + 1)
                for g in range(2, 4):
                    V.tensor_scalar(dst[:, 4 + g, :], T[:, 3, (g - 2) * S:(g - 1) * S], cols["we_pool_scale_2"][:, g:g + 1], None,
                                    ALU.mult).then_inc(pool_ok, 1)
            turn_evict("o_x", lambda i: HT[:, i, :])
            turn_evict("o_c", lambda i: HC[:, i, :])
            mod_columns(2)
            mod_columns(3)
            mod_gate(0, 1)
            diagonal(2, gtg[:, 0, 1, 0, :])
            mod_scale(0, 1)
            mod_scale(1, 0)
            product_evict("out_x0", Y, D)
            spread_row(2, bc2[:, 0, :])
            diagonal(3, gtg[:, 0, 1, 1, :])
            evicted("out_x0")
            residual("p_x0", Y, bc[:, 0, :], x)
            norm("nf_x0", x, Y)
            dve.wait_ge(turn_act, turn["o_c"][1] + 2)
            dve.wait_ge(turn_dve, turn["o_c"][2] + 2)
            product_evict("out_c0", Z, D, 0, 1)
            spread_row(3, bc2[:, 1, :])
            w_low("_x0", 0)
            x_split("_x0", "hf_x0", lambda i: hscale[:, 0, 1, 0, i:i + 1], lambda i: modcol[:, 0, 24 + i, 0:1])
            product_evict("out_c0", Z, D, 1)
            w_low("_x0", 1)
            up_block("_x0", 0)
            evicted("out_c0")
            inverse_rms("p_c0", Z, junk)
            for t in range(NT):
                up_block("_x0", 1 + t)
                residual_tile("p_c0", Z, bc[:, 1, :], cx, t)
            up_block("_x0", 3)
            inverse_rms("nf_c0", cx, Z)
            up_block("_x0", 4)
            norm_tile("nf_c0", cx, Z)
            up_loop("_x0", 2)
            down_weights("_x0", last=2 * FB + 6)
            x_split("_c0", "hf_c0", lambda i: hscale[:, 0, 1, 1, i:i + 1], lambda i: modcol[:, 0, 24 + i, 1:2])
            down_weights("_x0", 2 * FB + 6)
            w_low("_c0", 0)
            down_evict("_x0", Y)
            w_low("_c0", 1)
            up_block("_c0", 0)
            evicted("down_x0")
            inverse_rms("pf_x0", Y, junk)
            for t in range(NT):
                up_block("_c0", 1 + t)
                residual_tile("pf_x0", Y, bc2[:, 0, :], x, t)
            up_block("_c0", 3)
            inverse_rms("n_x1", x, Y)
            up_block("_c0", 4)
            norm_tile("n_x1", x, Y)
            up_loop("_c0", 2)
            down_weights("_c0")
            down_evict("_c0", Z)
            turn_evict("h_x1", lambda i: HT[:, i, :], lambda i: hscale[:, 1, 0, 0, i:i + 1], lambda i: modcol[:, 1, i, 0:1])
            evicted("down_c0")
            residual("pf_c0", Z, bc2[:, 1, :], cx)
            norm("n_c1", cx, Z)
            for b in range(2):
                block_evict("qkv_x1", b, px, N_ODD)
            blocks_in("qkv_x1", 2)
            for t in range(NT):
                rope_axial(px[:, t, 0:D], t, 16)
            block_evict("qkv_x1", 2, px, N_ODD)
            blocks_in("qkv_x1", 3)
            turn_evict("h_c1", lambda i: HC[:, i, :], lambda i: hscale[:, 1, 0, 1, i:i + 1], lambda i: modcol[:, 1, i, 1:2])
            for t in range(NT):
                rope_axial(px[:, t, D:D + S], t, 4)
            step.wait()
            double_keys(0, px[:, :, D:D + S], 4)
            product_evict("kv_c1", pc[:, :, D:N_ODD], NB)
            evicted("kv_c1")
            double_keys(2, pc[:, :, D:D + S], 4)
            step.wait()
            V.engine_nop().then_inc(qk_ready, 1)
            turn_evict("q_1", lambda i: qT[:, i, :])
            turn_evict("k_1", lambda i: kT[:, i % 4, (i // 4) * S:(i // 4 + 1) * S])
            dve.wait_ge(band_in, 16)
            attention("a1x", band, 0)
            turn_evict("o_1", lambda i: HT[:, i, :])
            mod_columns(4)
            mod_gate(1, 0)
            diagonal(4, gtg[:, 1, 0, 0, :])
            product_evict("out_x1", Y, D)
            spread_row(4, bc[:, 0, :])
            evicted("out_x1")
            residual("p_x1", Y, bc[:, 0, :], x)
            norm("nf_x1", x, Y)
            mod_evict(5)
            mod_columns(5)
            mod_scale(1, 1)
            mod_gate(1, 1)
            w_low("_x1", 0)
            x_split("_x1", "hf_x1", lambda i: hscale[:, 1, 1, 0, i:i + 1], lambda i: modcol[:, 1, 24 + i, 0:1])
            w_low("_x1", 1)
            diagonal(5, gtg[:, 1, 1, 0, :])
            up_block("_x1", 0)
            spread_row(5, bc[:, 1, :], 2)
            up_block("_x1", 1)
            up_block("_x1", 2)
            up_loop("_x1", 1)
            down_weights("_x1")
            down_evict("_x1", Y)
            evicted("down_x1")
            residual("pf_x1", Y, bc[:, 1, :], x)


def shape_constants():
    f32 = np.float32
    pos = np.arange(S)
    tile = lambda a: np.ascontiguousarray(a.reshape(NT, P, *a.shape[1:]).swapaxes(0, 1)).astype(f32)
    causal = np.where(pos[None, :P] <= pos[:P, None], 0.0, MASKED)
    band = np.concatenate([np.where(np.abs(pos[None, :] - pos[:, None]) <= 128, 0.0, MASKED), np.zeros((S, S))], axis=1)

    def angles(at, freq):
        a = at.astype(f32)[:, None] * freq[None, :]
        return np.cos(a).astype(f32), np.sin(a).astype(f32)

    f1 = (f32(500000.0) ** (-np.arange(8, dtype=f32) / f32(8))).astype(f32)
    f2 = (f32(10000.0) ** (-np.arange(16, dtype=f32) / f32(16))).astype(f32)
    rope1 = np.stack(angles(pos, f1), axis=1)
    (cr, sr), (cc, sc) = angles(pos // 64, f2), angles(pos % 64, f2)
    rope2 = np.stack([np.concatenate([cr, cc], 1), np.concatenate([sr, sc], 1)], axis=1)
    pool = np.zeros((4, S, S))
    for g, w in enumerate((2, 4, 8, 16)):
        lo, hi = np.clip(pos - w // 2, 0, S), np.clip(pos + w - w // 2, 0, S)
        inside = (pos[:, None] >= lo[None, :]) & (pos[:, None] < hi[None, :])
        pool[g] = inside / (hi - lo)[None, :] - np.eye(S)
    pool = pool.reshape(4, NT, P, S).transpose(2, 0, 1, 3)
    return {"ident": np.eye(P, dtype=f32), "causal": causal.astype(f32), "band": tile(band), "rope1": tile(rope1),
            "rope2": tile(rope2), "pool": np.ascontiguousarray(pool).astype(f32)}


def kernel(**inputs):
    import numpy as _np
    import concourse.bacc as _bacc
    from concourse import mybir as _mybir
    from concourse.bass_utils import run_bass_kernel_spmd as _run

    nc = _bacc.Bacc("TRN2", target_bir_lowering=False, num_devices=1)
    arrays, t_in, consts = {}, {}, {}
    for name, a in inputs.items():
        a = _np.ascontiguousarray(a)
        arrays[f"in_{name}"] = a
        t_in[name] = nc.dram_tensor(f"in_{name}", a.shape, _mybir.dt.from_np(a.dtype), kind="ExternalInput").ap()
    for name, a in shape_constants().items():
        arrays[f"const_{name}"] = a
        consts[name] = nc.dram_tensor(f"const_{name}", a.shape, _mybir.dt.from_np(a.dtype), kind="ExternalInput").ap()
    out = nc.dram_tensor("out", (1, S, D), F32, kind="ExternalOutput").ap()
    build(nc, t_in, consts, out)
    r = _run(nc, [arrays], core_ids=[0])
    return r.results[0]["out"]
```
